# Optimizing a Trainium2 kernel written in Bass

```python
import math
import jax, jax.numpy as jnp
from jax import lax
import numpy as np

D_MODEL = 1024
BATCH = 1
SEQ = 256
DEPTH = 1

HEAD_DIM = D_MODEL // 16
GLA_HEADS = 4
GLA_DK = HEAD_DIM // 2
GLA_DV = HEAD_DIM
GLA_GATE_RANK = 16
GLA_GATE_TAU = 16.0
GLA_CHUNK = 64
CONV_CH = 4 * HEAD_DIM
CONV_GROUPS = 4
CONV_WIDTH = 31
DIFF_HEADS = 4
DIFF_D = HEAD_DIM
Q_BLOCK = 128
D_MIX = GLA_HEADS * GLA_DV + CONV_CH + DIFF_HEADS * 2 * DIFF_D
IN_SPLITS = (GLA_HEADS * GLA_DK, GLA_HEADS * GLA_DK, GLA_HEADS * GLA_DV, GLA_GATE_RANK,
             GLA_HEADS * GLA_DV, 2 * CONV_CH, DIFF_HEADS * 2 * DIFF_D,
             DIFF_HEADS * 2 * DIFF_D, DIFF_HEADS * 2 * DIFF_D)
N_IN = sum(IN_SPLITS)
N_GROUPS = 4
EXPERTS_PER_GROUP = 4
N_EXPERTS = N_GROUPS * EXPERTS_PER_GROUP
TOP_K = 2
D_EXPERT = D_MODEL // 4
EPS = 1e-6


def rms_norm(x, g):
    xf = x.astype(jnp.float32)
    y = xf * lax.rsqrt(jnp.mean(xf * xf, axis=-1, keepdims=True) + EPS)
    return (y * g.astype(jnp.float32)).astype(x.dtype)

def gla_mixer(q, k, v, gate_lr, out_gate, w_gate, b_gate, norm_g):
    B, S, _ = q.shape
    dt = q.dtype
    f32 = jnp.float32
    H, DK, DV, C = GLA_HEADS, GLA_DK, GLA_DV, GLA_CHUNK
    nc = S // C
    log_a = jax.nn.log_sigmoid((gate_lr @ w_gate + b_gate).astype(f32)) / GLA_GATE_TAU

    def to_chunks(t, d):
        return t.astype(f32).reshape(B, nc, C, H, d).transpose(1, 0, 3, 2, 4)

    qc = to_chunks(q, DK) * (DK ** -0.5)
    kc = to_chunks(k, DK)
    vc = to_chunks(v, DV)
    gc = to_chunks(log_a, DK)
    causal = jnp.tril(jnp.ones((C, C), dtype=bool))

    def step(state, inp):
        qi, ki, vi, gi = inp
        b = jnp.cumsum(gi, axis=2)
        o_inter = jnp.einsum('bhik,bhkv->bhiv', qi * jnp.exp(b), state)
        diff = b[:, :, :, None, :] - b[:, :, None, :, :]
        decay = jnp.exp(jnp.where(causal[:, :, None], diff, -jnp.inf))
        scores = jnp.einsum('bhik,bhjk,bhijk->bhij', qi, ki, decay)
        o = o_inter + jnp.einsum('bhij,bhjv->bhiv', scores, vi)
        b_last = b[:, :, -1:, :]
        new_state = (jnp.exp(b_last[:, :, 0, :])[..., None] * state
                     + jnp.einsum('bhjk,bhjv->bhkv', ki * jnp.exp(b_last - b), vi))
        return new_state, o

    s0 = jnp.zeros((B, H, DK, DV), f32)
    _, o = lax.scan(step, s0, (qc, kc, vc, gc))
    o = o.transpose(1, 0, 3, 2, 4).reshape(B, S, H, DV)
    o = rms_norm(o, norm_g).reshape(B, S, H * DV)
    o = o * jax.nn.silu(out_gate.astype(f32))
    return o.astype(dt)

def conv_mixer(u, w, b, gn_g, gn_b):
    dt = u.dtype
    a, gt = jnp.split(u, 2, axis=-1)
    z = a * jax.nn.sigmoid(gt)
    zp = jnp.pad(z, ((0, 0), (CONV_WIDTH - 1, 0), (0, 0)))
    y = lax.conv_general_dilated(zp, w[:, None, :].astype(dt), (1,), 'VALID',
                                 dimension_numbers=('NWC', 'WIO', 'NWC'),
                                 feature_group_count=CONV_CH) + b
    B, S, _ = y.shape
    yf = y.astype(jnp.float32).reshape(B, S, CONV_GROUPS, CONV_CH // CONV_GROUPS)
    mu = jnp.mean(yf, axis=-1, keepdims=True)
    var = jnp.mean(jnp.square(yf - mu), axis=-1, keepdims=True)
    yn = ((yf - mu) * lax.rsqrt(var + EPS)).reshape(B, S, CONV_CH)
    yn = yn * gn_g.astype(jnp.float32) + gn_b.astype(jnp.float32)
    return jax.nn.silu(yn).astype(dt)

def diff_attention(q, k, v, qn_g, kn_g, lq1, lk1, lq2, lk2, subln_g, lambda_init):
    B, S, _ = q.shape
    H, D = DIFF_HEADS, DIFF_D
    f32 = jnp.float32
    qh = rms_norm(q.reshape(B, S, H, 2, D), qn_g).transpose(0, 2, 3, 1, 4)
    kh = rms_norm(k.reshape(B, S, H, 2, D), kn_g).transpose(0, 2, 3, 1, 4)
    vh = v.reshape(B, S, H, 2 * D).transpose(0, 2, 1, 3)
    lam = (jnp.exp(jnp.sum(lq1.astype(f32) * lk1.astype(f32)))
           - jnp.exp(jnp.sum(lq2.astype(f32) * lk2.astype(f32))) + lambda_init)
    scale = D ** -0.5
    k_pos = jnp.arange(S)

    def block(i):
        start = i * Q_BLOCK
        qb = lax.dynamic_slice_in_dim(qh, start, Q_BLOCK, axis=3)
        s = jnp.einsum('bhmqd,bhmkd->bhmqk', qb, kh).astype(f32) * scale
        q_pos = start + jnp.arange(Q_BLOCK)
        s = jnp.where(k_pos[None, :] <= q_pos[:, None], s, -jnp.inf)
        p = jax.nn.softmax(s, axis=-1)
        a = p[:, :, 0] - lam * p[:, :, 1]
        return jnp.einsum('bhqk,bhkv->bhqv', a.astype(vh.dtype), vh)

    o = lax.map(block, jnp.arange(S // Q_BLOCK))
    o = o.transpose(1, 0, 3, 2, 4).reshape(B, S, H, 2 * D)
    o = rms_norm(o, subln_g) * (1.0 - lambda_init)
    return o.reshape(B, S, H * 2 * D)

def hier_moe(h, wg, bg, we, be, w_gate, w_up, w_down):
    B, S, D = h.shape
    f32 = jnp.float32
    t = h.reshape(-1, D)
    T = t.shape[0]
    glog = (t @ wg + bg).astype(f32)
    gprob = jax.nn.softmax(glog, axis=-1)
    g_onehot = jax.nn.one_hot(jnp.argmax(glog, axis=-1), N_GROUPS, dtype=f32)
    p_group = jnp.sum(gprob * g_onehot, axis=-1, keepdims=True)
    elog = (t @ we + be).astype(f32).reshape(T, N_GROUPS, EXPERTS_PER_GROUP)
    elog_sel = jnp.einsum('tge,tg->te', elog, g_onehot)
    eprob = jax.nn.softmax(elog_sel, axis=-1)
    top_p, top_i = lax.top_k(eprob, TOP_K)
    top_p = top_p / jnp.sum(top_p, axis=-1, keepdims=True)
    w_local = jnp.sum(jax.nn.one_hot(top_i, EXPERTS_PER_GROUP, dtype=f32) * top_p[..., None], axis=1)
    gates = (g_onehot[:, :, None] * w_local[:, None, :]).reshape(T, N_EXPERTS) * p_group
    gates = gates.astype(t.dtype)
    y = jnp.zeros_like(t)
    for e in range(N_EXPERTS):
        hid = jax.nn.silu(t @ w_gate[e]) * (t @ w_up[e])
        y = y + gates[:, e:e + 1] * (hid @ w_down[e])
    return y.reshape(B, S, D)

def first_inputs(seed: int = 0) -> dict:
    key = jax.random.key(seed)
    ks = jax.random.split(key, 32)
    L, D, f32 = DEPTH, D_MODEL, jnp.float32

    def nrm(k, shape, scale):
        return jax.random.normal(k, shape, f32) * scale

    def gain(k, shape):
        return 1.0 + 0.02 * jax.random.normal(k, shape, f32)

    return {
        'x': nrm(ks[0], (BATCH, SEQ, D), 1.0),
        'mix_norm_g': gain(ks[1], (L, D)),
        'w_in': nrm(ks[2], (L, D, N_IN), D ** -0.5),
        'gla_gate_w': nrm(ks[3], (L, GLA_GATE_RANK, GLA_HEADS * GLA_DK), GLA_GATE_RANK ** -0.5),
        'gla_gate_b': nrm(ks[4], (L, GLA_HEADS * GLA_DK), 0.1),
        'gla_norm_g': gain(ks[5], (L, GLA_DV)),
        'conv_w': nrm(ks[6], (L, CONV_WIDTH, CONV_CH), CONV_WIDTH ** -0.5),
        'conv_b': nrm(ks[7], (L, CONV_CH), 0.02),
        'conv_norm_g': gain(ks[8], (L, CONV_CH)),
        'conv_norm_b': nrm(ks[9], (L, CONV_CH), 0.02),
        'diff_qnorm_g': gain(ks[10], (L, DIFF_D)),
        'diff_knorm_g': gain(ks[11], (L, DIFF_D)),
        'diff_lq1': nrm(ks[12], (L, DIFF_D), 0.1),
        'diff_lk1': nrm(ks[13], (L, DIFF_D), 0.1),
        'diff_lq2': nrm(ks[14], (L, DIFF_D), 0.1),
        'diff_lk2': nrm(ks[15], (L, DIFF_D), 0.1),
        'diff_subln_g': gain(ks[16], (L, 2 * DIFF_D)),
        'w_out': nrm(ks[17], (L, D_MIX, D), D_MIX ** -0.5),
        'ffn_norm_g': gain(ks[18], (L, D)),
        'router_group_w': nrm(ks[19], (L, D, N_GROUPS), D ** -0.5),
        'router_group_b': nrm(ks[20], (L, N_GROUPS), 0.01),
        'router_expert_w': nrm(ks[21], (L, D, N_EXPERTS), D ** -0.5),
        'router_expert_b': nrm(ks[22], (L, N_EXPERTS), 0.01),
        'expert_w_gate': nrm(ks[23], (L, N_EXPERTS, D, D_EXPERT), D ** -0.5),
        'expert_w_up': nrm(ks[24], (L, N_EXPERTS, D, D_EXPERT), D ** -0.5),
        'expert_w_down': nrm(ks[25], (L, N_EXPERTS, D_EXPERT, D), D_EXPERT ** -0.5),
    }

def first_block(x, mix_norm_g, w_in, gla_gate_w, gla_gate_b, gla_norm_g, conv_w, conv_b,
              conv_norm_g, conv_norm_b, diff_qnorm_g, diff_knorm_g, diff_lq1, diff_lk1,
              diff_lq2, diff_lk2, diff_subln_g, w_out, ffn_norm_g, router_group_w,
              router_group_b, router_expert_w, router_expert_b, expert_w_gate, expert_w_up,
              expert_w_down):
    offsets = [int(o) for o in np.cumsum(IN_SPLITS)[:-1]]
    for l in range(DEPTH):
        hn = rms_norm(x, mix_norm_g[l])
        proj = hn @ w_in[l]
        gq, gk, gv, glr, gog, cu, dq, dk, dv = jnp.split(proj, offsets, axis=-1)
        o_gla = gla_mixer(gq, gk, gv, glr, gog, gla_gate_w[l], gla_gate_b[l], gla_norm_g[l])
        o_conv = conv_mixer(cu, conv_w[l], conv_b[l], conv_norm_g[l], conv_norm_b[l])
        lambda_init = 0.8 - 0.6 * math.exp(-0.3 * l)
        o_diff = diff_attention(dq, dk, dv, diff_qnorm_g[l], diff_knorm_g[l], diff_lq1[l],
                                diff_lk1[l], diff_lq2[l], diff_lk2[l], diff_subln_g[l], lambda_init)
        mix = jnp.concatenate([o_gla, o_conv, o_diff], axis=-1)
        x = x + mix @ w_out[l]
        x = x + hier_moe(rms_norm(x, ffn_norm_g[l]), router_group_w[l], router_group_b[l],
                         router_expert_w[l], router_expert_b[l], expert_w_gate[l],
                         expert_w_up[l], expert_w_down[l])
    return x


DEPTH_2 = 2

HEAD_DIM_2 = D_MODEL // 16
NSA_HEADS = 8
NSA_KV_GROUPS = 2
FOX_HEADS = 4
MOBA_HEADS = 4
MIX_WIDTH = (NSA_HEADS + FOX_HEADS + MOBA_HEADS) * HEAD_DIM_2
ROPE_DIM = HEAD_DIM_2 // 4
ROPE_THETA = 500000.0
CMP_LEN = 32
CMP_STRIDE = 16
CMP_HIDDEN = 4 * HEAD_DIM_2
SLC_LEN = 64
SLC_TOPN = 8
WIN = 512
MOBA_BLOCK = 256
MOBA_TOPK = 3
QBLOCK = 128
GATHER_CHUNK = 32
D_FF = 256 * ((8 * D_MODEL // 3 + 255) // 256)
FOX_FGATE_BIAS = 3.0
MAX_POS_OFFSET = 4096

_NSA_KV = NSA_KV_GROUPS * HEAD_DIM_2
IN_SPLITS_2 = (
    ("nsa_q", NSA_HEADS * HEAD_DIM_2),
    ("nsa_kc", _NSA_KV), ("nsa_vc", _NSA_KV),
    ("nsa_ks", _NSA_KV), ("nsa_vs", _NSA_KV),
    ("nsa_kw", _NSA_KV), ("nsa_vw", _NSA_KV),
    ("nsa_gate", 3 * NSA_HEADS),
    ("fox_q", FOX_HEADS * HEAD_DIM_2), ("fox_k", FOX_HEADS * HEAD_DIM_2),
    ("fox_v", FOX_HEADS * HEAD_DIM_2), ("fox_f", FOX_HEADS),
    ("moba_q", MOBA_HEADS * HEAD_DIM_2), ("moba_k", MOBA_HEADS * HEAD_DIM_2),
    ("moba_v", MOBA_HEADS * HEAD_DIM_2),
)
IN_COLS = sum(w for _, w in IN_SPLITS_2)


def rms_norm_2(x, g):
    xf = x.astype(jnp.float32)
    y = xf * lax.rsqrt(jnp.mean(xf * xf, axis=-1, keepdims=True) + EPS)
    return (y * g.astype(jnp.float32)).astype(x.dtype)

def ada_norm(x, g, shift, scale):
    return rms_norm_2(x, g) * (1 + scale[:, None, :]) + shift[:, None, :]

def swiglu(h, w13, w2):
    a, b = jnp.split(h @ w13, 2, axis=-1)
    return (jax.nn.silu(a) * b) @ w2

def masked_softmax(s, mask):
    s = jnp.where(mask, s.astype(jnp.float32), -jnp.inf)
    m = jnp.max(s, axis=-1, keepdims=True)
    m = jnp.where(jnp.isfinite(m), m, 0.0)
    e = jnp.exp(s - m)
    return e / jnp.maximum(jnp.sum(e, axis=-1, keepdims=True), 1e-30)

def rope_tables(positions):
    inv = ROPE_THETA ** (-jnp.arange(0, ROPE_DIM, 2, dtype=jnp.float32) / ROPE_DIM)
    ang = positions.astype(jnp.float32)[..., None] * inv
    return jnp.cos(ang), jnp.sin(ang)

def apply_rope(x, cos, sin):
    r, rest = x[..., :ROPE_DIM], x[..., ROPE_DIM:]
    r1, r2 = r[..., :ROPE_DIM // 2], r[..., ROPE_DIM // 2:]
    c, s = cos[:, :, None, :], sin[:, :, None, :]
    rot = jnp.concatenate([r1 * c - r2 * s, r2 * c + r1 * s], axis=-1).astype(x.dtype)
    return jnp.concatenate([rot, rest], axis=-1)

def split_blocks(a, axis, size):
    n = a.shape[axis] // size
    a = a.reshape(a.shape[:axis] + (n, size) + a.shape[axis + 1:])
    return jnp.moveaxis(a, axis, 0)

def merge_blocks(a, axis):
    a = jnp.moveaxis(a, 0, axis)
    return a.reshape(a.shape[:axis] + (a.shape[axis] * a.shape[axis + 1],) + a.shape[axis + 2:])

def nsa_mixer(q, kc, vc, ks, vs, kw, vw, gates, cmp_pos, cmp_w1, cmp_w2):
    B, S = q.shape[0], q.shape[1]
    G, R, D = NSA_KV_GROUPS, NSA_HEADS // NSA_KV_GROUPS, HEAD_DIM_2
    scale = D ** -0.5
    qg = q.reshape(B, S, G, R, D).transpose(0, 2, 3, 1, 4)
    t = np.arange(S)

    n_c = (S - CMP_LEN) // CMP_STRIDE + 1
    win_idx = np.arange(n_c)[:, None] * CMP_STRIDE + np.arange(CMP_LEN)[None, :]

    def compress(z, pos, w1, w2):
        zb = z[:, win_idx] + pos[None, None, :, None, :]
        zb = zb.transpose(0, 3, 1, 2, 4).reshape(B, G, n_c, CMP_LEN * D)
        return jax.nn.gelu(zb @ w1) @ w2

    kcmp = compress(kc, cmp_pos[0], cmp_w1[0], cmp_w2[0])
    vcmp = compress(vc, cmp_pos[1], cmp_w1[1], cmp_w2[1])
    cmp_end = np.arange(n_c) * CMP_STRIDE + CMP_LEN - 1
    cmp_mask = cmp_end[None, :] <= t[:, None]
    s_cmp = jnp.einsum('bgrsd,bgcd->bgrsc', qg, kcmp) * scale
    p_cmp = masked_softmax(s_cmp, cmp_mask)
    o_cmp = jnp.einsum('bgrsc,bgcd->bgrsd', p_cmp.astype(vcmp.dtype), vcmp)

    n_s = S // SLC_LEN
    c0 = np.arange(n_c)[:, None] * CMP_STRIDE
    j0 = np.arange(n_s)[None, :] * SLC_LEN
    overlap = ((c0 < j0 + SLC_LEN) & (c0 + CMP_LEN > j0)).astype(np.float32)
    imp = jnp.einsum('bgrsc,cj->bgsj', p_cmp, jnp.asarray(overlap))
    tb = (t // SLC_LEN)[:, None]
    jj = np.arange(n_s)[None, :]
    valid = jj <= tb
    forced = (jj == 0) | (jj == tb) | (jj == tb - 1)
    imp = jnp.where(valid, jnp.where(forced, jnp.inf, imp), -jnp.inf)
    n_top = min(SLC_TOPN, n_s)
    top_val, top_idx = lax.top_k(imp, n_top)
    top_ok = top_val > -jnp.inf

    ks_blk = ks.reshape(B, n_s, SLC_LEN, G, D).transpose(0, 3, 1, 2, 4)
    vs_blk = vs.reshape(B, n_s, SLC_LEN, G, D).transpose(0, 3, 1, 2, 4)
    C = GATHER_CHUNK
    bi = jnp.arange(B)[:, None, None]
    gi = jnp.arange(G)[None, :, None]
    k_sel = n_top * SLC_LEN

    def slc_chunk(args):
        qc, idx, ok, q0 = args
        flat = idx.reshape(B, G, C * n_top)
        kg = ks_blk[bi, gi, flat].reshape(B, G, C, k_sel, D)
        vg = vs_blk[bi, gi, flat].reshape(B, G, C, k_sel, D)
        kpos = (idx[..., None] * SLC_LEN + jnp.arange(SLC_LEN)).reshape(B, G, C, k_sel)
        qpos = q0 + jnp.arange(C)
        mask = jnp.repeat(ok, SLC_LEN, axis=-1) & (kpos <= qpos[:, None])
        s = jnp.einsum('bgrcd,bgckd->bgrck', qc, kg) * scale
        p = masked_softmax(s, mask[:, :, None])
        return jnp.einsum('bgrck,bgckd->bgrcd', p.astype(vg.dtype), vg)

    o_slc = lax.map(slc_chunk, (split_blocks(qg, 3, C), split_blocks(top_idx, 2, C),
                                split_blocks(top_ok, 2, C), jnp.arange(S // C) * C))
    o_slc = merge_blocks(o_slc, 3)

    kw_p = jnp.pad(kw.transpose(0, 2, 1, 3), ((0, 0), (0, 0), (WIN, 0), (0, 0)))
    vw_p = jnp.pad(vw.transpose(0, 2, 1, 3), ((0, 0), (0, 0), (WIN, 0), (0, 0)))
    span = WIN + QBLOCK

    def win_block(args):
        qb, q0 = args
        kb = lax.dynamic_slice_in_dim(kw_p, q0, span, axis=2)
        vb = lax.dynamic_slice_in_dim(vw_p, q0, span, axis=2)
        qpos = q0 + jnp.arange(QBLOCK)
        kpos = q0 - WIN + jnp.arange(span)
        d = qpos[:, None] - kpos[None, :]
        mask = (kpos[None, :] >= 0) & (d >= 0) & (d < WIN)
        s = jnp.einsum('bgrqd,bgkd->bgrqk', qb, kb) * scale
        p = masked_softmax(s, mask)
        return jnp.einsum('bgrqk,bgkd->bgrqd', p.astype(vb.dtype), vb)

    o_win = lax.map(win_block, (split_blocks(qg, 3, QBLOCK), jnp.arange(S // QBLOCK) * QBLOCK))
    o_win = merge_blocks(o_win, 3)

    g = gates.reshape(B, S, G, R, 3).transpose(0, 2, 3, 1, 4)
    o = g[..., 0:1] * o_cmp + g[..., 1:2] * o_slc + g[..., 2:3] * o_win
    return o.transpose(0, 3, 1, 2, 4).reshape(B, S, NSA_HEADS * D)

def fox_mixer(q, k, v, f_logit, f_bias):
    B, S, H, D = q.shape
    scale = D ** -0.5
    logf = jax.nn.log_sigmoid((f_logit + f_bias).astype(jnp.float32))
    F = jnp.cumsum(logf, axis=1).transpose(0, 2, 1)
    qt, kt, vt = (a.transpose(0, 2, 1, 3) for a in (q, k, v))
    kpos = jnp.arange(S)

    def blk(args):
        qb, Fq, q0 = args
        s = (jnp.einsum('bhqd,bhkd->bhqk', qb, kt).astype(jnp.float32) * scale
             + Fq[..., None] - F[:, :, None, :])
        qpos = q0 + jnp.arange(QBLOCK)
        p = masked_softmax(s, kpos[None, :] <= qpos[:, None])
        return jnp.einsum('bhqk,bhkd->bhqd', p.astype(vt.dtype), vt)

    o = lax.map(blk, (split_blocks(qt, 2, QBLOCK), split_blocks(F, 2, QBLOCK),
                      jnp.arange(S // QBLOCK) * QBLOCK))
    o = merge_blocks(o, 2)
    return o.transpose(0, 2, 1, 3).reshape(B, S, H * D)

def moba_mixer(q, k, v):
    B, S, H, D = q.shape
    scale = D ** -0.5
    qt, kt, vt = (a.transpose(0, 2, 1, 3) for a in (q, k, v))
    NB = -(-S // MOBA_BLOCK)
    Sp = NB * MOBA_BLOCK
    kp = jnp.pad(kt, ((0, 0), (0, 0), (0, Sp - S), (0, 0)))
    vp = jnp.pad(vt, ((0, 0), (0, 0), (0, Sp - S), (0, 0)))
    kb = kp.reshape(B, H, NB, MOBA_BLOCK, D)
    vb = vp.reshape(B, H, NB, MOBA_BLOCK, D)
    n_sel = min(MOBA_TOPK, NB - 1)
    C = GATHER_CHUNK
    t = np.arange(S)
    xs = (split_blocks(qt, 2, C), jnp.arange(S // C) * C)
    if n_sel > 0:
        kmean = jnp.mean(kb.astype(jnp.float32), axis=3)
        gate = jnp.einsum('bhsd,bhnd->bhsn', qt.astype(jnp.float32), kmean)
        past = np.arange(NB)[None, :] < (t // MOBA_BLOCK)[:, None]
        gate = jnp.where(past, gate, -jnp.inf)
        top_val, top_idx = lax.top_k(gate, n_sel)
        xs = xs + (split_blocks(top_idx, 2, C), split_blocks(top_val > -jnp.inf, 2, C))
    bi = jnp.arange(B)[:, None, None]
    hi = jnp.arange(H)[None, :, None]
    k_sel = n_sel * MOBA_BLOCK

    def chunk(args):
        qc, q0 = args[0], args[1]
        own = q0 // MOBA_BLOCK
        k_own = lax.dynamic_slice_in_dim(kp, own * MOBA_BLOCK, MOBA_BLOCK, axis=2)
        v_own = lax.dynamic_slice_in_dim(vp, own * MOBA_BLOCK, MOBA_BLOCK, axis=2)
        qpos = q0 + jnp.arange(C)
        own_pos = own * MOBA_BLOCK + jnp.arange(MOBA_BLOCK)
        s_own = jnp.einsum('bhcd,bhkd->bhck', qc, k_own) * scale
        m_own = jnp.broadcast_to(own_pos[None, :] <= qpos[:, None], s_own.shape)
        if n_sel == 0:
            p = masked_softmax(s_own, m_own)
            return jnp.einsum('bhck,bhkd->bhcd', p.astype(v_own.dtype), v_own)
        idx, ok = args[2], args[3]
        flat = idx.reshape(B, H, C * n_sel)
        kg = kb[bi, hi, flat].reshape(B, H, C, k_sel, D)
        vg = vb[bi, hi, flat].reshape(B, H, C, k_sel, D)
        s_sel = jnp.einsum('bhcd,bhckd->bhck', qc, kg) * scale
        m_sel = jnp.repeat(ok, MOBA_BLOCK, axis=-1)
        p = masked_softmax(jnp.concatenate([s_sel, s_own], axis=-1),
                           jnp.concatenate([m_sel, m_own], axis=-1))
        p = p.astype(vg.dtype)
        return (jnp.einsum('bhck,bhckd->bhcd', p[..., :k_sel], vg)
                + jnp.einsum('bhck,bhkd->bhcd', p[..., k_sel:], v_own))

    o = merge_blocks(lax.map(chunk, xs), 2)
    return o.transpose(0, 2, 1, 3).reshape(B, S, H * D)

def token_mixer(h, w_in, f_bias, cmp_pos, cmp_w1, cmp_w2, w_out, cos, sin):
    B, S, _ = h.shape
    proj = h @ w_in
    parts = {}
    off = 0
    for name, width in IN_SPLITS_2:
        parts[name] = proj[..., off:off + width]
        off += width

    def heads(a, n):
        return a.reshape(B, S, n, HEAD_DIM_2)

    o_nsa = nsa_mixer(
        apply_rope(heads(parts['nsa_q'], NSA_HEADS), cos, sin),
        apply_rope(heads(parts['nsa_kc'], NSA_KV_GROUPS), cos, sin), heads(parts['nsa_vc'], NSA_KV_GROUPS),
        apply_rope(heads(parts['nsa_ks'], NSA_KV_GROUPS), cos, sin), heads(parts['nsa_vs'], NSA_KV_GROUPS),
        apply_rope(heads(parts['nsa_kw'], NSA_KV_GROUPS), cos, sin), heads(parts['nsa_vw'], NSA_KV_GROUPS),
        jax.nn.sigmoid(parts['nsa_gate']).reshape(B, S, NSA_HEADS, 3),
        cmp_pos, cmp_w1, cmp_w2)
    o_fox = fox_mixer(heads(parts['fox_q'], FOX_HEADS), heads(parts['fox_k'], FOX_HEADS),
                      heads(parts['fox_v'], FOX_HEADS), parts['fox_f'], f_bias)
    o_moba = moba_mixer(apply_rope(heads(parts['moba_q'], MOBA_HEADS), cos, sin),
                        apply_rope(heads(parts['moba_k'], MOBA_HEADS), cos, sin),
                        heads(parts['moba_v'], MOBA_HEADS))
    return jnp.concatenate([o_nsa, o_fox, o_moba], axis=-1) @ w_out

def second_inputs(seed: int = 0) -> dict:
    key = jax.random.key(seed)
    ks = jax.random.split(key, 16)
    D = D_MODEL

    def nrm(k, shape, s):
        return jax.random.normal(k, shape, jnp.float32) * s

    x = nrm(ks[0], (BATCH, SEQ, D), 1.0)
    c = nrm(ks[1], (BATCH, D), 1.0)
    offset = jax.random.randint(ks[2], (BATCH, 1), 0, MAX_POS_OFFSET, dtype=jnp.int32)
    positions = offset + jnp.arange(SEQ, dtype=jnp.int32)[None, :]
    return {
        "x": x,
        "c": c,
        "positions": positions,
        "norm_g": 1.0 + nrm(ks[3], (DEPTH_2, 3, D), 0.05),
        "w_ada": nrm(ks[4], (DEPTH_2, D, 9 * D), 0.5 * D ** -0.5),
        "b_ada": nrm(ks[5], (DEPTH_2, 9 * D), 0.01),
        "w_in": nrm(ks[6], (DEPTH_2, D, IN_COLS), D ** -0.5),
        "fox_fbias": FOX_FGATE_BIAS + nrm(ks[7], (DEPTH_2, FOX_HEADS), 0.1),
        "cmp_pos": nrm(ks[8], (DEPTH_2, 2, CMP_LEN, HEAD_DIM_2), 0.1),
        "cmp_w1": nrm(ks[9], (DEPTH_2, 2, CMP_LEN * HEAD_DIM_2, CMP_HIDDEN), (CMP_LEN * HEAD_DIM_2) ** -0.5),
        "cmp_w2": nrm(ks[10], (DEPTH_2, 2, CMP_HIDDEN, HEAD_DIM_2), CMP_HIDDEN ** -0.5),
        "w_out": nrm(ks[11], (DEPTH_2, MIX_WIDTH, D), MIX_WIDTH ** -0.5),
        "ffn_w13": nrm(ks[12], (DEPTH_2, 2, D, 2 * D_FF), D ** -0.5),
        "ffn_w2": nrm(ks[13], (DEPTH_2, 2, D_FF, D), D_FF ** -0.5),
        "final_g": 1.0 + nrm(ks[14], (D,), 0.05),
    }

def second_block(x, c, positions, norm_g, w_ada, b_ada, w_in, fox_fbias, cmp_pos, cmp_w1, cmp_w2,
              w_out, ffn_w13, ffn_w2, final_g):
    cos, sin = rope_tables(positions)
    c_act = jax.nn.silu(c)
    B = x.shape[0]
    for l in range(DEPTH_2):
        mod = (c_act @ w_ada[l] + b_ada[l]).reshape(B, 3, 3, D_MODEL)
        h = ada_norm(x, norm_g[l, 0], mod[:, 0, 0], mod[:, 0, 1])
        x = x + 0.5 * mod[:, 0, 2][:, None, :] * swiglu(h, ffn_w13[l, 0], ffn_w2[l, 0])
        h = ada_norm(x, norm_g[l, 1], mod[:, 1, 0], mod[:, 1, 1])
        x = x + mod[:, 1, 2][:, None, :] * token_mixer(h, w_in[l], fox_fbias[l], cmp_pos[l], cmp_w1[l],
                                                        cmp_w2[l], w_out[l], cos, sin)
        h = ada_norm(x, norm_g[l, 2], mod[:, 2, 0], mod[:, 2, 1])
        x = x + 0.5 * mod[:, 2, 2][:, None, :] * swiglu(h, ffn_w13[l, 1], ffn_w2[l, 1])
    return rms_norm_2(x, final_g)


def setup_inputs(seed=0):
    out = dict(first_inputs(seed))
    for name, value in second_inputs(seed + 1).items():
        if name != "x":
            out[name + "_2"] = value
    return out


def reference(
    x, mix_norm_g, w_in, gla_gate_w, gla_gate_b, gla_norm_g, conv_w, conv_b, conv_norm_g,
    conv_norm_b, diff_qnorm_g, diff_knorm_g, diff_lq1, diff_lk1, diff_lq2, diff_lk2,
    diff_subln_g, w_out, ffn_norm_g, router_group_w, router_group_b, router_expert_w,
    router_expert_b, expert_w_gate, expert_w_up, expert_w_down, c_2, positions_2, norm_g_2,
    w_ada_2, b_ada_2, w_in_2, fox_fbias_2, cmp_pos_2, cmp_w1_2, cmp_w2_2, w_out_2, ffn_w13_2,
    ffn_w2_2, final_g_2,
):
    x = first_block(
        x, mix_norm_g, w_in, gla_gate_w, gla_gate_b, gla_norm_g, conv_w, conv_b, conv_norm_g,
        conv_norm_b, diff_qnorm_g, diff_knorm_g, diff_lq1, diff_lk1, diff_lq2, diff_lk2,
        diff_subln_g, w_out, ffn_norm_g, router_group_w, router_group_b, router_expert_w,
        router_expert_b, expert_w_gate, expert_w_up, expert_w_down,
    )
    return second_block(
        x, c_2, positions_2, norm_g_2, w_ada_2, b_ada_2, w_in_2, fox_fbias_2, cmp_pos_2,
        cmp_w1_2, cmp_w2_2, w_out_2, ffn_w13_2, ffn_w2_2, final_g_2,
    )


_drawn_inputs = setup_inputs


def setup_inputs(seed=0):
    import zlib

    import numpy as np

    out = dict(_drawn_inputs(seed))
    spreads = {}
    factors = {'gla_norm_g': 5.258,
     'conv_norm_g': 5.446,
     'conv_norm_b': 8.0,
     'diff_qnorm_g': 2.752,
     'diff_knorm_g': 2.942,
     'diff_lq2': 8.0,
     'diff_subln_g': 2.906,
     'router_group_b': 6.696,
     'router_expert_b': 7.85,
     'norm_g_2': 3.64,
     'b_ada_2': 6.119,
     'fox_fbias_2': 64.0,
     'cmp_pos_2': 7.072}
    for name, (base, spread) in spreads.items():
        noise = np.random.default_rng([zlib.crc32(name.encode()), seed]).standard_normal(out[name].shape)
        drawn = base * np.exp(spread * noise) if base else spread * noise
        out[name] = __import__('jax').numpy.asarray(drawn.astype(out[name].dtype))
    for name, factor in factors.items():
        out[name] = (out[name] * factor).astype(out[name].dtype)
    return out
```

```python
from contextlib import ExitStack

import numpy as np
import concourse.bass as bass
from concourse import mybir

ALU = mybir.AluOpType
ACT = mybir.ActivationFunctionType
F32 = mybir.dt.float32
F32R = mybir.dt.float32r
I32 = mybir.dt.int32
X = mybir.AxisListType.X

D = 1024
EPS = 1e-6
UW = 2048
NRAW = 4
NADA = 2
NSPL = 3
NACC = 4
NEG = -3.0e38

COLS = [("mixg", 8), ("ffng", 8), ("ng2", 48), ("glab", 1), ("convb", 2), ("convw", 62),
        ("c", 8), ("bada", 144), ("pos", 64), ("glaw", 128)]
ROWS = [("glang", 64), ("cng", 256), ("cnb", 256), ("qn", 64), ("kn", 64), ("lq1", 64), ("lk1", 64),
        ("lq2", 64), ("lk2", 64), ("subg", 128), ("rb", 20), ("foxb", 8), ("inv", 8)]


def offsets(table):
    at, out = 0, {}
    for name, n in table:
        out[name] = (at, n)
        at += n
    return out, at


COFF, NCOL = offsets(COLS)
ROFF, NROW = offsets(ROWS)


class Tok:

    def __init__(self, eng, sem=None, value=None):
        self.eng, self.sem, self.value, self.used = eng, sem, value, False


class Queues:

    def __init__(self, nc, sems):
        self.nc, self.sems = nc, sems
        self.q = {e: [] for e in sems}
        self.last = {}
        self.dma_count = {}
        self.bar = {}

    def put(self, eng, fn, waits=(), chain=False):
        tok = Tok(eng)
        flat = []

        def add(w):
            if w is None:
                return
            if isinstance(w, Tok):
                w.used = True
                flat.append(w)
            else:
                for v in w:
                    add(v)

        add(waits)
        if eng in self.bar:
            flat.append(self.bar.pop(eng))
        if chain and eng in self.last:
            add(self.last[eng])
        self.q[eng].append((fn, flat, tok))
        self.last[eng] = tok
        return tok

    def dma(self, eng, fn, sem, waits=()):
        flat = []

        def add(w):
            if w is None:
                return
            if isinstance(w, Tok):
                w.used = True
                flat.append(w)
            else:
                for v in w:
                    add(v)

        add(waits)
        n = self.dma_count.get(id(sem), 0) + 16
        self.dma_count[id(sem)] = n
        tok = Tok("dma", sem, n)
        self.q[eng].append((lambda e: fn(e).then_inc(sem, 16), flat, None))
        return tok

    def number(self):
        for eng, items in self.q.items():
            n = 0
            for _, _, tok in items:
                if tok is not None and tok.used:
                    n += 1
                    tok.sem, tok.value = self.sems[eng], n

    def run(self, eng, e):
        seen = {}
        for fn, waits, tok in self.q[eng]:
            need = {}
            for w in waits:
                k = id(w.sem)
                if w.value > max(seen.get(k, 0), need.get(k, (None, 0))[1]):
                    need[k] = (w.sem, w.value)
            for k, (s, v) in need.items():
                e.wait_ge(s, v)
                seen[k] = v
            ins = fn(e)
            if tok is not None and tok.used:
                ins.then_inc(tok.sem, 1)


class Build:
    def __init__(self, nc, io, order, dry, stage, dbg):
        self.nc, self.io, self.order, self.dry = nc, io, order, dry
        self.stage, self.dbg = stage, dbg
        self.asked = []

    def pe(self, fn, w=()):
        return self.Q.put("pe", fn, w)

    def dve(self, fn, w=(), chain=True):
        return self.Q.put("dve", fn, w, chain)

    def act(self, fn, w=(), chain=True):
        return self.Q.put("act", fn, w, chain)

    def pool(self, fn, w=(), chain=True):
        return self.Q.put("pool", fn, w, chain)

    def tt(self, out, a, b, op, w=(), chain=True):
        return self.dve(lambda e: e.tensor_tensor(out, a, b, op), w, chain)

    def ptt(self, out, a, b, op, w=()):
        return self.pool(lambda e: e.tensor_tensor(out, a, b, op), w, False)

    def ts(self, out, a, s1, op0, s2=None, op1=None, w=(), chain=True):
        if op1 is None:
            return self.dve(lambda e: e.tensor_scalar(out, a, s1, None, op0), w, chain)
        return self.dve(lambda e: e.tensor_scalar(out, a, s1, s2, op0, op1), w, chain)

    def cp(self, out, a, w=(), chain=True):
        return self.dve(lambda e: e.tensor_copy(out, a), w, chain)

    def acopy(self, out, a, w=(), chain=True, scale=1.0):
        return self.act(lambda e: e.activation(out, a, ACT.Copy, scale=scale), w, chain)

    def af(self, out, a, f, w=(), chain=True, **kw):
        return self.act(lambda e: e.activation(out, a, f, **kw), w, chain)

    def mm(self, out, lhsT, rhs, start, stop, w=()):
        return self.pe(lambda e: e.matmul(out, lhsT, rhs, start=start, stop=stop), w)

    def tr(self, out, in_, w=()):
        ident = self.ident[0:in_.shape[0], 0:in_.shape[0]]
        return self.pe(lambda e: e.transpose(out, in_, ident), [w, self.cw])

    def debug(self, name, ap, w):
        if name in self.dbg and not self.dry:
            t = self.Q.dma("sp", lambda e: e.dma_start(self.dbg[name], ap), self.s_out, w)
            self.Q.bar = {e: t for e in ("pe", "dve", "act", "pool")}

    def load(self, n):
        key, width = self.order[n]
        slot = n % NRAW
        raw = self.raw[:, slot, 0:width]
        src = self.io["wu"][n, :, 0:width]
        self.loaded.append(self.Q.dma("sp", lambda e: e.dma_start(raw, src), self.s_raw[slot],
                                      self.rawfree[slot]))
        self.rawfree[slot] = None

    def split(self, n):
        key, width = self.order[n]
        slot, m = n % NRAW, self.nsplit % NSPL
        self.nsplit += 1
        raw = self.raw[:, slot, 0:width]
        hi, lo = self.whi[:, m, 0:width], self.wlo[:, m, 0:width]
        th = self.acopy(hi, raw, [self.loaded[n], self.splfree[m]], chain=False)
        tl = self.tt(lo, raw, hi.bitcast(F32), ALU.subtract, [self.loaded[n], th, self.splfree[m]], chain=False)
        self.rawfree[slot] = [th, tl]
        self.splfree[m] = None
        self.ready[n] = (m, th, tl)

    def take(self, key, width=UW, split=True):
        n = self.nunit
        self.nunit += 1
        self.asked.append((key, width))
        if self.dry:
            self.order.append((key, width))
            self.order_split[n] = split
        assert self.order[n] == (key, width)
        total = n + 1 if self.dry else len(self.order)
        self.ahead(n)
        return n

    def ahead(self, n):
        total = n + 1 if self.dry else len(self.order)
        k = max(self.nload, n)
        while self.nload < min(n + NRAW, total):
            if self.nload - NRAW >= 0 and self.rawfree[self.nload % NRAW] is None:
                break
            self.load(self.nload)
            self.nload += 1
        while self.nahead < min(n + NSPL, total, self.nload):
            if self.order_split[self.nahead]:
                if self.nsplit >= NSPL and self.splfree[self.nsplit % NSPL] is None:
                    break
                self.split(self.nahead)
            self.nahead += 1
            while self.nload < min(n + NRAW, total) and self.rawfree[self.nload % NRAW] is not None:
                self.load(self.nload)
                self.nload += 1
        assert self.nahead > n, (n, self.nahead, self.nload)

    def give(self, n, tok):
        if self.order_split[n]:
            self.splfree[self.ready[n][0]] = tok
        else:
            self.rawfree[n % NRAW] = tok

    def lin_rows(self, bank, hT, kts, n, kt0, off, width, step, t, first, last, w=()):
        m, th, tl = self.ready[n]
        hi, lo = hT
        tok = None
        for i, kt in enumerate(kts):
            wh = self.whi[:, m, off + i * step:off + i * step + width]
            wl = self.wlo[:, m, off + i * step:off + i * step + width]
            xh, xl = hi[:, kt, t * 128:t * 128 + 128], lo[:, kt, t * 128:t * 128 + 128]
            f = first and i == 0
            la = last and i == len(kts) - 1
            self.mm(bank, xh, wh, f, False, [w, th] if i == 0 else ())
            self.mm(bank, xl, wh, False, False)
            tok = self.mm(bank, xh, wl, False, la, [tl] if i == 0 else ())
        return tok

    def up(self, name, j, hT, hw, first):
        n1 = self.take((name, "a", j))
        self.acc_a = n1
        outs = []
        m1, th1, tl1 = self.ready[n1]
        hi, lo = hT
        ab = []

        def tile(n, f, bank, w):
            m, th, tl = self.ready[n]
            for kt in range(8):
                c = kt * 256 + f * 128
                wh, wl = self.whi[:, m, c:c + 128], self.wlo[:, m, c:c + 128]
                self.mm(bank, wh, hi[:, kt, :], kt == 0, False, [w, th] if kt == 0 else ())
                self.mm(bank, wh, lo[:, kt, :], False, False)
                tok = self.mm(bank, wl, hi[:, kt, :], False, kt == 7, [tl] if kt == 0 else ())
            return tok

        ta = [None, None]
        bk = [4 + (2 * self.upn + f) % 4 for f in range(2)] if False else [4, 5]
        for f in range(2):
            ta[f] = tile(n1, f, self.ps[:, bk[f], 0:256], [hw, self.bfree[bk[f]]])
        self.give(n1, ta[1])
        n2 = self.take((name, "b", j))
        tb = [None, None]
        done = []
        for f in range(2):
            if f == 1 and len(self.accs) > 1:
                done, tk = self.sum_acc(7, 1)
            tb[f] = tile(n2, f, self.ps[:, 6 + f, 0:256], [hw, self.bfree[6 + f]])
        self.give(n2, tb[1])
        self.modlate = self.put_mod(7, done, tb[1])
        return ta, tb

    def hidden(self, f, ta, tb, hi, lo, free, gate=None, gw=None):
        r = self.hr % 4
        self.hr += 1
        s, p = self.sil[:, r, :], self.prd[:, r, :]
        t1 = self.af(s, self.ps[:, 4 + f, 0:256], ACT.Silu, [ta, self.silfree[r]], chain=False)
        self.bfree[4 + f] = t1
        late = self.modlate if f == 1 else None
        if gate is not None:
            t0 = self.tt(p, self.ps[:, 6 + f, 0:256], gate, ALU.mult, [tb, gw, self.silfree[r]], chain=False)
            self.bfree[6 + f] = [t0, late]
            t2 = self.tt(p, p, s, ALU.mult, [t1, t0], chain=False)
        else:
            t2 = self.tt(p, self.ps[:, 6 + f, 0:256], s, ALU.mult, [tb, t1, self.silfree[r]], chain=False)
            self.bfree[6 + f] = [t2, late]
        t3 = self.acopy(hi, p, [t2, free], chain=False)
        t4 = self.tt(lo, p, hi.bitcast(F32), ALU.subtract, [t3, free], chain=False)
        self.silfree[r] = [t3, t4]
        return [t3, t4]

    def rstd(self, out, ss, n, w):
        m = ss.shape[-1]
        t = self.ts(out, ss, 1.0 / n, ALU.mult, EPS, ALU.add, w)
        return self.pool(lambda e: e.tensor_tensor(out, out, self.mhalf[:, 0:m], ALU.pow), [t, self.cw])

    def norm_T(self, g, shift, gw):
        toks = []
        tn = []
        for t in range(2):
            tk = self.af(self.xn[:, t, :], self.x[:, t, :], ACT.Square, [self.xw, self.xnfree],
                         accum_out=self.st[:, t:t + 1])
            tn.append(tk)
        r = self.rstd(self.st[:, 2:4], self.st[:, 0:2], D, tn)
        for t in range(2):
            toks.append(self.ts(self.xn[:, t, :], self.x[:, t, :], self.st[:, 2 + t:3 + t], ALU.mult, w=[r]))
        last = None
        es = []
        for kp in range(4):
            b = kp
            for k in range(2):
                kt = 2 * kp + k
                for t in range(2):
                    o = self.ps[:, b, k * 256 + t * 128:k * 256 + t * 128 + 128]
                    tk = self.tr(o, self.xn[:, t, kt * 128:kt * 128 + 128], [toks[t], self.bfree[b]])
            for k in range(2):
                kt = 2 * kp + k
                src = self.ps[:, b, k * 256:k * 256 + 256]
                if shift is None:
                    e = self.ts(self.hT[:, kt, :], src, g[:, kt:kt + 1], ALU.mult, w=[tk, gw, self.mixfree], chain=False)
                else:
                    e = self.ts(self.hT[:, kt, :], src, g[:, kt:kt + 1], ALU.mult, shift[:, kt:kt + 1], ALU.add,
                                w=[tk, gw, self.mixfree], chain=False)
                es.append(e)
            self.bfree[b] = e
            last = tk
        self.xnfree = last
        hs = []
        for q in range(2):
            h = self.acopy(self.hhi[:, 4 * q:4 * q + 4, :], self.hT[:, 4 * q:4 * q + 4, :], [es[4 * q + 3], self.hfree],
                           chain=False)
            l = self.tt(self.hlo[:, 4 * q:4 * q + 4, :], self.hT[:, 4 * q:4 * q + 4, :],
                        self.hhi[:, 4 * q:4 * q + 4, :].bitcast(F32), ALU.subtract, [h], chain=False)
            hs += [h, l]
        self.mixfree = hs
        self.silfree = [hs] * 4
        return hs

    def T4(self, dst, srcs, w, free=None, b=7, scale=None, eng="dve"):
        for i, s in enumerate(srcs):
            tk = self.tr(self.ps[0:s.shape[-1], b, i * 128:i * 128 + 128], s, [w, self.bfree[b]])
        n = len(srcs)
        src = self.ps[0:srcs[0].shape[-1], b, 0:n * 128]
        if scale is not None:
            e = self.ts(dst, src, scale, ALU.mult, w=[tk, free], chain=False)
        elif eng == "act":
            e = self.acopy(dst, src, [tk, free], chain=False)
        else:
            e = self.cp(dst, src, [tk, free], chain=False)
        self.bfree[b] = e
        return e

    def attention(self, heads, vd, scale, w, emit, extra=None):
        G = 2
        n = len(heads)
        st = {}

        def scores(g):
            r = g % 2
            toks = []
            for i in range(G):
                qT, kT, V = heads[g * G + i]
                b = 2 * r + i
                bank = self.ps[:, b, :]
                m = [(bank[:, 0:128], qT[:, 0:128], kT[:, 0:128], 0, 0, 128),
                     (bank[:, 128:384], qT[:, 128:256], kT[:, 0:256], 1, 0, 256)]
                for (o, q_, k_, qt, k0, kn) in m:
                    first = self.mm(o, q_, k_, True, extra is None, [w, self.bfree[b]])
                    tk = first
                    if extra is not None:
                        tk = extra(g * G + i, o, qt, kn)
                toks.append(tk)
            S = self.asb[:, r, :, :]
            ps2 = self.ps[:, 2 * r:2 * r + 2, 0:384]
            mask = self.mask[:, :].unsqueeze(1).to_broadcast([128, 2, 384])
            if scale is None:
                ta = self.tt(S, ps2, mask, ALU.add, [toks, self.asfree[r]])
            else:
                ta = self.tt(S, ps2, mask, ALU.add, [toks, self.asfree[r]])
            self.bfree[2 * r] = self.bfree[2 * r + 1] = ta
            mx = self.amx[:, r, :, :]
            t1 = self.dve(lambda e: e.tensor_reduce(mx[:, 0, :], S[:, :, 0:128], X, ALU.max), [ta], chain=False)
            t2 = self.dve(lambda e: e.tensor_reduce(mx[:, 1, :], S[:, :, 128:384], X, ALU.max), [ta], chain=False)
            t3 = self.ts(self.anm[:, r, :, :], mx, -scale, ALU.mult, w=[t1, t2, self.anfree[r]], chain=False)
            P = self.apb[:, r, :, :]
            te = []
            for i in range(G):
                for t in range(2):
                    a, z = (0, 128) if t == 0 else (128, 384)
                    te.append(self.af(P[:, i, a:z], S[:, i, a:z], ACT.Exp, [t3, self.apfree[r], self.arfree[r]], chain=False,
                                      scale=scale, bias=self.anm[:, r, t, i:i + 1],
                                      accum_out=self.ars[:, r, t, i:i + 1]))
            self.asfree[r] = te
            self.anfree[r] = te
            tr = self.dve(lambda e: e.reciprocal(self.ari[:, r, :, :], self.ars[:, r, :, :]), [te, self.aifree[r]], chain=False)
            self.arfree[r] = tr
            st[g] = (te, tr)

        def values(g):
            r = g % 2
            te, tr = st[g]
            pt = self.apt[:, r, :, :]
            ev = []
            for i in range(G):
                b = 4 + i
                for c in range(3):
                    tk = self.tr(self.ps[:, b, c * 128:c * 128 + 128], self.apb[:, r, i, c * 128:c * 128 + 128],
                                 [te[2 * i:2 * i + 2], self.bfree[b]])
                if i == 0:
                    e = self.acopy(pt[:, i, :], self.ps[:, b, 0:384], [tk, self.aptfree[r]], chain=False)
                else:
                    e = self.cp(pt[:, i, :], self.ps[:, b, 0:384], [tk, self.aptfree[r]], chain=False)
                self.bfree[b] = e
                ev.append(e)
            self.apfree[r] = tk
            b = 6 + r
            for i in range(G):
                V = heads[g * G + i][2]
                for t in range(2):
                    o = self.ps[:, b, (i * 2 + t) * 128:(i * 2 + t) * 128 + vd]
                    if t == 0:
                        tk = self.mm(o, pt[:, i, 0:128], V(0), True, True, [ev[i], w, self.bfree[b]])
                    else:
                        self.mm(o, pt[:, i, 128:256], V(0), True, False)
                        tk = self.mm(o, pt[:, i, 256:384], V(1), False, True)
            self.aptfree[r] = tk
            last = []
            for i in range(G):
                for t in range(2):
                    o = self.ps[:, b, (i * 2 + t) * 128:(i * 2 + t) * 128 + vd]
                    last.append(emit(g * G + i, t, o, self.ari[:, r, t, i:i + 1], [tk, tr]))
            self.bfree[b] = last
            self.aifree[r] = last
            return last

        out = []
        scores(0)
        for g in range(n // G):
            if g + 1 < n // G:
                scores(g + 1)
            out += values(g)
            if self.nada < self.adagoal:
                self.fill(3)
                self.flush(keep=1)
        return out


    def to_T(self, src, w):
        es, last = [], None
        for kp in range(4):
            b = kp
            for k in range(2):
                kt = 2 * kp + k
                for t in range(2):
                    o = self.ps[:, b, k * 256 + t * 128:k * 256 + t * 128 + 128]
                    last = self.tr(o, src[:, t, kt * 128:kt * 128 + 128], [w, self.bfree[b]])
            dst = self.xnT[:, 2 * kp:2 * kp + 2, :].rearrange("p a b -> p (a b)")
            e = self.cp(dst, self.ps[:, b, :], [last, self.hfree], chain=False)
            self.bfree[b] = e
            es.append(e)
        hs = []
        for q in range(2):
            h = self.acopy(self.hhi[:, 4 * q:4 * q + 4, :], self.xnT[:, 4 * q:4 * q + 4, :],
                           [es[2 * q + 1], self.hfree], chain=False)
            l = self.tt(self.hlo[:, 4 * q:4 * q + 4, :], self.xnT[:, 4 * q:4 * q + 4, :],
                        self.hhi[:, 4 * q:4 * q + 4, :].bitcast(F32), ALU.subtract, [h, self.hfree], chain=False)
            hs += [h, l]
        return hs, last

    def proj_cb(self, name, ncols, hT, hw, evac):
        for c in range(0, ncols, 512):
            width = min(512, ncols - c)
            bt = [None, None]
            for half in range(2):
                n = self.take((name, c, half), 4 * width)
                for t in range(2):
                    b = (2 * (c // 512) + t) % 4
                    bt[t] = self.lin_rows(self.ps[:, b, 0:width], hT, range(4 * half, 4 * half + 4), n, 0, 0, width,
                                          width, t, half == 0, half == 1, [hw, self.bfree[b]] if half == 0 else [hw])
                self.give(n, bt[1])
            for t in range(2):
                b = (2 * (c // 512) + t) % 4
                self.bfree[b] = evac(c, t, self.ps[:, b, 0:width], width, bt[t])
            if self.nada < self.adagoal:
                self.fill(2)
                self.flush(keep=1)
        return bt[1]

    def group_norm(self, y, ng, gs, sq, st, w):
        self.tt(sq, y, y, ALU.mult, w)
        t = self.dve(lambda e: e.tensor_reduce(st, sq, X, ALU.add), chain=True)
        r = self.rstd(st, st, gs, [t])
        return self.tt(y, y, st.unsqueeze(2).to_broadcast([128, ng, gs]), ALU.mult, [r])

    def negabs(self, out, a, w):
        return self.dve(lambda e: e.scalar_tensor_tensor(out, a, -1.0, a, ALU.mult, ALU.min), w, True)

    def log_sigmoid(self, z, a, w):
        self.negabs(a, z, w)
        t = self.Q.last["dve"]
        self.af(a, a, ACT.Exp, [t])
        t = self.af(a, a, ACT.Ln, bias=1.0)
        self.ts(z, z, 0.0, ALU.min)
        return self.tt(z, z, a, ALU.subtract, [t])

    def first_mixer(self):
        pj = self.pj1
        cw = self.cw
        hs = self.norm_T(self.col("mixg"), None, cw)
        pw = []

        def evac(c, t, bank, width, tk):
            if t == 0:
                e = self.acopy(pj[:, t, c:c + width], bank, [tk], chain=False)
            else:
                e = self.cp(pj[:, t, c:c + width], bank, [tk], chain=False)
            pw.append(e)
            return e

        last = self.proj_cb(("w_in", 0), 2832, (self.hhi, self.hlo), hs, evac)
        self.hfree = last
        self.debug("pj1", pj[:, :, :], pw)
        sc = self.scr
        qk = sc(0, [128, 2, 256])
        bb = sc(2, [128, 256])
        aa = sc(3, [128, 256])
        qe = sc(4, [128, 8, 256])
        ke = sc(12, [128, 8, 256])
        o = sc(20, [128, 8, 64])
        osq = sc(22, [128, 8, 64])
        mk = self.att(0, [128, 8, 128])
        st = self.att(4, [128, 2, 3, 128])
        glr = self.att(8, [16, 256])
        tq = self.T4(qk[:, 0, :], [pj[:, 0, 0:128], pj[:, 1, 0:128]], [pw, last], scale=float(32 ** -0.5), b=4)
        tk_ = self.T4(qk[:, 1, :], [pj[:, 0, 128:256], pj[:, 1, 128:256]], [pw, last], b=5)
        tg = self.T4(glr, [pj[:, 0, 512:528], pj[:, 1, 512:528]], [pw, last], b=6)
        z = self.ps[:, 7, 0:256]
        t = self.mm(z, self.col("glaw")[0:16, :], glr, True, True, [tg, cw, self.bfree[7]])
        t = self.ts(aa, z, self.col("glab"), ALU.add, w=[t, cw])
        self.bfree[7] = t
        t = self.log_sigmoid(aa, bb, [t])
        t = self.ts(aa, aa, 1.0 / 16.0, ALU.mult)
        t = self.dve(lambda e: e.tensor_tensor_scan(bb, self.ones[:, 0:256], aa, 0.0, ALU.mult, ALU.add), [t], True)
        lv = []
        for li, s in enumerate([128, 64, 32, 16, 8, 4, 2, 1]):
            nb = 128 // s
            bv = bb.rearrange("p (n s) -> p n s", s=2 * s)
            dv = ke[:, li, :].rearrange("p (n s) -> p n s", s=2 * s)
            lv.append(self.tt(dv, bv, bv[:, :, s - 1:s].to_broadcast([128, nb, 2 * s]), ALU.subtract, [t], chain=False))
        t = self.negabs(ke[:, :, :], ke[:, :, :], lv)
        t = self.af(ke[:, :, :], ke[:, :, :], ACT.Exp, [t])
        t1 = self.tt(qe, ke, qk[:, 0, :].unsqueeze(1).to_broadcast([128, 8, 256]), ALU.mult, [t, tq])
        t2 = self.tt(ke, ke, qk[:, 1, :].unsqueeze(1).to_broadcast([128, 8, 256]), ALU.mult, [t, t1, tk_])
        ob = self.ps[:, 6, :].rearrange("p (a b) -> p a b", b=64)
        stf = [None, None]
        mkf = None
        for h in range(4):
            P = slice(32 * h, 32 * h + 32)
            r = h % 2
            b01 = self.ps[:, 4 + r, 0:128]
            t = self.mm(b01, ke[P, 0, 0:128], qe[P, 0, 128:256], True, True, [t1, t2, self.bfree[4 + r]])
            e1 = self.acopy(st[:, r, 1, :], b01, [t, stf[r]], chain=False)
            self.bfree[4 + r] = e1
            ev = [e1]
            for blk in range(2):
                B = slice(128 * blk, 128 * blk + 128)
                for l in range(8):
                    bank = 2 * blk + l // 4
                    oo = self.ps[:, bank, (l % 4) * 128:(l % 4) * 128 + 128]
                    if l < 7:
                        a_, b_ = ke[P, l + 1, B], qe[P, l + 1, B]
                    else:
                        a_, b_ = qk[P, 1, B], qk[P, 0, B]
                    t = self.mm(oo, a_, b_, True, True, [self.bfree[bank], t1, t2])
                e2 = self.tt(mk, self.ps[:, 2 * blk:2 * blk + 2, :].rearrange("p a (b c) -> p (a b) c", c=128),
                             self.gmask, ALU.mult, [t, cw])
                self.bfree[2 * blk] = self.bfree[2 * blk + 1] = e2
                ms = mk.rearrange("p l i -> p i l")
                dst = st[:, r, 2 * blk, :]
                ev.append(self.dve(lambda e, dst=dst, ms=ms: e.tensor_reduce(dst, ms, X, ALU.add), [stf[r]], True))
            v = [pj[:, t_, 256 + 64 * h:320 + 64 * h] for t_ in range(2)]
            self.mm(ob[:, h, :], st[:, r, 0, :], v[0], True, True, [ev, self.bfree[6]])
            self.mm(ob[:, 4 + h, :], st[:, r, 1, :], v[0], True, False)
            stf[r] = t = self.mm(ob[:, 4 + h, :], st[:, r, 2, :], v[1], False, True)
            self.fill(4)
            self.flush(keep=1)
        t = self.cp(o, ob, [t])
        self.bfree[6] = t
        self.group_norm(o, 8, 64, osq, self.st[:, 16:24], [t])
        t = self.tt(o, o, self.row("glang").unsqueeze(1).to_broadcast([128, 8, 64]), ALU.mult, [cw])
        tz = self.af(osq, pj[:, :, 528:784], ACT.Silu, [t])
        for t_ in range(2):
            mg = self.tt(self.mix[:, t_, 0:256], o[:, 4 * t_:4 * t_ + 4, :].rearrange("p a b -> p (a b)"),
                        osq[:, 4 * t_:4 * t_ + 4, :].rearrange("p a b -> p (a b)"), ALU.mult, [tz])
        z = sc(4, [128, 2, 256])
        zT = sc(6, [128, 2, 288])
        dg = sc(9, [128, 4, 128])
        yf = sc(11, [128, 2, 256])
        y = sc(13, [128, 8, 64])
        ysq = sc(15, [128, 8, 64])
        t = self.af(z, pj[:, :, 1040:1296], ACT.Sigmoid, [t, mg])
        t = self.tt(z, z, pj[:, :, 784:1040], ALU.mult, [t])
        t0 = self.dve(lambda e: e.memset(zT[:, :, 0:32], 0.0), [t1], True)
        tz = []
        for ct in range(2):
            tz.append(self.T4(zT[:, ct, 30:286], [z[:, 0, 128 * ct:128 * ct + 128], z[:, 1, 128 * ct:128 * ct + 128]],
                              [t], free=t0, b=4 + ct))
        dgf = [None] * 4
        n = 0
        for ct in range(2):
            for k in range(31):
                r = n % 4
                c = self.col("convw")[:, 31 * ct + k:31 * ct + k + 1]
                d = self.ts(dg[:, r, :], self.ident, c, ALU.mult, w=[cw, dgf[r], t2 if n < 4 else None, stf], chain=False)
                dgf[r] = tt_ = self.mm(self.ps[:, ct, 0:256], dg[:, r, :], zT[:, ct, k:k + 256], k == 0, k == 30,
                                       [d, tz, self.bfree[ct]])
                n += 1
                if k % 8 == 7:
                    self.fill(2)
                    self.flush(keep=1)
            e = self.ts(yf[:, ct, :], self.ps[:, ct, 0:256], self.col("convb")[:, ct:ct + 1], ALU.add, w=[tt_])
            self.bfree[ct] = e
        for t_ in range(2):
            for ct in range(2):
                t = self.tr(self.ps[:, 2, (2 * t_ + ct) * 128:(2 * t_ + ct) * 128 + 128],
                            yf[:, ct, 128 * t_:128 * t_ + 128], [e, self.bfree[2]])
        bk = self.ps[:, 2, :].rearrange("p (a b) -> p a b", b=64)
        mu = self.st[:, 24:32]
        t = self.cp(y, bk, [t])
        self.bfree[2] = t
        self.dve(lambda e: e.tensor_reduce(mu, y, X, ALU.add), [], True)
        self.ts(mu, mu, 1.0 / 64, ALU.mult)
        self.tt(y, y, mu.unsqueeze(2).to_broadcast([128, 8, 64]), ALU.subtract)
        self.group_norm(y, 8, 64, ysq, self.st[:, 16:24], [])
        y2 = y.rearrange("p (t c) d -> p t (c d)", t=2)
        self.tt(y2, y2, self.row("cng").unsqueeze(1).to_broadcast([128, 2, 256]), ALU.mult)
        t = self.tt(y2, y2, self.row("cnb").unsqueeze(1).to_broadcast([128, 2, 256]), ALU.add)
        m2 = self.af(self.mix[:, :, 256:512], y2, ACT.Silu, [t])
        lam = self.st[:, 32:36]
        l4 = self.row("lq1")[:, 0:64]
        lw = sc(15, [128, 2, 64])
        self.tt(lw[:, 0, :], self.row("lq1"), self.row("lk1"), ALU.mult, [cw])
        self.tt(lw[:, 1, :], self.row("lq2"), self.row("lk2"), ALU.mult)
        t = self.dve(lambda e: e.tensor_reduce(lam[:, 0:2], lw, X, ALU.add), [], True)
        t = self.af(lam[:, 0:2], lam[:, 0:2], ACT.Exp, [t])
        t = self.tt(lam[:, 2:3], lam[:, 1:2], lam[:, 0:1], ALU.subtract, [t])
        lamt = self.ts(lam[:, 3:4], lam[:, 2:3], -0.2, ALU.add)
        q = pj[:, :, 1296:2320]
        q4 = pj[:, :, 1296:2320].rearrange("p t (g d) -> p t g d", d=64)
        dsq = sc(16, [128, 2, 16, 64])
        ss = self.st2[:, 0:32].rearrange("p (t g) -> p t g", t=2)
        t = self.tt(dsq, q4, q4, ALU.mult, [m2, dgf])
        t = self.dve(lambda e: e.tensor_reduce(ss, dsq, X, ALU.add), [], True)
        r = self.rstd(self.st2[:, 0:32], self.st2[:, 0:32], 64, [t])
        for t_ in range(2):
            self.tt(q4[:, t_], q4[:, t_], ss[:, t_].unsqueeze(2).to_broadcast([128, 16, 64]), ALU.mult, [r])
            self.tt(q4[:, t_, 0:8], q4[:, t_, 0:8], self.row("qn").unsqueeze(1).to_broadcast([128, 8, 64]), ALU.mult)
            t = self.tt(q4[:, t_, 8:16], q4[:, t_, 8:16], self.row("kn").unsqueeze(1).to_broadcast([128, 8, 64]), ALU.mult)
        QK = sc(0, [128, 4, 2, 256])
        qw = []
        for h in range(4):
            c = 128 * h
            qw.append(self.T4(QK[:, h].rearrange("p a b -> p (a b)"), [q[:, 0, c:c + 128], q[:, 1, c:c + 128],
                      q[:, 0, 512 + c:640 + c], q[:, 1, 512 + c:640 + c]], [t], b=4 + h, eng="act" if h % 2 else "dve"))
        DO = sc(8, [128, 2, 8, 128])
        heads = []
        for h in range(4):
            for m in range(2):
                heads.append((QK[64 * m:64 * m + 64, h, 0, :], QK[64 * m:64 * m + 64, h, 1, :],
                              lambda t_, h=h: pj[:, t_, 2320 + 128 * h:2448 + 128 * h]))

        def emit(i, t_, o_, ri, w):
            return self.ts(DO[:, t_, i, :], o_, ri, ALU.mult, w=w, chain=False)

        self.asfree = [[t], [t]]
        self.apfree = [None, None]
        ow = self.attention(heads, 128, 0.125, [qw, t], emit)
        D5 = DO.rearrange("p t (h m) d -> p t h m d", m=2)
        od = sc(0, [128, 8, 128])
        odq = sc(16, [128, 8, 128])
        for t_ in range(2):
            t = self.dve(lambda e, t_=t_: e.scalar_tensor_tensor(od[:, 4 * t_:4 * t_ + 4, :], D5[:, t_, :, 1, :],
                         lam[:, 3:4], D5[:, t_, :, 0, :], ALU.mult, ALU.add), [ow, lamt], True)
        self.group_norm(od, 8, 128, odq, self.st[:, 16:24], [t])
        self.ts(od, od, 0.8, ALU.mult)
        for t_ in range(2):
            m3 = self.tt(self.mix[:, t_, 512:1024].rearrange("p (h d) -> p h d", d=128), od[:, 4 * t_:4 * t_ + 4, :],
                         self.row("subg").unsqueeze(1).to_broadcast([128, 4, 128]), ALU.mult)
        self.debug("mix1", self.mix[:, :, :], [m3, m2, mg])
        self.pjfree = [ow, m3]
        self.hfree = [m3, ow]
        hs, tl = self.to_T(self.mix, [m3, m2, mg])

        def evac2(c, t, bank, width, tk):
            e = self.tt(self.x[:, t, c:c + width], bank, self.x[:, t, c:c + width], ALU.add, [tk])
            self.xw.append(e)
            return e

        self.xw = []
        self.hfree = self.proj_cb(("w_out", 0), 1024, (self.hhi, self.hlo), hs, evac2)
        self.debug("x1", self.x[:, :, :], self.xw)

    def first_max(self, oh, v, big, n, w):
        mx, eq, idx = big
        self.dve(lambda e: e.tensor_reduce(mx, v, X, ALU.max), w, True)
        self.tt(eq, v, mx.unsqueeze(2).to_broadcast([128, 2, 4]), ALU.is_equal)
        self.tt(eq, eq, self.iom4[:, 0:8].rearrange("p (a b) -> p a b", a=2), ALU.mult)
        self.dve(lambda e: e.tensor_reduce(idx, eq, X, ALU.min), [], True)
        self.tt(oh, self.iom4[:, 0:8].rearrange("p (a b) -> p a b", a=2), idx.unsqueeze(2).to_broadcast([128, 2, 4]),
                ALU.is_equal)
        return mx

    def moe(self):
        cw = self.cw
        hs = self.norm_T(self.col("ffng"), None, cw)
        for t in range(2):
            for kt in range(8):
                tk = self.mm(self.ps[:, 7, t * 32:t * 32 + 20], self.hT[:, kt, t * 128:t * 128 + 128],
                             self.rw[:, kt, :], kt == 0, kt == 7, [hs, cw, self.bfree[7]])
        f = self.frt
        lg = f(0, [128, 2, 20])
        t = self.tt(lg, self.ps[:, 7, 0:64].rearrange("p (t c) -> p t c", t=2)[:, :, 0:20],
                    self.row("rb").unsqueeze(1).to_broadcast([128, 2, 20]), ALU.add, [tk, cw, self.pjfree])
        self.bfree[7] = t
        self.debug("lg", lg, [t])
        mx, eq, idx = f(40, [128, 2]), f(42, [128, 2, 4]), f(50, [128, 2])
        goh, e8, pg = f(52, [128, 2, 4]), f(60, [128, 2, 4]), f(68, [128, 2])
        g = lg[:, :, 0:4]
        self.first_max(goh, g, (mx, eq, idx), 4, [])
        t = self.tt(e8, g, mx.unsqueeze(2).to_broadcast([128, 2, 4]), ALU.subtract)
        t = self.af(e8, e8, ACT.Exp, [t])
        self.dve(lambda e: e.tensor_reduce(pg, e8, X, ALU.add), [t], True)
        self.dve(lambda e: e.reciprocal(pg, pg), [], True)
        es, tmp = f(70, [128, 2, 4, 4]), f(102, [128, 2, 4])
        el = lg[:, :, 4:20].rearrange("p t (g e) -> p t g e", g=4)
        for t_ in range(2):
            self.tt(es[:, t_], el[:, t_], goh[:, t_].unsqueeze(2).to_broadcast([128, 4, 4]), ALU.mult)
        for t_ in range(2):
            t = self.dve(lambda e, t_=t_: e.tensor_reduce(tmp[:, t_, :], es[:, t_].rearrange("p g e -> p e g"), X, ALU.add), [], True)
        m1, oh1, oh2, m2 = f(110, [128, 2]), f(112, [128, 2, 4]), f(120, [128, 2, 4]), f(128, [128, 2])
        self.dve(lambda e: e.tensor_reduce(m1, tmp, X, ALU.max), [], True)
        t = self.tt(tmp, tmp, m1.unsqueeze(2).to_broadcast([128, 2, 4]), ALU.subtract)
        t = self.af(tmp, tmp, ACT.Exp, [t])
        self.first_max(oh1, tmp, (mx, eq, idx), 4, [t])
        self.ts(e8, oh1, -2.0, ALU.mult)
        self.tt(e8, e8, tmp, ALU.add)
        self.first_max(oh2, e8, (mx, eq, idx), 4, [])
        self.cp(m2, mx)
        den = f(130, [128, 2])
        self.ts(den, m2, 1.0, ALU.add)
        self.dve(lambda e: e.reciprocal(den, den), [], True)
        self.tt(den, den, pg, ALU.mult)
        self.tt(oh2, oh2, m2.unsqueeze(2).to_broadcast([128, 2, 4]), ALU.mult)
        self.tt(oh1, oh1, oh2, ALU.add)
        self.tt(oh1, oh1, den.unsqueeze(2).to_broadcast([128, 2, 4]), ALU.mult)
        for t_ in range(2):
            t = self.tt(es[:, t_], goh[:, t_].unsqueeze(2).to_broadcast([128, 4, 4]),
                        oh1[:, t_].unsqueeze(1).to_broadcast([128, 4, 4]), ALU.mult)
        self.debug("gates", es, [t])
        gT = f(160, [16, 256])
        t = self.T4(gT, [es[:, 0].rearrange("p a b -> p (a b)"), es[:, 1].rearrange("p a b -> p (a b)")], [t], b=7)
        gb = self.gateb
        gw = []
        for p in range(8):
            b = 4 + p % 4
            for k in range(2):
                tk = self.mm(self.ps[:, b, 256 * k:256 * k + 256], self.sel16[:, 2 * p + k, :], gT, True, True,
                             [t, cw, self.bfree[b]])
            dst = gb[:, 2 * p:2 * p + 2, :].rearrange("p a b -> p (a b)")
            if p % 2:
                e = self.acopy(dst, self.ps[:, b, :], [tk, self.pjfree], chain=False)
            else:
                e = self.cp(dst, self.ps[:, b, :], [tk, self.pjfree], chain=False)
            self.bfree[b] = e
            gw.append(e)
        self.cw2 = self.Q.dma("act", lambda e: e.dma_start(self.w2, self.io["cw2"]), self.s_c[6], [tk])
        hf = [None, None]

        def down(e_, hid):
            n = self.take(("down", e_))
            m, th, tl = self.ready[n]
            for t_ in range(2):
                for c in range(2):
                    b = 2 * t_ + c
                    for k in range(2):
                        hi = self.mhid[:, e_ % 2, 0, k, t_ * 128:t_ * 128 + 128]
                        lo = self.mhid[:, e_ % 2, 1, k, t_ * 128:t_ * 128 + 128]
                        wh = self.whi[:, m, k * 1024 + c * 512:k * 1024 + c * 512 + 512]
                        wl = self.wlo[:, m, k * 1024 + c * 512:k * 1024 + c * 512 + 512]
                        s = e_ == 0 and k == 0
                        w = [hid, th, tl, self.bfree[b] if s else None]
                        self.mm(self.ps[:, b, :], hi, wh, s, False, w)
                        self.mm(self.ps[:, b, :], lo, wh, False, False)
                        tk = self.mm(self.ps[:, b, :], hi, wl, False, e_ == 15 and k == 1)
            self.give(n, tk)
            hf[e_ % 2] = tk
            return tk

        prev = None
        for e_ in range(16):
            ta, tb = self.up(("moe", e_), 0, (self.hhi, self.hlo), hs, False)
            hid = []
            for f_ in range(2):
                hid += self.hidden(f_, ta[f_], tb[f_], self.mhid[:, e_ % 2, 0, f_, :], self.mhid[:, e_ % 2, 1, f_, :],
                                   [hf[e_ % 2], self.pjfree], gate=gb[:, e_, :], gw=gw)
            self.fill()
            if prev is not None:
                down(e_ - 1, prev)
                self.fill()
            prev = hid
        self.hfree = tb[1]
        tk = down(15, prev)
        self.flush()
        self.xw = []
        for t_ in range(2):
            for c in range(2):
                b = 2 * t_ + c
                e = self.tt(self.x[:, t_, c * 512:c * 512 + 512], self.ps[:, b, :], self.x[:, t_, c * 512:c * 512 + 512],
                            ALU.add, [tk])
                self.bfree[b] = e
                self.xw.append(e)
        self.hidfree = [tk, self.xw]
        self.debug("x2", self.x[:, :, :], self.xw)

    def fill(self, k=1):
        for _ in range(k):
            if self.nada >= self.adagoal:
                return
            n = self.nada
            self.nada += 1
            l, j, half = n // 72, n // 2 % 36, n % 2
            slot, r = n % NADA, (n // 2) % NACC
            dst, src = self.adaw[:, slot, :], self.io["wada"][n]
            ld = self.Q.dma("sp", lambda e, dst=dst, src=src: e.dma_start(dst, src), self.s_ada[slot], self.adafree[slot])
            w = self.adaw[:, slot, :].rearrange("p (k c) -> p k c", k=4)
            acc = self.acc[:, r, :]
            c = self.ca[:, 4 * half:4 * half + 4].unsqueeze(2).to_broadcast([128, 4, 256])
            first = [ld, self.cact]
            t = self.ptt(w, w, c, ALU.mult, first)
            t = self.ptt(w[:, 0:2, :], w[:, 0:2, :], w[:, 2:4, :], ALU.add, [t])
            if half:
                t = self.ptt(w[:, 0, :], w[:, 0, :], w[:, 1, :], ALU.add, [t])
                t = self.ptt(acc, w[:, 0, :], acc, ALU.add, [t, self.adalast])
            else:
                t = self.ptt(acc, w[:, 0, :], w[:, 1, :], ALU.add, [t, self.accfree[r]])
            self.adafree[slot] = self.adalast = t
            if half:
                self.accs.append((l, j, r, t))

    def sum_acc(self, bank, keep):
        tk = None
        out = self.accs[:max(0, len(self.accs) - keep)]
        self.accs = self.accs[len(out):]
        for i, (l, j, r, t) in enumerate(out):
            for k in range(2):
                c = 256 + 2 * i + k
                tk = self.mm(self.ps[:, bank, c:c + 1], self.acc[:, r, 128 * k:128 * k + 128], self.ones[:, 0:1],
                             True, True, [t, self.bfree[bank]])
            self.accfree[r] = tk
        return out, tk

    def put_mod(self, bank, done, w):
        if not done:
            return None
        l, j, n = done[0][0], done[0][1], 2 * len(done)
        t = self.tt(self.mod2[:, 72 * l + 2 * j:72 * l + 2 * j + n], self.ps[:, bank, 256:256 + n],
                    self.col("bada")[:, 72 * l + 2 * j:72 * l + 2 * j + n], ALU.add, [w, self.cw], chain=False)
        for l, _, _, _ in done:
            self.modt[l] = t
        return t

    def flush(self, bank=7, keep=0):
        if len(self.accs) > keep:
            done, tk = self.sum_acc(bank, keep)
            self.bfree[bank] = self.put_mod(bank, done, tk)

    def ada(self, l):
        while self.nada < 72 * (l + 1):
            self.fill()
            if len(self.accs) >= 3:
                self.flush(keep=1)
        self.flush()
        self.adagoal = 144
        self.mod = self.mod2[:, 72 * l:72 * l + 72]
        self.debug("mod%d" % l, self.mod, [self.modt[l]])
        m4 = self.mod.rearrange("p (i s k) -> p i s k", i=3, s=3)
        ng = self.col("ng2")[:, 24 * l:24 * l + 24].rearrange("p (i k) -> p i k", i=3)
        self.modw = self.dve(lambda e: e.scalar_tensor_tensor(m4[:, :, 1, :], m4[:, :, 1, :], 1.0, ng, ALU.add, ALU.mult),
                             [self.modt[l], self.cw], True)

    def gate_rows(self, i):
        m4 = self.mod.rearrange("p (i s k) -> p i s k", i=3, s=3)
        f = 0.5 if i != 1 else 1.0
        gw = []
        for c in range(2):
            for k in range(4):
                dgt = self.dgt[:, k, :]
                col = m4[:, i, 2, 4 * c + k:4 * c + k + 1]
                d = self.ts(dgt, self.ident, col, ALU.mult, f, ALU.mult, w=[self.modw, self.dgtf[k]], chain=False)
                self.dgtf[k] = tk = self.mm(self.ps[:, 4 + c, 128 * k:128 * k + 128], self.ones[:, 0:128], dgt, True, True,
                                            [d, self.bfree[4 + c]])
            e = self.acopy(self.gbc[:, 512 * c:512 * c + 512], self.ps[:, 4 + c, :], [tk, self.gbcfree], chain=False)
            self.bfree[4 + c] = e
            gw.append(e)
        self.gw = gw

    def gated_add(self, i, t_, c, bank, tk):
        tmp = self.xn[:, t_, c:c + 512]
        a = self.tt(tmp, bank, self.gbc[:, c:c + 512], ALU.mult, [tk, self.gw, self.xnfree], chain=False)
        self.gbcfree = a
        xs = self.x[:, t_, c:c + 512]
        b = self.tt(xs, xs, tmp, ALU.add, [a], chain=False)
        self.xw.append(b)
        return a

    def ffn(self, l, i):
        mod = self.mod.rearrange("p (i s k) -> p i s k", i=3, s=3)
        hs = self.norm_T(mod[:, 2 * i, 1, :], mod[:, 2 * i, 0, :], self.modw)
        hid = []
        for j in range(11):
            ta, tb = self.up(("ffn", l, i), j, (self.hhi, self.hlo), hs, False)
            for f_ in range(2):
                ft = 2 * j + f_
                hid.append(self.hidden(f_, ta[f_], tb[f_], self.hidhi[:, ft, :], self.hidlo[:, ft, :], self.hidfree))
            self.fill()
        self.hfree = tb[1]
        self.flush()
        self.gate_rows(2 * i)
        for j in range(11):
            n = self.take(("w2", l, i, j))
            m, th, tl = self.ready[n]
            for t_ in range(2):
                for c in range(2):
                    b = 2 * t_ + c
                    for k in range(2):
                        ft = 2 * j + k
                        hi = self.hidhi[:, ft, t_ * 128:t_ * 128 + 128]
                        lo = self.hidlo[:, ft, t_ * 128:t_ * 128 + 128]
                        wh = self.whi[:, m, k * 1024 + c * 512:k * 1024 + c * 512 + 512]
                        wl = self.wlo[:, m, k * 1024 + c * 512:k * 1024 + c * 512 + 512]
                        s = j == 0 and k == 0
                        self.mm(self.ps[:, b, :], hi, wh, s, False, [hid[ft], th, tl, self.bfree[b] if s else None])
                        self.mm(self.ps[:, b, :], lo, wh, False, False)
                        tk = self.mm(self.ps[:, b, :], hi, wl, False, j == 10 and k == 1)
            self.give(n, tk)
            if j < 10:
                self.fill(1)
                self.flush(keep=1)
        self.hidfree = [tk]
        self.xw = []
        for t_ in range(2):
            for c in range(2):
                self.bfree[2 * t_ + c] = self.gated_add(2 * i, t_, 512 * c, self.ps[:, 2 * t_ + c, :], tk)
        self.xnfree = None
        self.debug("xf%d%d" % (l, i), self.x[:, :, :], self.xw)

    def rope_tables(self):
        f = self.rsc
        pos, ang, k, r = f(0, [128, 2]), f(2, [128, 2, 8]), f(18, [128, 2, 8]), f(34, [128, 2, 8])
        self.cp(pos, self.posi, [self.cw])
        for t_ in range(2):
            self.ts(ang[:, t_, :], self.row("inv"), pos[:, t_:t_ + 1], ALU.mult)
        two_pi = 2 * np.pi
        c1 = 6.28125
        c2 = float(np.float32(int((two_pi - c1) * 2 ** 20) / 2 ** 20))
        c3 = float(np.float32(two_pi - c1 - c2))
        magic = 12582912.0
        for out, quarter, add in ((self.sinT, 0.0, 0.0), (self.cosT, 0.25, float(np.pi / 2))):
            self.ts(k, ang, float(1 / two_pi), ALU.mult, quarter, ALU.add)
            self.ts(k, k, magic, ALU.add)
            self.ts(k, k, magic, ALU.subtract)
            self.dve(lambda e: e.scalar_tensor_tensor(r, k, -c1, ang, ALU.mult, ALU.add), [], True)
            self.dve(lambda e: e.scalar_tensor_tensor(r, k, -c2, r, ALU.mult, ALU.add), [], True)
            self.dve(lambda e: e.scalar_tensor_tensor(r, k, -c3, r, ALU.mult, ALU.add), [], True)
            self.ts(r, r, add, ALU.add)
            t = self.ts(r, r, 3.1415925, ALU.min, -3.1415925, ALU.max)
            t = self.af(out, r, ACT.Sin, [t])
            self.cp(pos, pos, [t])
        self.ropew = t
        self.debug("cos", self.cosT, [t])

    def rope(self, lo, nh, w):
        pj = self.pj2
        v = pj[:, :, lo:lo + 64 * nh].rearrange("p t (h d) -> p t h d", d=64)
        r1, r2 = v[:, :, :, 0:8], v[:, :, :, 8:16]
        sh = [128, 2, nh, 8]
        c = self.cosT.unsqueeze(2).to_broadcast(sh)
        s = self.sinT.unsqueeze(2).to_broadcast(sh)
        a, b, d, e = [self.rsc(64 + 160 * i, [128, 2, nh, 8]) for i in range(4)]
        self.tt(a, r1, c, ALU.mult, [w, self.ropew])
        self.tt(b, r2, s, ALU.mult, chain=False)
        self.tt(d, r1, s, ALU.mult, chain=False)
        self.tt(e, r2, c, ALU.mult, chain=False)
        t = self.tt(r1, a, b, ALU.subtract)
        return self.tt(r2, e, d, ALU.add)

    def mixer(self, l):
        pj = self.pj2
        cw = self.cw
        mod = self.mod.rearrange("p (i s k) -> p i s k", i=3, s=3)
        hs = self.norm_T(mod[:, 1, 1, :], mod[:, 1, 0, :], self.modw)
        pw = []

        def evac(c, t, bank, width, tk):
            if t == 0:
                e = self.acopy(pj[:, t, c:c + width], bank, [tk, self.hidfree], chain=False)
            else:
                e = self.cp(pj[:, t, c:c + width], bank, [tk, self.hidfree], chain=False)
            pw.append(e)
            return e

        last = self.proj_cb(("w_in2", l), 2844, (self.hhi, self.hlo), hs, evac)
        self.hfree = last
        for lo, nh in ((0, 10), (768, 2), (1024, 2), (2076, 8)):
            rw = self.rope(lo, nh, pw)
        self.debug("pj2", pj[:, :, :], [rw])
        sc = self.scr
        QN = sc(0, [128, 4, 256])
        KS = sc(4, [128, 2, 256])
        ZZ = sc(6, [128, 4, 256])
        A = sc(10, [128, 2, 16, 30])
        Ah = self.ahi
        Al = self.alo
        w0 = [rw, pw, last]
        mixf = self.mix.rearrange("p a b -> p (a b)")
        QR = mixf[:, 0:1024].rearrange("p (t h g d) -> p t h g d", t=2, h=4, g=2)
        DU = mixf[:, 1024:2048].rearrange("p (t j r d) -> p t j r d", t=2, j=4, r=2)
        wq, wd = [], []
        for t_ in range(2):
            src = pj[:, t_, 0:512].rearrange("p (g h d) -> p h g d", g=2, d=64)
            wq.append(self.cp(QR[:, t_], src, [w0, self.mixfree], chain=False))
            src = pj[:, t_, 512:768].rearrange("p (j d) -> p j d", d=64).unsqueeze(2).to_broadcast([128, 4, 2, 64])
            wd.append(self.acopy(DU[:, t_], src, [w0, self.mixfree], chain=False))
        tq = []
        for hp in range(2):
            for j in range(2):
                h = 2 * hp + j
                for t_ in range(2):
                    tk = self.tr(self.ps[:, hp, (2 * j + t_) * 128:(2 * j + t_) * 128 + 128], QR[:, t_, h].rearrange("p g d -> p (g d)"), [wq, self.bfree[hp]])
            e = self.cp(QN[:, 2 * hp:2 * hp + 2, :].rearrange("p a b -> p (a b)"), self.ps[:, hp, :], [tk, last], chain=False)
            self.bfree[hp] = e
            tq.append(e)
        tks = self.T4(KS[:, 0:2, :].rearrange("p a b -> p (a b)"),
                      [pj[:, 0, 768:896], pj[:, 1, 768:896], pj[:, 0, 1024:1152], pj[:, 1, 1024:1152]], w0, b=2, eng="act")
        tz = []
        for kv in range(2):
            for g in range(2):
                j = 2 * kv + g
                for t_ in range(2):
                    dup = DU[:, t_, j].rearrange("p r d -> p (r d)")
                    tk = self.tr(self.ps[:, 4 + kv, (2 * g + t_) * 128:(2 * g + t_) * 128 + 128], dup, [wd, self.bfree[4 + kv]])
            src = self.ps[:, 4 + kv, :].rearrange("p (g t) -> p g t", g=2)
            e1 = self.cp(ZZ[0:64, 2 * kv:2 * kv + 2, :], src[0:64], [tk, last], chain=False)
            e2 = self.cp(ZZ[64:128, 2 * kv:2 * kv + 2, 0:255], src[64:128, :, 1:256], [tk, last], chain=False)
            self.bfree[4 + kv] = [e1, e2]
            tz += [e1, e2]
        ta = []
        for kv in range(2):
            for g in range(2):
                for m in range(2):
                    v = ZZ[:, 2 * kv + g, :].rearrange("p (c k two) -> p k c two", k=8, two=2)[:, :, m:m + 15, 0]
                    p = self.col("pos")[:, 32 * l + 16 * kv + 8 * m:32 * l + 16 * kv + 8 * m + 8]
                    ta.append(self.tt(A[:, kv, 8 * m:8 * m + 8, 15 * g:15 * g + 15], v,
                                      p.unsqueeze(2).to_broadcast([128, 8, 15]), ALU.add, [tz, cw, self.afree], chain=False))
        th = self.acopy(Ah, A, [ta, self.afree])
        tl = self.tt(Al, A, Ah.bitcast(F32), ALU.subtract, [th])
        hg = sc(14, [30, 2, 256])
        HT = sc(16, [128, 2, 2, 30])
        KC = sc(17, [128, 30])
        VC = self.rsc(64, [15, 2, 64])
        th2 = []
        for kv in range(2):
            b = 4 + kv
            for half in range(2):
                n = self.take(("cw1", l, kv, half))
                m, wh_, wl_ = self.ready[n]
                for k in range(8):
                    kt = 8 * half + k
                    wh, wl = self.whi[:, m, 256 * k:256 * k + 256], self.wlo[:, m, 256 * k:256 * k + 256]
                    o_ = self.ps[0:30, b, 0:256]
                    self.mm(o_, Ah[:, kv, kt, :], wh, kt == 0, False, [tl, th, wh_, wl_, self.bfree[b]])
                    self.mm(o_, Al[:, kv, kt, :], wh, False, False)
                    tk = self.mm(o_, Ah[:, kv, kt, :], wl, False, kt == 15)
                self.give(n, tk)
            e = self.af(hg[:, kv, :], self.ps[0:30, b, 0:256], ACT.Gelu_apprx_tanh, [tk])
            self.bfree[b] = e
            for k in range(2):
                tk2 = self.tr(self.ps[:, 6 + kv, 128 * k:128 * k + 30], hg[:, kv, 128 * k:128 * k + 128], [e, self.bfree[6 + kv]])
            e = self.cp(HT[:, kv], self.ps[:, 6 + kv, 0:256].rearrange("p (a b) -> p a b", a=2)[:, :, 0:30], [tk2])
            self.bfree[6 + kv] = e
            th2.append(e)
        self.afree = tk
        for k in range(2):
            tk = self.mm(self.ps[:, 4, 0:30], self.cw2k[:, l, k, :], HT[:, 0, k, :], k == 0, k == 1, [th2, self.cw2, self.bfree[4]])
        ek = self.cp(KC, self.ps[:, 4, 0:30], [tk])
        self.bfree[4] = ek
        for g in range(2):
            for k in range(2):
                tk = self.mm(self.ps[0:15, 5, 64 * g:64 * g + 64], HT[:, 1, k, 15 * g:15 * g + 15], self.cw2v[:, l, k, :],
                             k == 0, k == 1, [th2, self.cw2, self.bfree[5]])
        ev = self.cp(VC, self.ps[0:15, 5, 0:128].rearrange("p (g d) -> p g d", g=2), [tk, rw])
        self.bfree[5] = ev
        self.debug("kc", KC, [ek])
        sg = self.frt(0, [128, 2, 24])
        tsg = self.af(sg, pj[:, :, 1280:1304], ACT.Sigmoid, [pw])
        sg4 = sg.rearrange("p t (h s) -> p t h s", s=3)
        for t_ in range(2):
            for h in range(8):
                g = h // 4
                c = (4 * t_ + h % 4) * 16
                tk = self.mm(self.ps[:, 6 + g, c:c + 15],
                             QN[64 * g:64 * g + 64, h % 4, 128 * t_:128 * t_ + 128],
                             KC[64 * g:64 * g + 64, 15 * g:15 * g + 15], True, True, [ek, tq, self.bfree[6 + g]])
        Sc = sc(18, [128, 2, 8, 15])
        for t_ in range(2):
            for g in range(2):
                pS = self.ps[:, 6 + g, 64 * t_:64 * t_ + 64].rearrange("p (a c) -> p a c", c=16)
                t = self.tt(Sc[:, t_, 4 * g:4 * g + 4], pS[:, :, 0:15],
                            self.cmask[:, t_, :].unsqueeze(1).to_broadcast([128, 4, 15]), ALU.add, [tk, cw])
        self.bfree[6] = self.bfree[7] = t
        S16 = Sc.rearrange("p t h c -> p (t h) c")
        mx, sm = self.st[:, 40:56], self.st[:, 56:72]
        self.dve(lambda e: e.tensor_reduce(mx, S16, X, ALU.max), [], True)
        self.ts(mx, mx, -1.0e30, ALU.max)
        t = self.tt(S16, S16, mx.unsqueeze(2).to_broadcast([128, 16, 15]), ALU.subtract)
        t = self.af(S16, S16, ACT.Exp, [t], scale=0.125)
        self.dve(lambda e: e.tensor_reduce(sm, S16, X, ALU.add), [t], True)
        self.ts(sm, sm, 1.0e-30, ALU.max)
        self.dve(lambda e: e.reciprocal(sm, sm), [], True)
        self.tt(sm.rearrange("p (t h) -> p t h", t=2), sm.rearrange("p (t h) -> p t h", t=2), sg4[:, :, :, 0], ALU.mult, [tsg])
        t = self.tt(S16, S16, sm.unsqueeze(2).to_broadcast([128, 16, 15]), ALU.mult)
        PC = self.att(0, [15, 16, 128])
        te = []
        for b in range(4):
            for j in range(4):
                tk = self.tr(self.ps[0:15, b, 128 * j:128 * j + 128], S16[:, 4 * b + j, :], [t, self.bfree[b]])
            e = self.cp(PC[:, 4 * b:4 * b + 4, :].rearrange("p a b -> p (a b)"), self.ps[0:15, b, :], [tk, self.afr()], chain=False)
            self.bfree[b] = e
            te.append(e)
        for t_ in range(2):
            for h in range(8):
                tk = self.mm(self.ps[:, 4 + t_, 64 * h:64 * h + 64], PC[:, 8 * t_ + h, :], VC[:, h // 4, :], True, True,
                             [te, ev, self.bfree[4 + t_]])
            e = self.cp(self.mix[:, t_, 0:512], self.ps[:, 4 + t_, :], [tk, self.mixfree, tq, tz])
            self.bfree[4 + t_] = e
        mixc = e
        self.debug("ocmp", self.mix[:, :, 0:512], [e])
        self.asfree = [[tk], [tk]]
        self.apfree = [tk, tk]
        self.aptfree = [tk, tk]
        for br, kc, vc in ((1, 0, 896), (2, 1, 1152)):
            heads = []
            for h in range(8):
                g = h // 4
                heads.append((QN[64 * g:64 * g + 64, h % 4, :], KS[64 * g:64 * g + 64, kc, :],
                              lambda t_, g=g, vc=vc: pj[:, t_, vc + 64 * g:vc + 64 * g + 64]))
            cf = self.frt(48, [128, 2, 8])

            def emit(i, t_, o_, ri, w, br=br):
                c = cf[:, t_, i:i + 1]
                a = self.tt(c, ri, sg4[:, t_, i, br:br + 1], ALU.mult, [w[1], tsg, mixc], chain=False)
                dst = self.mix[:, t_, 64 * i:64 * i + 64]
                return self.dve(lambda e: e.scalar_tensor_tensor(dst, o_, c, dst, ALU.mult, ALU.add), [a, w], False)

            ow = self.attention(heads, 64, 0.125, [tq, tks, w0], emit)
        lf, la = self.frt(64, [128, 2, 4]), self.frt(72, [128, 2, 4])
        t = self.tt(lf, pj[:, :, 2072:2076], self.row("foxb")[:, 4 * l:4 * l + 4].unsqueeze(1).to_broadcast([128, 2, 4]),
                    ALU.add, [cw, pw])
        t = self.log_sigmoid(lf, la, [t])
        F8 = sc(18, [1, 4, 256])
        nF = self.rsc(0, [1, 4, 256])
        for h in range(4):
            b = 4 + h // 2
            o_ = self.ps[0:1, b, 256 * (h % 2):256 * (h % 2) + 256]
            for t_ in range(2):
                tk = self.mm(o_, lf[:, t_, h:h + 1], self.triu[:, t_, :], t_ == 0, t_ == 1, [t, cw, self.bfree[b]])
        src = self.ps[0:1, 4:6, :].rearrange("p a (b c) -> p (a b) c", c=256)
        e1 = self.ts(F8, src, 8.0, ALU.mult, w=[tk])
        e2 = self.ts(nF, src, -8.0, ALU.mult, w=[tk])
        self.bfree[4] = self.bfree[5] = e2
        QF = sc(6, [128, 4, 256])
        QM = sc(10, [128, 4, 256])
        tf = []
        for base, dst in ((1304, QF), (2076, QM)):
            for j in range(2):
                a, b_ = base + 128 * j, base + 256 + 128 * j
                bnk = 6 + j
                tf.append(self.T4(dst[:, 2 * j:2 * j + 2, :].rearrange("p a b -> p (a b)"),
                                  [pj[:, 0, a:a + 128], pj[:, 1, a:a + 128], pj[:, 0, b_:b_ + 128], pj[:, 1, b_:b_ + 128]],
                                  [w0, ow], free=self.afree, b=bnk, eng="act" if j else "dve"))

        def extra(i, o_, qt, kn):
            self.mm(o_, F8[0:1, i, 128 * qt:128 * qt + 128], self.ones[0:1, 0:kn], False, False, [e1, e2])
            return self.mm(o_, self.ones[0:1, 0:128], nF[0:1, i, 0:kn], False, True)

        for base, Q_, vcol, ex in ((512, QF, 1816, extra), (768, QM, 2588, None)):
            heads = []
            for h in range(4):
                P = slice(64 * (h % 2), 64 * (h % 2) + 64)
                heads.append((Q_[P, 2 * (h // 2), :], Q_[P, 2 * (h // 2) + 1, :],
                              lambda t_, h=h, vcol=vcol: pj[:, t_, vcol + 64 * h:vcol + 64 * h + 64]))

            def emit2(i, t_, o_, ri, w, base=base):
                return self.ts(self.mix[:, t_, base + 64 * i:base + 64 * i + 64], o_, ri, ALU.mult, w=[w, self.mixfree], chain=False)

            ow = [ow, self.attention(heads, 64, 0.125, [tf], emit2, extra=ex)]
        self.debug("mix2", self.mix[:, :, :], [ow])
        self.hfree = [ow]
        hs, tl = self.to_T(self.mix, ow)
        self.mixfree = tl
        self.hidfree = [ow, tl]

        def evac2(c, t, bank, width, tk):
            return self.gated_add(1, t, c, bank, tk)

        self.dgtf = [ow] * 4
        self.gate_rows(1)
        self.xw = []
        self.hfree = self.proj_cb(("w_out2", l), 1024, (self.hhi, self.hlo), hs, evac2)
        self.xnfree = None
        self.debug("xm%d" % l, self.x[:, :, :], self.xw)

    def afr(self):
        return [self.asfree, self.apfree, self.aptfree, self.pjfree]

    def final(self):
        tn = []
        for t in range(2):
            tn.append(self.af(self.xn[:, t, :], self.x[:, t, :], ACT.Square, [self.xw, self.xnfree],
                              accum_out=self.st[:, t:t + 1]))
        r = self.rstd(self.st[:, 2:4], self.st[:, 0:2], D, tn)
        fg = self.fing
        dl = self.Q.dma("sp", lambda e: e.dma_start(fg, self.io["fing"].to_broadcast([128, D])), self.s_fg, [self.hfree])
        out = self.io["out"].rearrange("b (t p) d -> p (b t) d", p=128)
        for t in range(2):
            o = self.xn[:, t, :]
            e = self.dve(lambda e, t=t, o=o: e.scalar_tensor_tensor(o, self.x[:, t, :], self.st[:, 2 + t:3 + t], fg,
                                                                    ALU.mult, ALU.mult), [r, dl], True)
            self.Q.dma("sp", lambda e, t=t, o=o: e.dma_start(out[:, t, :], o), self.s_out, [e])

    def col(self, name):
        a, n = COFF[name]
        return self.colp[:, a:a + n]

    def row(self, name):
        a, n = ROFF[name]
        return self.rowp[:, a:a + n]

    def build(self):
        nc, io = self.nc, self.io
        with ExitStack() as ctx:
            def sb(name, shape, dt=F32):
                return ctx.enter_context(nc.sbuf_tensor(name, shape, dt))

            self.ps = ctx.enter_context(nc.psum_tensor("ps", [128, 8, 512], F32))[:, :, :]
            self.raw = sb("raw", [128, NRAW, UW])[:, :, :]
            self.whi = sb("whi", [128, NSPL, UW], F32R)[:, :, :]
            self.wlo = sb("wlo", [128, NSPL, UW], F32R)[:, :, :]
            self.x = sb("x", [128, 2, D])[:, :, :]
            def over(name, shape):
                at = (nc.sbuf_base + 31) // 32 * 32
                base = sb(name, shape)
                assert nc.sbuf_base == at + 4 * shape[1]
                return base, nc.alloc_sbuf_tensor_at(name + "_r", shape, F32R, offset=at)

            hreg, hr = over("hreg", [128, 6144])
            self.hhi = hr[:, 0:2048].rearrange("p (a b) -> p a b", b=256)
            self.hlo = hr[:, 2048:4096].rearrange("p (a b) -> p a b", b=256)
            self.xn = hreg[:, 4096:6144].rearrange("p (a b) -> p a b", a=2)
            self.xnT = hreg[:, 4096:6144].rearrange("p (a b) -> p a b", b=256)
            self.fing = hreg[:, 0:1024]
            ireg, ir = over("ireg", [128, 11264])
            self.hidhi = ir[:, 0:5632].rearrange("p (a b) -> p a b", b=256)
            self.hidlo = ir[:, 5632:11264].rearrange("p (a b) -> p a b", b=256)
            self.pj1 = ireg[:, 0:5664].rearrange("p (a b) -> p a b", a=2)
            self.pj2 = ireg[:, 0:5688].rearrange("p (a b) -> p a b", a=2)
            self.gateb = ireg[:, 0:4096].rearrange("p (a b) -> p a b", b=256)
            self.mhid = ir[:, 4096:6144].rearrange("p (a b c d) -> p a b c d", a=2, b=2, c=2)
            at = 5696
            self.asb = ireg[:, at:at + 1536].rearrange("p (a b c) -> p a b c", a=2, b=2)
            self.apb = ireg[:, at + 1536:at + 3072].rearrange("p (a b c) -> p a b c", a=2, b=2)
            self.apt = ireg[:, at + 3072:at + 4608].rearrange("p (a b c) -> p a b c", a=2, b=2)
            self.frt_at = at + 4608
            self.mix = sb("mix", [128, 2, D])[:, :, :]
            mixf = self.mix.rearrange("p a b -> p (a b)")
            self.hT = mixf.rearrange("p (a b) -> p a b", b=256)
            self.sil = mixf[:, 0:1024].rearrange("p (a b) -> p a b", b=256)
            self.prd = mixf[:, 1024:2048].rearrange("p (a b) -> p a b", b=256)
            greg = sb("greg", [128, 3072])
            self.gbc = greg[:, 0:1024]
            self.mod2 = sb("mod", [128, 144])[:, :]
            self.acc = sb("acc", [128, NACC, 256])[:, :, :]
            self.adaw = sb("adaw", [128, NADA, 1024])[:, :, :]
            self.ca = sb("ca", [128, 8])[:, :]
            self.colp = sb("colp", [128, NCOL])[:, :]
            self.rowp = sb("rowp", [128, NROW])[:, :]
            cst = sb("cst", [128, NCST])
            def c_(name):
                a, n = CSOFF[name]
                return cst[:, a:a + n]
            self.ident, self.ones, self.mask = c_("ident"), c_("ones"), c_("mask")
            self.triu = c_("triu").rearrange("p (a b) -> p a b", a=2)
            self.mhalf, self.iom4 = c_("mhalf"), c_("iom4")
            self.cmask = c_("cmask").rearrange("p (a b) -> p a b", a=2)
            gf = greg[:, :]
            self.gmask = gf[:, 0:1024].rearrange("p (a b) -> p a b", b=128)
            self.sel16 = gf[0:16, 1024:3072].rearrange("p (a b) -> p a b", b=128)
            self.rw = sb("rw", [128, 8, 20])[:, :, :]
            w2 = greg[:, 1024:1792]
            self.w2 = w2
            self.cw2k = w2[:, 0:512].rearrange("p (l k c) -> p l k c", l=2, k=2)
            self.cw2v = w2[:, 512:768].rearrange("p (l k c) -> p l k c", l=2, k=2)
            self.posi = sb("posi", [128, 2], I32)[:, :]
            self.st = sb("st", [128, 72])[:, :]
            self.st2 = sb("st2", [128, 48])[:, :]
            self.cosT = sb("cosT", [128, 2, 8])[:, :, :]
            self.sinT = sb("sinT", [128, 2, 8])[:, :, :]
            rs = sb("rs", [128, 1088])
            self.dgt = rs[:, 512:1024].rearrange("p (a b) -> p a b", b=128)
            an = sb("an", [128, 40])
            self.amx = an[:, 0:8].rearrange("p (a b c) -> p a b c", a=2, b=2)
            self.anm = an[:, 8:16].rearrange("p (a b c) -> p a b c", a=2, b=2)
            self.ars = an[:, 16:24].rearrange("p (a b c) -> p a b c", a=2, b=2)
            self.ari = an[:, 24:32].rearrange("p (a b c) -> p a b c", a=2, b=2)
            hr2 = hreg[:, :]

            def view(base, at, shape):
                n = int(np.prod(shape[1:]))
                v = base[0:shape[0], at:at + n]
                names = "abcd"[:len(shape) - 1]
                if len(shape) == 2:
                    return v
                pat = "p (%s) -> p %s" % (" ".join(names), " ".join(names))
                return v.rearrange(pat, **{k: s for k, s in zip(names, shape[1:])})

            self.scr = lambda kb, shape: view(hr2, kb * 256, shape)
            self.att = lambda kb, shape: view(ireg[:, :], at + kb * 256, shape)
            self.frt = lambda o, shape: view(ireg[:, :], self.frt_at + o, shape)
            self.rsc = lambda o, shape: view(rs[:, :], o, shape)
            areg = ir[:, at + 2048:at + 3968]
            self.ahi = areg[:, 0:960].rearrange("p (a b c) -> p a b c", a=2, b=16)
            self.alo = areg[:, 960:1920].rearrange("p (a b c) -> p a b c", a=2, b=16)

            sems = {e: ctx.enter_context(nc.semaphore("s_" + e)) for e in ("pe", "dve", "act", "pool", "sp")}
            self.s_raw = [ctx.enter_context(nc.semaphore(f"s_raw{i}")) for i in range(NRAW)]
            self.s_c = [ctx.enter_context(nc.semaphore(f"s_c{i}")) for i in range(8)]
            self.s_ada = [ctx.enter_context(nc.semaphore(f"s_ada{i}")) for i in range(NADA)]
            self.s_out = ctx.enter_context(nc.semaphore("s_out"))
            self.s_fg = ctx.enter_context(nc.semaphore("s_fg"))

            self.Q = Queues(nc, sems)
            self.nunit = self.nload = self.nahead = self.nsplit = 0
            self.upn = self.hr = 0
            self.loaded, self.ready = [], {}
            self.rawfree = [[] for _ in range(NRAW)]
            self.splfree = [[] for _ in range(NSPL)]
            self.bfree = [None] * 8
            self.silfree = [None] * 4
            self.xnfree = self.hfree = self.pjfree = self.mixfree = None
            self.hidfree = self.modfree = self.gbcfree = self.afree = None
            self.dgtf = [None] * 4
            self.asfree, self.apfree, self.aptfree = [None] * 2, [None] * 2, [None] * 2
            self.anfree, self.arfree, self.aifree = [None] * 2, [None] * 2, [None] * 2

            ld = lambda i, dst, src: self.Q.dma("act", lambda e: e.dma_start(dst, src), self.s_c[i])
            xt = [ld(0, self.x, io["x"].rearrange("b (t p) d -> p (b t) d", p=128))]
            self.xw = xt
            self.cw = [ld(1, self.colp, io["colp"]), ld(2, self.rowp, io["rowp"].to_broadcast([128, NROW])),
                       ld(3, cst[:, :], io["cst"]), ld(4, gf, io["cst2"]), ld(5, self.rw, io["rw"]),
                       ld(7, self.posi, io["pos"])]
            self.nada, self.adafree, self.adalast = 0, [None] * NADA, None
            self.adagoal = 72
            self.accs, self.accfree, self.modt, self.modlate = [], [None] * NACC, [None] * 2, None
            self.cact = self.af(self.ca, self.col("c"), ACT.Silu, [self.cw])
            self.run_stages()

            self.left = nc.sbuf_usable_end - nc.sbuf_base
            self.Q.number()
            block = ctx.enter_context(nc.Block())
            Q = self.Q
            n_out = Q.dma_count.get(id(self.s_out), 0)

            @block.sync
            def _(e):
                Q.run("sp", e)
                e.wait_ge(self.s_out, n_out)

            @block.scalar
            def _(e):
                Q.run("act", e)

            @block.vector
            def _(e):
                Q.run("dve", e)

            @block.gpsimd
            def _(e):
                Q.run("pool", e)

            @block.tensor
            def _(e):
                Q.run("pe", e)

    def run_stages(self):
        s = self.stage
        self.first_mixer()
        if s >= 2:
            self.moe()
        if s >= 3:
            self.rope_tables()
            for l in range(2):
                if l == 0:
                    self.gbcfree = self.xw
                self.ada(l)
                self.ffn(l, 0)
                if s >= 4:
                    self.mixer(l)
                    self.ffn(l, 1)
                if s < 5:
                    break
        self.final()


CONSTS = [("ident", 128), ("ones", 256), ("mask", 384), ("triu", 512), ("mhalf", 32), ("iom4", 8), ("cmask", 30)]
CSOFF, NCST = offsets(CONSTS)


def constants():
    f = np.float32
    c = np.zeros((128, NCST), f)
    p = np.arange(128)

    def put(name, a):
        at, n = CSOFF[name]
        c[:, at:at + n] = np.asarray(a, f).reshape(128, n)

    put("ident", np.eye(128))
    put("ones", np.ones((128, 256)))
    k = np.arange(256)
    put("mask", np.concatenate([np.where(k[None, :128] <= p[:, None], 0, NEG),
                                np.where(k[None, :] <= 128 + p[:, None], 0, NEG)], 1))
    put("triu", np.stack([(128 * t + p[:, None] <= k[None, :]) for t in range(2)], 1))
    put("mhalf", np.full((128, 32), -0.5))
    put("iom4", np.tile(np.arange(4) - 4, (128, 2)))
    ce = np.arange(15) * 16 + 31
    put("cmask", np.stack([np.where(ce[None, :] <= 128 * t + p[:, None], 0, NEG) for t in range(2)], 1))
    c2 = np.zeros((128, 3072), f)
    g = np.zeros((128, 8, 128), f)
    j, i = p[:, None], p[None, :]
    for n, s in enumerate([64, 32, 16, 8, 4, 2, 1]):
        g[:, n, :] = (j // (2 * s) == i // (2 * s)) & (j % (2 * s) < s) & (i % (2 * s) >= s)
    g[:, 7, :] = np.eye(128)
    c2[:, 0:1024] = g.reshape(128, 1024)
    for e in range(16):
        c2[e, 1024 + 128 * e:1152 + 128 * e] = 1.0
    return c, c2


def tall(w):
    return w.reshape(w.shape[0] // 128, 128, -1).transpose(1, 0, 2).reshape(128, -1)


def unit(inp, key):
    name = key[0]
    kind = name[0] if isinstance(name, tuple) else name
    if kind in ("w_in", "w_out", "w_in2", "w_out2"):
        w = inp[{"w_in": "w_in", "w_out": "w_out", "w_in2": "w_in_2", "w_out2": "w_out_2"}[kind]][name[1]]
        c, half = key[1], key[2]
        return tall(w[512 * half:512 * half + 512, c:c + 512])
    if kind == "moe":
        w = inp["expert_w_gate" if key[1] == "a" else "expert_w_up"][0, name[1]]
        return tall(w)
    if kind == "down":
        return tall(inp["expert_w_down"][0, key[1]])
    if kind == "ffn":
        c = 256 * key[2] + (0 if key[1] == "a" else 2816)
        return tall(inp["ffn_w13_2"][name[1], name[2]][:, c:c + 256])
    if kind == "w2":
        _, l, i, j = key
        return tall(inp["ffn_w2_2"][l, i][256 * j:256 * j + 256])
    if kind == "cw1":
        _, l, kv, half = key
        return tall(inp["cmp_w1_2"][l, kv][1024 * half:1024 * half + 1024])
    raise KeyError(key)


def stream(inp, order):
    out = np.zeros((len(order), 128, UW), np.float32)
    for n, (key, width) in enumerate(order):
        out[n, :, :width] = unit(inp, key)
    return out


def ada_stream(inp):
    w = inp["w_ada_2"].reshape(2, 2, 4, 128, 36, 256)
    return np.ascontiguousarray(w.transpose(0, 4, 1, 3, 2, 5)).reshape(144, 128, 1024)


def cols(v):
    return np.ascontiguousarray(v.reshape(-1, 128).T)


def small_inputs(inp):
    f = np.float32
    colp = np.zeros((128, NCOL), f)

    def put(name, a):
        at, n = COFF[name]
        colp[0:a.shape[0], at:at + n] = a.reshape(a.shape[0], n)

    put("mixg", cols(inp["mix_norm_g"]))
    put("ffng", cols(inp["ffn_norm_g"]))
    put("ng2", cols(inp["norm_g_2"]))
    put("glab", cols(inp["gla_gate_b"]))
    put("convb", cols(inp["conv_b"]))
    put("convw", inp["conv_w"][0].T.reshape(2, 128, 31).transpose(1, 0, 2))
    put("c", cols(inp["c_2"]))
    put("bada", cols(inp["b_ada_2"]))
    put("pos", cols(inp["cmp_pos_2"]))
    put("glaw", inp["gla_gate_w"][0])
    rowp = np.zeros((1, NROW), f)

    def row(name, a):
        at, n = ROFF[name]
        rowp[0, at:at + n] = a.reshape(-1)

    row("glang", inp["gla_norm_g"])
    row("cng", inp["conv_norm_g"])
    row("cnb", inp["conv_norm_b"])
    row("qn", inp["diff_qnorm_g"])
    row("kn", inp["diff_knorm_g"])
    row("lq1", inp["diff_lq1"])
    row("lk1", inp["diff_lk1"])
    row("lq2", inp["diff_lq2"])
    row("lk2", inp["diff_lk2"])
    row("subg", inp["diff_subln_g"])
    row("rb", np.concatenate([inp["router_group_b"][0], inp["router_expert_b"][0]]))
    row("foxb", inp["fox_fbias_2"])
    row("inv", np.float32(500000.0) ** (-np.arange(0, 16, 2, dtype=f) / f(16)))
    rw = np.concatenate([inp["router_group_w"][0], inp["router_expert_w"][0]], 1)
    rw = np.ascontiguousarray(rw.reshape(8, 128, 20).transpose(1, 0, 2))
    w2 = inp["cmp_w2_2"].reshape(2, 2, 2, 128, 64)
    wk = np.concatenate([w2[:, 0], w2[:, 0]], -1).transpose(2, 0, 1, 3).reshape(128, 512)
    wv = w2[:, 1].transpose(2, 0, 1, 3).reshape(128, 256)
    cw2 = np.ascontiguousarray(np.concatenate([wk, wv], 1))
    pos = np.ascontiguousarray(inp["positions_2"].reshape(2, 128).T)
    c, c2 = constants()
    return {"x": np.ascontiguousarray(inp["x"]), "colp": colp, "rowp": rowp, "rw": rw, "cw2": cw2, "pos": pos,
            "cst": c, "cst2": c2, "fing": np.ascontiguousarray(inp["final_g_2"].reshape(1, D))}


SHAPES = {"x": (1, 256, D), "colp": (128, NCOL), "rowp": (1, NROW), "rw": (128, 8, 20), "cw2": (128, 768),
          "cst": (128, NCST), "cst2": (128, 3072), "fing": (1, D)}


def program(nc, order, split, stage=9, dbg=None):
    io = {k: nc.dram_tensor("in_" + k, s, F32, kind="ExternalInput").ap() for k, s in SHAPES.items()}
    io["pos"] = nc.dram_tensor("in_pos", (128, 2), I32, kind="ExternalInput").ap()
    io["wu"] = nc.dram_tensor("in_wu", (len(order) if order else 400, 128, UW), F32, kind="ExternalInput").ap()
    io["wada"] = nc.dram_tensor("in_wada", (144, 128, 1024), F32, kind="ExternalInput").ap()
    io["out"] = nc.dram_tensor("out_0", (1, 256, D), F32, kind="ExternalOutput").ap()
    dd = {k: nc.dram_tensor("dbg_" + k, s, F32, kind="ExternalOutput").ap() for k, s in (dbg or {}).items()}
    b = Build(nc, io, order, order is None, stage, dd)
    b.order_split = split if order else {}
    if order is None:
        b.order = []
    b.build()
    return b.asked, b.order_split


def kernel(**inputs):
    import concourse.bacc as bacc
    from concourse.bass_utils import run_bass_kernel_spmd

    inp = {k: np.asarray(v) for k, v in inputs.items()}
    order, split = program(bacc.Bacc("TRN2", target_bir_lowering=False, num_devices=1), None, None)
    nc = bacc.Bacc("TRN2", target_bir_lowering=False, num_devices=1)
    program(nc, order, split)
    arrays = {"in_" + k: v for k, v in small_inputs(inp).items()}
    arrays["in_wu"] = stream(inp, order)
    arrays["in_wada"] = ada_stream(inp)
    r = run_bass_kernel_spmd(nc, [arrays], core_ids=[0])
    return r.results[0]["out_0"]
```

```python
from contextlib import ExitStack

import numpy as np
import concourse.bass as bass
from concourse import mybir

ALU = mybir.AluOpType
ACT = mybir.ActivationFunctionType
F32 = mybir.dt.float32
F32R = mybir.dt.float32r
I32 = mybir.dt.int32
X = mybir.AxisListType.X

D = 1024
EPS = 1e-6
UW = 2048
NRAW = 4
NADA = 2
NSPL = 3
NACC = 4
NEG = -3.0e38

COLS = [("mixg", 8), ("ffng", 8), ("ng2", 48), ("glab", 1), ("convb", 2), ("convw", 62),
        ("c", 8), ("bada", 144), ("pos", 64), ("glaw", 128)]
ROWS = [("glang", 64), ("cng", 256), ("cnb", 256), ("qn", 64), ("kn", 64), ("lq1", 64), ("lk1", 64),
        ("lq2", 64), ("lk2", 64), ("subg", 128), ("rb", 20), ("foxb", 8), ("inv", 8)]


def offsets(table):
    at, out = 0, {}
    for name, n in table:
        out[name] = (at, n)
        at += n
    return out, at


COFF, NCOL = offsets(COLS)
ROFF, NROW = offsets(ROWS)


class Tok:

    def __init__(self, eng, sem=None, value=None):
        self.eng, self.sem, self.value, self.used = eng, sem, value, False


class Queues:

    def __init__(self, nc, sems):
        self.nc, self.sems = nc, sems
        self.q = {e: [] for e in sems}
        self.last = {}
        self.dma_count = {}
        self.bar = {}

    def put(self, eng, fn, waits=(), chain=False):
        tok = Tok(eng)
        flat = []

        def add(w):
            if w is None:
                return
            if isinstance(w, Tok):
                w.used = True
                flat.append(w)
            else:
                for v in w:
                    add(v)

        add(waits)
        if eng in self.bar:
            flat.append(self.bar.pop(eng))
        if chain and eng in self.last:
            add(self.last[eng])
        self.q[eng].append((fn, flat, tok))
        self.last[eng] = tok
        return tok

    def dma(self, eng, fn, sem, waits=()):
        flat = []

        def add(w):
            if w is None:
                return
            if isinstance(w, Tok):
                w.used = True
                flat.append(w)
            else:
                for v in w:
                    add(v)

        add(waits)
        n = self.dma_count.get(id(sem), 0) + 16
        self.dma_count[id(sem)] = n
        tok = Tok("dma", sem, n)
        self.q[eng].append((lambda e: fn(e).then_inc(sem, 16), flat, None))
        return tok

    def number(self):
        for eng, items in self.q.items():
            n = 0
            for _, _, tok in items:
                if tok is not None and tok.used:
                    n += 1
                    tok.sem, tok.value = self.sems[eng], n

    def run(self, eng, e):
        seen = {}
        for fn, waits, tok in self.q[eng]:
            need = {}
            for w in waits:
                k = id(w.sem)
                if w.value > max(seen.get(k, 0), need.get(k, (None, 0))[1]):
                    need[k] = (w.sem, w.value)
            for k, (s, v) in need.items():
                e.wait_ge(s, v)
                seen[k] = v
            ins = fn(e)
            if tok is not None and tok.used:
                ins.then_inc(tok.sem, 1)


class Build:
    def __init__(self, nc, io, order, dry, stage, dbg):
        self.nc, self.io, self.order, self.dry = nc, io, order, dry
        self.stage, self.dbg = stage, dbg
        self.asked = []

    def pe(self, fn, w=()):
        return self.Q.put("pe", fn, w)

    def dve(self, fn, w=(), chain=True):
        return self.Q.put("dve", fn, w, chain)

    def act(self, fn, w=(), chain=True):
        return self.Q.put("act", fn, w, chain)

    def pool(self, fn, w=(), chain=True):
        return self.Q.put("pool", fn, w, chain)

    def tt(self, out, a, b, op, w=(), chain=True):
        return self.dve(lambda e: e.tensor_tensor(out, a, b, op), w, chain)

    def ptt(self, out, a, b, op, w=()):
        return self.pool(lambda e: e.tensor_tensor(out, a, b, op), w, False)

    def ts(self, out, a, s1, op0, s2=None, op1=None, w=(), chain=True):
        if op1 is None:
            return self.dve(lambda e: e.tensor_scalar(out, a, s1, None, op0), w, chain)
        return self.dve(lambda e: e.tensor_scalar(out, a, s1, s2, op0, op1), w, chain)

    def cp(self, out, a, w=(), chain=True):
        return self.dve(lambda e: e.tensor_copy(out, a), w, chain)

    def acopy(self, out, a, w=(), chain=True, scale=1.0):
        return self.act(lambda e: e.activation(out, a, ACT.Copy, scale=scale), w, chain)

    def af(self, out, a, f, w=(), chain=True, **kw):
        return self.act(lambda e: e.activation(out, a, f, **kw), w, chain)

    def mm(self, out, lhsT, rhs, start, stop, w=()):
        return self.pe(lambda e: e.matmul(out, lhsT, rhs, start=start, stop=stop), w)

    def tr(self, out, in_, w=()):
        ident = self.ident[0:in_.shape[0], 0:in_.shape[0]]
        return self.pe(lambda e: e.transpose(out, in_, ident), [w, self.cw])

    def debug(self, name, ap, w):
        if name in self.dbg and not self.dry:
            t = self.Q.dma("sp", lambda e: e.dma_start(self.dbg[name], ap), self.s_out, w)
            self.Q.bar = {e: t for e in ("pe", "dve", "act", "pool")}

    def load(self, n):
        key, width = self.order[n]
        slot = n % NRAW
        raw = self.raw[:, slot, 0:width]
        src = self.io["wu"][n, :, 0:width]
        self.loaded.append(self.Q.dma("sp", lambda e: e.dma_start(raw, src), self.s_raw[slot],
                                      self.rawfree[slot]))
        self.rawfree[slot] = None

    def split(self, n):
        key, width = self.order[n]
        slot, m = n % NRAW, self.nsplit % NSPL
        self.nsplit += 1
        raw = self.raw[:, slot, 0:width]
        hi, lo = self.whi[:, m, 0:width], self.wlo[:, m, 0:width]
        th = self.acopy(hi, raw, [self.loaded[n], self.splfree[m]], chain=False)
        tl = self.tt(lo, raw, hi.bitcast(F32), ALU.subtract, [self.loaded[n], th, self.splfree[m]], chain=False)
        self.rawfree[slot] = [th, tl]
        self.splfree[m] = None
        self.ready[n] = (m, th, tl)

    def take(self, key, width=UW, split=True):
        n = self.nunit
        self.nunit += 1
        self.asked.append((key, width))
        if self.dry:
            self.order.append((key, width))
            self.order_split[n] = split
        assert self.order[n] == (key, width)
        total = n + 1 if self.dry else len(self.order)
        self.ahead(n)
        return n

    def ahead(self, n):
        total = n + 1 if self.dry else len(self.order)
        k = max(self.nload, n)
        while self.nload < min(n + NRAW, total):
            if self.nload - NRAW >= 0 and self.rawfree[self.nload % NRAW] is None:
                break
            self.load(self.nload)
            self.nload += 1
        while self.nahead < min(n + NSPL, total, self.nload):
            if self.order_split[self.nahead]:
                if self.nsplit >= NSPL and self.splfree[self.nsplit % NSPL] is None:
                    break
                self.split(self.nahead)
            self.nahead += 1
            while self.nload < min(n + NRAW, total) and self.rawfree[self.nload % NRAW] is not None:
                self.load(self.nload)
                self.nload += 1
        assert self.nahead > n, (n, self.nahead, self.nload)

    def give(self, n, tok):
        if self.order_split[n]:
            self.splfree[self.ready[n][0]] = tok
        else:
            self.rawfree[n % NRAW] = tok

    def lin_rows(self, bank, hT, hw, kts, n, off, width, step, t, first, last, w=()):
        m, th, tl = self.ready[n]
        hi, lo = hT
        tok = None
        for i, kt in enumerate(kts):
            wh = self.whi[:, m, off + i * step:off + i * step + width]
            wl = self.wlo[:, m, off + i * step:off + i * step + width]
            xh, xl = hi[:, kt, t * 128:t * 128 + 128], lo[:, kt, t * 128:t * 128 + 128]
            f = first and i == 0
            la = last and i == len(kts) - 1
            self.mm(bank, xh, wh, f, False, [w, hw[kt // 2], th] if i == 0 else hw[kt // 2])
            self.mm(bank, xl, wh, False, False)
            tok = self.mm(bank, xh, wl, False, la, [tl] if i == 0 else ())
        return tok

    def up(self, name, j, hT, hw, first):
        n1 = self.take((name, "a", j))
        self.acc_a = n1
        outs = []
        m1, th1, tl1 = self.ready[n1]
        hi, lo = hT
        ab = []

        def tile(n, f, bank, w):
            m, th, tl = self.ready[n]
            for kt in range(8):
                c = kt * 256 + f * 128
                wh, wl = self.whi[:, m, c:c + 128], self.wlo[:, m, c:c + 128]
                self.mm(bank, wh, hi[:, kt, :], kt == 0, False, [w, hw[kt // 2], th] if kt == 0 else hw[kt // 2])
                self.mm(bank, wh, lo[:, kt, :], False, False)
                tok = self.mm(bank, wl, hi[:, kt, :], False, kt == 7, [tl] if kt == 0 else ())
            return tok

        ta = [None, None]
        for f in range(2):
            ta[f] = tile(n1, f, self.ps[:, 4 + f, 0:256], [self.bfree[4 + f]])
        self.give(n1, ta[1])
        n2 = self.take((name, "b", j))
        tb = [None, None]
        done = []
        for f in range(2):
            if f == 1 and len(self.accs) > 1:
                done, tk = self.sum_acc(7, 1)
            tb[f] = tile(n2, f, self.ps[:, 6 + f, 0:256], [self.bfree[6 + f]])
        self.give(n2, tb[1])
        self.modlate = self.put_mod(7, done, tb[1])
        return ta, tb

    def hidden(self, f, ta, tb, hi, lo, free, gate=None, gw=None):
        r = self.hr % 4
        self.hr += 1
        s, p = self.sil[:, r, :], self.prd[:, r, :]
        t1 = self.af(s, self.ps[:, 4 + f, 0:256], ACT.Silu, [ta, self.silfree[r]], chain=False)
        self.bfree[4 + f] = t1
        late = self.modlate if f == 1 else None
        if gate is not None:
            t0 = self.tt(p, self.ps[:, 6 + f, 0:256], gate, ALU.mult, [tb, gw, self.silfree[r]], chain=False)
            self.bfree[6 + f] = [t0, late]
            t2 = self.tt(p, p, s, ALU.mult, [t1, t0], chain=False)
        else:
            t2 = self.tt(p, self.ps[:, 6 + f, 0:256], s, ALU.mult, [tb, t1, self.silfree[r]], chain=False)
            self.bfree[6 + f] = [t2, late]
        t3 = self.acopy(hi, p, [t2, free], chain=False)
        t4 = self.tt(lo, p, hi.bitcast(F32), ALU.subtract, [t3, free], chain=False)
        self.silfree[r] = [t3, t4]
        return [t3, t4]

    def rstd(self, out, ss, n, w):
        m = ss.shape[-1]
        t = self.ts(out, ss, 1.0 / n, ALU.mult, EPS, ALU.add, w)
        return self.pool(lambda e: e.tensor_tensor(out, out, self.mhalf[:, 0:m], ALU.pow), [t, self.cw])

    def norm_T(self, g, shift, gw):
        dg, sq = [], []
        for t in range(2):
            tk = self.af(self.xn[:, t, :], self.x[:, t, :], ACT.Square, [self.xw[t], self.xnfree], chain=False,
                         accum_out=self.st[:, t:t + 1])
            sq.append(tk)
            r = self.rstd(self.st[:, 2 + t:3 + t], self.st[:, t:t + 1], D, [tk])
            d = self.ts(self.dgt[:, t, :], self.ident, self.st[:, 2 + t:3 + t], ALU.mult, w=[r, self.dgtf[t]])
            dg.append(d)
        self.xnfree = sq
        tk = [None] * 4
        for kp in range(4):
            for t in range(2):
                for k in range(2):
                    kt = 2 * kp + k
                    o = self.ps[:, kp, k * 256 + t * 128:k * 256 + t * 128 + 128]
                    tk[kp] = self.mm(o, self.x[:, t, kt * 128:kt * 128 + 128], self.dgt[:, t, :], True, True,
                                     [dg[t], self.bfree[kp]])
        self.dgtf[0] = self.dgtf[1] = tk[3]
        hs = []
        for kp in range(4):
            es = []
            for k in range(2):
                kt = 2 * kp + k
                src = self.ps[:, kp, k * 256:k * 256 + 256]
                w = [tk[kp], gw, self.mixfree]
                if kp % 2:
                    bias = 0.0 if shift is None else shift[:, kt:kt + 1]
                    e = self.af(self.hT[:, kt, :], src, ACT.Identity, w, chain=False, scale=g[:, kt:kt + 1], bias=bias)
                elif shift is None:
                    e = self.ts(self.hT[:, kt, :], src, g[:, kt:kt + 1], ALU.mult, w=w, chain=False)
                else:
                    e = self.ts(self.hT[:, kt, :], src, g[:, kt:kt + 1], ALU.mult, shift[:, kt:kt + 1], ALU.add,
                                w=w, chain=False)
                es.append(e)
            self.bfree[kp] = es
            hs.append(self.halves(kp, self.hT, es))
        self.mixfree = hs
        self.silfree = [hs] * 4
        return hs

    def halves(self, kp, src, w):
        c = slice(2 * kp, 2 * kp + 2)
        h = self.acopy(self.hhi[:, c, :], src[:, c, :], [w, self.hfree], chain=False)
        l = self.tt(self.hlo[:, c, :], src[:, c, :], self.hhi[:, c, :].bitcast(F32), ALU.subtract, [h, w], chain=False)
        return [h, l]

    def T4(self, dst, srcs, w, free=None, b=7, scale=None, eng="dve"):
        for i, s in enumerate(srcs):
            tk = self.tr(self.ps[0:s.shape[-1], b, i * 128:i * 128 + 128], s, [w, self.bfree[b]])
        n = len(srcs)
        src = self.ps[0:srcs[0].shape[-1], b, 0:n * 128]
        if scale is not None:
            e = self.ts(dst, src, scale, ALU.mult, w=[tk, free], chain=False)
        elif eng == "act":
            e = self.acopy(dst, src, [tk, free], chain=False)
        else:
            e = self.cp(dst, src, [tk, free], chain=False)
        self.bfree[b] = e
        return e

    def attention(self, jobs, scale):
        n = len(jobs)
        exps, moved = {}, {}

        def scores(g):
            r, job = g % 2, jobs[g]
            toks = []
            for i, (qT, kT, _) in enumerate(job["heads"]):
                b = 2 * r + i
                for j, (qt, kt) in enumerate(((0, 0), (1, 0), (1, 1))):
                    o = self.ps[:, b, 128 * j:128 * j + 128]
                    ex = job["extra"]
                    self.mm(o, qT[:, 128 * qt:128 * qt + 128], kT[:, 128 * kt:128 * kt + 128], True,
                            ex is None and qt != kt, [job["w"], self.bfree[b]])
                    if ex is not None:
                        ex(i, o, qt, kt, qt != kt)
                    if qt == kt:
                        self.mm(o, self.identb, self.trib, False, True, [self.bw])
                toks.append(self.Q.last["pe"])
            ps2 = self.ps[:, 2 * r:2 * r + 2, :]
            mx = self.amx[:, r, :, :]
            t1 = self.dve(lambda e: e.tensor_reduce(mx[:, :, 0], ps2[:, :, 0:128], X, ALU.max), [toks], chain=False)
            t2 = self.dve(lambda e: e.tensor_reduce(mx[:, :, 1], ps2[:, :, 128:384], X, ALU.max), [toks], chain=False)
            t3 = self.ts(self.anm[:, r, :, :], mx, -scale, ALU.mult, w=[t1, t2, self.anfree[r]], chain=False)
            P = self.apb[:, r, :, :]
            te = []
            for i in range(2):
                for t in range(2):
                    a, z = (0, 128) if t == 0 else (128, 384)
                    te.append(self.af(P[:, i, a:z], ps2[:, i, a:z], ACT.Exp, [t3, self.apfree[r], self.arfree[r]], chain=False,
                                      scale=scale, bias=self.anm[:, r, i, t:t + 1],
                                      accum_out=self.ars[:, r, i, t:t + 1]))
                self.bfree[2 * r + i] = te[-2:]
            self.anfree[r] = te
            exps[g] = te

        def turn(g):
            r, te = g % 2, exps[g]
            tr = self.dve(lambda e: e.reciprocal(self.ari[:, r, :, :], self.ars[:, r, :, :]), [te, self.aifree[r]], chain=False)
            self.arfree[r] = tr
            pt = self.apt[:, r, :, :]
            ev = []
            for i in range(2):
                b = 4 + i
                for c in range(3):
                    tk = self.tr(self.ps[:, b, c * 128:c * 128 + 128], self.apb[:, r, i, c * 128:c * 128 + 128],
                                 [te[2 * i:2 * i + 2], self.bfree[b]])
                if i == 0:
                    e = self.acopy(pt[:, i, :], self.ps[:, b, 0:384], [tk, self.aptfree[r]], chain=False)
                else:
                    e = self.cp(pt[:, i, :], self.ps[:, b, 0:384], [tk, self.aptfree[r]], chain=False)
                self.bfree[b] = e
                ev.append(e)
            self.apfree[r] = tk
            moved[g] = (ev, tr)

        def values(g):
            r, job = g % 2, jobs[g]
            ev, tr = moved[g]
            pt, vd, b = self.apt[:, r, :, :], job["vd"], 6 + r
            for i, (_, _, V) in enumerate(job["heads"]):
                for t in range(2):
                    o = self.ps[:, b, (i * 2 + t) * 128:(i * 2 + t) * 128 + vd]
                    if t == 0:
                        tk = self.mm(o, pt[:, i, 0:128], V(0), True, True, [ev[i], job["w"], self.bfree[b]])
                    else:
                        self.mm(o, pt[:, i, 128:256], V(0), True, False)
                        tk = self.mm(o, pt[:, i, 256:384], V(1), False, True)
            self.aptfree[r] = tk
            o = self.ps[:, b, :].rearrange("p (i t d) -> p i t d", i=2, t=2)[:, :, :, 0:vd]
            first, last = job["emit"](o, self.ari[:, r, :, :].unsqueeze(3).to_broadcast([128, 2, 2, vd]),
                                      self.ari[:, r, :, :], [tk, tr])
            self.bfree[b] = first
            self.aifree[r] = first
            return last

        out = []
        for g in range(n + 2):
            if g < n:
                scores(g)
            if 0 <= g - 1 < n:
                turn(g - 1)
            if g >= 2:
                out.append(values(g - 2))
                if self.nada < self.adagoal:
                    self.fill(3)
                    self.flush(keep=1)
        return out

    def to_T(self, src, w):
        es, last = [], None
        for kp in range(4):
            b = kp
            for k in range(2):
                kt = 2 * kp + k
                for t in range(2):
                    o = self.ps[:, b, k * 256 + t * 128:k * 256 + t * 128 + 128]
                    last = self.tr(o, src[:, t, kt * 128:kt * 128 + 128], [w, self.bfree[b]])
            dst = self.xnT[:, 2 * kp:2 * kp + 2, :].rearrange("p a b -> p (a b)")
            e = self.cp(dst, self.ps[:, b, :], [last, self.hfree], chain=False)
            self.bfree[b] = e
            es.append(e)
        return [self.halves(kp, self.xnT, [es[kp]]) for kp in range(4)], last

    def proj_cb(self, name, ncols, hT, hw, evac):
        for c in range(0, ncols, 512):
            width = min(512, ncols - c)
            bt = [None, None]
            for half in range(2):
                n = self.take((name, c, half), 4 * width)
                for t in range(2):
                    b = (2 * (c // 512) + t) % 4
                    bt[t] = self.lin_rows(self.ps[:, b, 0:width], hT, hw, range(4 * half, 4 * half + 4), n, 0, width,
                                          width, t, half == 0, half == 1, self.bfree[b] if half == 0 else None)
                self.give(n, bt[1])
            for t in range(2):
                b = (2 * (c // 512) + t) % 4
                self.bfree[b] = evac(c, t, self.ps[:, b, 0:width], width, bt[t])
            if self.nada < self.adagoal:
                self.fill(2)
                self.flush(keep=1)
        return bt[1]

    def group_norm(self, y, ng, gs, sq, st, w):
        self.tt(sq, y, y, ALU.mult, w)
        t = self.dve(lambda e: e.tensor_reduce(st, sq, X, ALU.add), chain=True)
        r = self.rstd(st, st, gs, [t])
        return self.tt(y, y, st.unsqueeze(2).to_broadcast([128, ng, gs]), ALU.mult, [r])

    def negabs(self, out, a, w):
        return self.dve(lambda e: e.scalar_tensor_tensor(out, a, -1.0, a, ALU.mult, ALU.min), w, True)

    def log_sigmoid(self, z, a, w):
        self.negabs(a, z, w)
        t = self.Q.last["dve"]
        self.af(a, a, ACT.Exp, [t])
        t = self.af(a, a, ACT.Ln, bias=1.0)
        self.ts(z, z, 0.0, ALU.min)
        return self.tt(z, z, a, ALU.subtract, [t])

    def first_mixer(self):
        pj = self.pj1
        cw = self.cw
        hs = self.norm_T(self.col("mixg"), None, cw)
        self.gmw = self.Q.dma("act", lambda e: e.dma_start(self.gf, self.io["cst2"]), self.s_c[4], hs)
        pw = []

        def evac(c, t, bank, width, tk):
            if t == 0:
                e = self.acopy(pj[:, t, c:c + width], bank, [tk], chain=False)
            else:
                e = self.cp(pj[:, t, c:c + width], bank, [tk], chain=False)
            pw.append(e)
            return e

        last = self.proj_cb(("w_in", 0), 2832, (self.hhi, self.hlo), hs, evac)
        self.hfree = last
        self.debug("pj1", pj[:, :, :], pw)
        sc = self.scr
        qk = sc(0, [128, 2, 256])
        bb = sc(2, [128, 256])
        aa = sc(3, [128, 256])
        qe = sc(4, [128, 8, 256])
        ke = sc(12, [128, 8, 256])
        o = sc(20, [128, 8, 64])
        osq = sc(22, [128, 8, 64])
        mk = self.att(0, [128, 8, 128])
        st = self.att(4, [128, 2, 3, 128])
        glr = self.att(8, [16, 256])
        tq = self.T4(qk[:, 0, :], [pj[:, 0, 0:128], pj[:, 1, 0:128]], [pw, last], scale=float(32 ** -0.5), b=4)
        tk_ = self.T4(qk[:, 1, :], [pj[:, 0, 128:256], pj[:, 1, 128:256]], [pw, last], b=5)
        tg = self.T4(glr, [pj[:, 0, 512:528], pj[:, 1, 512:528]], [pw, last], b=6)
        z = self.ps[:, 7, 0:256]
        t = self.mm(z, self.col("glaw")[0:16, :], glr, True, True, [tg, cw, self.bfree[7]])
        t = self.ts(aa, z, self.col("glab"), ALU.add, w=[t, cw])
        self.bfree[7] = t
        t = self.log_sigmoid(aa, bb, [t])
        t = self.ts(aa, aa, 1.0 / 16.0, ALU.mult)
        t = self.dve(lambda e: e.tensor_tensor_scan(bb, self.ones[:, 0:256], aa, 0.0, ALU.mult, ALU.add), [t], True)
        lv = []
        for li, s in enumerate([128, 64, 32, 16, 8, 4, 2, 1]):
            nb = 128 // s
            bv = bb.rearrange("p (n s) -> p n s", s=2 * s)
            dv = ke[:, li, :].rearrange("p (n s) -> p n s", s=2 * s)
            lv.append(self.tt(dv, bv, bv[:, :, s - 1:s].to_broadcast([128, nb, 2 * s]), ALU.subtract, [t], chain=False))
        t = self.negabs(ke[:, :, :], ke[:, :, :], lv)
        t = self.af(ke[:, :, :], ke[:, :, :], ACT.Exp, [t])
        t1 = self.tt(qe, ke, qk[:, 0, :].unsqueeze(1).to_broadcast([128, 8, 256]), ALU.mult, [t, tq])
        t2 = self.tt(ke, ke, qk[:, 1, :].unsqueeze(1).to_broadcast([128, 8, 256]), ALU.mult, [t, t1, tk_])
        ob = self.ps[:, 6, :].rearrange("p (a b) -> p a b", b=64)
        stf = [None, None]
        mkf = None
        for h in range(4):
            P = slice(32 * h, 32 * h + 32)
            r = h % 2
            b01 = self.ps[:, 4 + r, 0:128]
            t = self.mm(b01, ke[P, 0, 0:128], qe[P, 0, 128:256], True, True, [t1, t2, self.bfree[4 + r]])
            e1 = self.acopy(st[:, r, 1, :], b01, [t, stf[r]], chain=False)
            self.bfree[4 + r] = e1
            ev = [e1]
            for blk in range(2):
                B = slice(128 * blk, 128 * blk + 128)
                for l in range(8):
                    bank = 2 * blk + l // 4
                    oo = self.ps[:, bank, (l % 4) * 128:(l % 4) * 128 + 128]
                    if l < 7:
                        a_, b_ = ke[P, l + 1, B], qe[P, l + 1, B]
                    else:
                        a_, b_ = qk[P, 1, B], qk[P, 0, B]
                    t = self.mm(oo, a_, b_, True, True, [self.bfree[bank], t1, t2])
                e2 = self.tt(mk, self.ps[:, 2 * blk:2 * blk + 2, :].rearrange("p a (b c) -> p (a b) c", c=128),
                             self.gmask, ALU.mult, [t, self.gmw])
                self.bfree[2 * blk] = self.bfree[2 * blk + 1] = e2
                ms = mk.rearrange("p l i -> p i l")
                dst = st[:, r, 2 * blk, :]
                ev.append(self.dve(lambda e, dst=dst, ms=ms: e.tensor_reduce(dst, ms, X, ALU.add), [stf[r]], True))
            v = [pj[:, t_, 256 + 64 * h:320 + 64 * h] for t_ in range(2)]
            self.mm(ob[:, h, :], st[:, r, 0, :], v[0], True, True, [ev, self.bfree[6]])
            self.mm(ob[:, 4 + h, :], st[:, r, 1, :], v[0], True, False)
            stf[r] = t = self.mm(ob[:, 4 + h, :], st[:, r, 2, :], v[1], False, True)
            self.fill(4)
            self.flush(keep=1)
        t = self.cp(o, ob, [t])
        self.bfree[6] = t
        self.group_norm(o, 8, 64, osq, self.st[:, 16:24], [t])
        t = self.tt(o, o, self.row("glang").unsqueeze(1).to_broadcast([128, 8, 64]), ALU.mult, [cw])
        tz = self.af(osq, pj[:, :, 528:784], ACT.Silu, [t])
        for t_ in range(2):
            mg = self.tt(self.mix[:, t_, 0:256], o[:, 4 * t_:4 * t_ + 4, :].rearrange("p a b -> p (a b)"),
                        osq[:, 4 * t_:4 * t_ + 4, :].rearrange("p a b -> p (a b)"), ALU.mult, [tz])
        z = sc(4, [128, 2, 256])
        zT = sc(6, [128, 2, 288])
        dg = sc(9, [128, 4, 128])
        yf = sc(11, [128, 2, 256])
        y = sc(13, [128, 8, 64])
        ysq = sc(15, [128, 8, 64])
        t = self.af(z, pj[:, :, 1040:1296], ACT.Sigmoid, [t, mg])
        t = self.tt(z, z, pj[:, :, 784:1040], ALU.mult, [t])
        t0 = self.dve(lambda e: e.memset(zT[:, :, 0:32], 0.0), [t1], True)
        tz = []
        for ct in range(2):
            tz.append(self.T4(zT[:, ct, 30:286], [z[:, 0, 128 * ct:128 * ct + 128], z[:, 1, 128 * ct:128 * ct + 128]],
                              [t], free=t0, b=4 + ct))
        dgf = [None] * 4
        n = 0
        for ct in range(2):
            for k in range(31):
                r = n % 4
                c = self.col("convw")[:, 31 * ct + k:31 * ct + k + 1]
                d = self.ts(dg[:, r, :], self.ident, c, ALU.mult, w=[cw, dgf[r], t2 if n < 4 else None, stf], chain=False)
                dgf[r] = tt_ = self.mm(self.ps[:, ct, 0:256], dg[:, r, :], zT[:, ct, k:k + 256], k == 0, k == 30,
                                       [d, tz, self.bfree[ct]])
                n += 1
                if k % 8 == 7:
                    self.fill(2)
                    self.flush(keep=1)
            e = self.ts(yf[:, ct, :], self.ps[:, ct, 0:256], self.col("convb")[:, ct:ct + 1], ALU.add, w=[tt_])
            self.bfree[ct] = e
        for t_ in range(2):
            for ct in range(2):
                t = self.tr(self.ps[:, 2, (2 * t_ + ct) * 128:(2 * t_ + ct) * 128 + 128],
                            yf[:, ct, 128 * t_:128 * t_ + 128], [e, self.bfree[2]])
        bk = self.ps[:, 2, :].rearrange("p (a b) -> p a b", b=64)
        mu = self.st[:, 24:32]
        t = self.cp(y, bk, [t])
        self.bfree[2] = t
        self.dve(lambda e: e.tensor_reduce(mu, y, X, ALU.add), [], True)
        self.ts(mu, mu, 1.0 / 64, ALU.mult)
        self.tt(y, y, mu.unsqueeze(2).to_broadcast([128, 8, 64]), ALU.subtract)
        self.group_norm(y, 8, 64, ysq, self.st[:, 16:24], [])
        y2 = y.rearrange("p (t c) d -> p t (c d)", t=2)
        self.tt(y2, y2, self.row("cng").unsqueeze(1).to_broadcast([128, 2, 256]), ALU.mult)
        t = self.tt(y2, y2, self.row("cnb").unsqueeze(1).to_broadcast([128, 2, 256]), ALU.add)
        m2 = self.af(self.mix[:, :, 256:512], y2, ACT.Silu, [t])
        lam = self.st[:, 32:36]
        l4 = self.row("lq1")[:, 0:64]
        lw = sc(15, [128, 2, 64])
        self.tt(lw[:, 0, :], self.row("lq1"), self.row("lk1"), ALU.mult, [cw])
        self.tt(lw[:, 1, :], self.row("lq2"), self.row("lk2"), ALU.mult)
        t = self.dve(lambda e: e.tensor_reduce(lam[:, 0:2], lw, X, ALU.add), [], True)
        t = self.af(lam[:, 0:2], lam[:, 0:2], ACT.Exp, [t])
        t = self.tt(lam[:, 2:3], lam[:, 1:2], lam[:, 0:1], ALU.subtract, [t])
        lamt = self.ts(lam[:, 3:4], lam[:, 2:3], -0.2, ALU.add)
        q = pj[:, :, 1296:2320]
        q4 = pj[:, :, 1296:2320].rearrange("p t (g d) -> p t g d", d=64)
        dsq = sc(16, [128, 2, 16, 64])
        ss = self.st2[:, 0:32].rearrange("p (t g) -> p t g", t=2)
        t = self.tt(dsq, q4, q4, ALU.mult, [m2, dgf])
        t = self.dve(lambda e: e.tensor_reduce(ss, dsq, X, ALU.add), [], True)
        r = self.rstd(self.st2[:, 0:32], self.st2[:, 0:32], 64, [t])
        for t_ in range(2):
            self.tt(q4[:, t_], q4[:, t_], ss[:, t_].unsqueeze(2).to_broadcast([128, 16, 64]), ALU.mult, [r])
            self.tt(q4[:, t_, 0:8], q4[:, t_, 0:8], self.row("qn").unsqueeze(1).to_broadcast([128, 8, 64]), ALU.mult)
            t = self.tt(q4[:, t_, 8:16], q4[:, t_, 8:16], self.row("kn").unsqueeze(1).to_broadcast([128, 8, 64]), ALU.mult)
        QK = sc(0, [128, 4, 2, 256])
        qw = []
        for h in range(4):
            c = 128 * h
            qw.append(self.T4(QK[:, h].rearrange("p a b -> p (a b)"), [q[:, 0, c:c + 128], q[:, 1, c:c + 128],
                      q[:, 0, 512 + c:640 + c], q[:, 1, 512 + c:640 + c]], [t], b=4 + h, eng="act" if h % 2 else "dve"))
        DO = sc(8, [128, 2, 8, 128])
        jobs = []
        for h in range(4):
            dst = DO[:, :, 2 * h:2 * h + 2, :].rearrange("p t i d -> p i t d")

            def emit(o_, rib, ri, w_, dst=dst):
                e = self.tt(dst, o_, rib, ALU.mult, w_, chain=False)
                return e, e

            jobs.append({"heads": [(QK[64 * m:64 * m + 64, h, 0, :], QK[64 * m:64 * m + 64, h, 1, :],
                                    lambda t_, h=h: pj[:, t_, 2320 + 128 * h:2448 + 128 * h]) for m in range(2)],
                         "vd": 128, "w": [qw, t], "extra": None, "emit": emit})
        self.apfree = [[t], [t]]
        ow = self.attention(jobs, 0.125)
        D5 = DO.rearrange("p t (h m) d -> p t h m d", m=2)
        od = sc(0, [128, 8, 128])
        odq = sc(16, [128, 8, 128])
        for t_ in range(2):
            t = self.dve(lambda e, t_=t_: e.scalar_tensor_tensor(od[:, 4 * t_:4 * t_ + 4, :], D5[:, t_, :, 1, :],
                         lam[:, 3:4], D5[:, t_, :, 0, :], ALU.mult, ALU.add), [ow, lamt], True)
        self.group_norm(od, 8, 128, odq, self.st[:, 16:24], [t])
        self.ts(od, od, 0.8, ALU.mult)
        for t_ in range(2):
            m3 = self.tt(self.mix[:, t_, 512:1024].rearrange("p (h d) -> p h d", d=128), od[:, 4 * t_:4 * t_ + 4, :],
                         self.row("subg").unsqueeze(1).to_broadcast([128, 4, 128]), ALU.mult)
        self.debug("mix1", self.mix[:, :, :], [m3, m2, mg])
        self.pjfree = [ow, m3]
        self.hfree = [m3, ow]
        hs, tl = self.to_T(self.mix, [m3, m2, mg])

        def evac2(c, t, bank, width, tk):
            e = self.tt(self.x[:, t, c:c + width], bank, self.x[:, t, c:c + width], ALU.add, [tk])
            self.xw[t].append(e)
            return e

        self.xw = [[], []]
        self.hfree = self.proj_cb(("w_out", 0), 1024, (self.hhi, self.hlo), hs, evac2)
        self.debug("x1", self.x[:, :, :], self.xw)

    def first_max(self, oh, v, big, n, w):
        mx, eq, idx = big
        self.dve(lambda e: e.tensor_reduce(mx, v, X, ALU.max), w, True)
        self.tt(eq, v, mx.unsqueeze(2).to_broadcast([128, 2, 4]), ALU.is_equal)
        self.tt(eq, eq, self.iom4[:, 0:8].rearrange("p (a b) -> p a b", a=2), ALU.mult)
        self.dve(lambda e: e.tensor_reduce(idx, eq, X, ALU.min), [], True)
        self.tt(oh, self.iom4[:, 0:8].rearrange("p (a b) -> p a b", a=2), idx.unsqueeze(2).to_broadcast([128, 2, 4]),
                ALU.is_equal)
        return mx

    def moe(self):
        cw = self.cw
        hs = self.norm_T(self.col("ffng"), None, cw)
        for t in range(2):
            for kt in range(8):
                tk = self.mm(self.ps[:, 7, t * 32:t * 32 + 20], self.hT[:, kt, t * 128:t * 128 + 128],
                             self.rw[:, kt, :], kt == 0, kt == 7, [hs, cw, self.bfree[7]])
        f = self.frt
        lg = f(0, [128, 2, 20])
        t = self.tt(lg, self.ps[:, 7, 0:64].rearrange("p (t c) -> p t c", t=2)[:, :, 0:20],
                    self.row("rb").unsqueeze(1).to_broadcast([128, 2, 20]), ALU.add, [tk, cw, self.pjfree])
        self.bfree[7] = t
        self.debug("lg", lg, [t])
        mx, eq, idx = f(40, [128, 2]), f(42, [128, 2, 4]), f(50, [128, 2])
        goh, e8, pg = f(52, [128, 2, 4]), f(60, [128, 2, 4]), f(68, [128, 2])
        g = lg[:, :, 0:4]
        self.first_max(goh, g, (mx, eq, idx), 4, [])
        t = self.tt(e8, g, mx.unsqueeze(2).to_broadcast([128, 2, 4]), ALU.subtract)
        t = self.af(e8, e8, ACT.Exp, [t])
        self.dve(lambda e: e.tensor_reduce(pg, e8, X, ALU.add), [t], True)
        self.dve(lambda e: e.reciprocal(pg, pg), [], True)
        es, tmp = f(70, [128, 2, 4, 4]), f(102, [128, 2, 4])
        el = lg[:, :, 4:20].rearrange("p t (g e) -> p t g e", g=4)
        for t_ in range(2):
            self.tt(es[:, t_], el[:, t_], goh[:, t_].unsqueeze(2).to_broadcast([128, 4, 4]), ALU.mult)
        for t_ in range(2):
            t = self.dve(lambda e, t_=t_: e.tensor_reduce(tmp[:, t_, :], es[:, t_].rearrange("p g e -> p e g"), X, ALU.add), [], True)
        m1, oh1, oh2, m2 = f(110, [128, 2]), f(112, [128, 2, 4]), f(120, [128, 2, 4]), f(128, [128, 2])
        self.dve(lambda e: e.tensor_reduce(m1, tmp, X, ALU.max), [], True)
        t = self.tt(tmp, tmp, m1.unsqueeze(2).to_broadcast([128, 2, 4]), ALU.subtract)
        t = self.af(tmp, tmp, ACT.Exp, [t])
        self.first_max(oh1, tmp, (mx, eq, idx), 4, [t])
        self.ts(e8, oh1, -2.0, ALU.mult)
        self.tt(e8, e8, tmp, ALU.add)
        self.first_max(oh2, e8, (mx, eq, idx), 4, [])
        self.cp(m2, mx)
        den = f(130, [128, 2])
        self.ts(den, m2, 1.0, ALU.add)
        self.dve(lambda e: e.reciprocal(den, den), [], True)
        self.tt(den, den, pg, ALU.mult)
        self.tt(oh2, oh2, m2.unsqueeze(2).to_broadcast([128, 2, 4]), ALU.mult)
        self.tt(oh1, oh1, oh2, ALU.add)
        self.tt(oh1, oh1, den.unsqueeze(2).to_broadcast([128, 2, 4]), ALU.mult)
        for t_ in range(2):
            t = self.tt(es[:, t_], goh[:, t_].unsqueeze(2).to_broadcast([128, 4, 4]),
                        oh1[:, t_].unsqueeze(1).to_broadcast([128, 4, 4]), ALU.mult)
        self.debug("gates", es, [t])
        gT = f(160, [16, 256])
        t = self.T4(gT, [es[:, 0].rearrange("p a b -> p (a b)"), es[:, 1].rearrange("p a b -> p (a b)")], [t], b=7)
        gb = self.gateb
        gw = []
        for p in range(8):
            b = 4 + p % 4
            for k in range(2):
                tk = self.mm(self.ps[:, b, 256 * k:256 * k + 256], self.sel16[:, 2 * p + k, :], gT, True, True,
                             [t, self.gmw, self.bfree[b]])
            dst = gb[:, 2 * p:2 * p + 2, :].rearrange("p a b -> p (a b)")
            if p % 2:
                e = self.acopy(dst, self.ps[:, b, :], [tk, self.pjfree], chain=False)
            else:
                e = self.cp(dst, self.ps[:, b, :], [tk, self.pjfree], chain=False)
            self.bfree[b] = e
            gw.append(e)
        self.cw2 = self.Q.dma("act", lambda e: e.dma_start(self.w2, self.io["cw2"]), self.s_c[6], [tk])
        hf = [None, None]
        tks = [None] * 4

        def down(e_, hid):
            n = self.take(("down", e_))
            m, th, tl = self.ready[n]
            for t_ in range(2):
                for c in range(2):
                    b = 2 * t_ + c
                    for k in range(2):
                        hi = self.mhid[:, e_ % 2, 0, k, t_ * 128:t_ * 128 + 128]
                        lo = self.mhid[:, e_ % 2, 1, k, t_ * 128:t_ * 128 + 128]
                        wh = self.whi[:, m, k * 1024 + c * 512:k * 1024 + c * 512 + 512]
                        wl = self.wlo[:, m, k * 1024 + c * 512:k * 1024 + c * 512 + 512]
                        s = e_ == 0 and k == 0
                        w = [hid, th, tl, self.bfree[b] if s else None]
                        self.mm(self.ps[:, b, :], hi, wh, s, False, w)
                        self.mm(self.ps[:, b, :], lo, wh, False, False)
                        tk = self.mm(self.ps[:, b, :], hi, wl, False, e_ == 15 and k == 1)
                    tks[b] = tk
            self.give(n, tk)
            hf[e_ % 2] = tk
            return tk

        prev = None
        for e_ in range(16):
            ta, tb = self.up(("moe", e_), 0, (self.hhi, self.hlo), hs, False)
            hid = []
            for f_ in range(2):
                hid += self.hidden(f_, ta[f_], tb[f_], self.mhid[:, e_ % 2, 0, f_, :], self.mhid[:, e_ % 2, 1, f_, :],
                                   [hf[e_ % 2], self.pjfree], gate=gb[:, e_, :], gw=gw)
            self.fill()
            if prev is not None:
                down(e_ - 1, prev)
                self.fill()
            prev = hid
        self.hfree = tb[1]
        tk = down(15, prev)
        self.flush()
        self.xw = [[], []]
        for t_ in range(2):
            for c in range(2):
                b = 2 * t_ + c
                e = self.tt(self.x[:, t_, c * 512:c * 512 + 512], self.ps[:, b, :], self.x[:, t_, c * 512:c * 512 + 512],
                            ALU.add, [tks[b]])
                self.bfree[b] = e
                self.xw[t_].append(e)
        self.hidfree = [tk, self.xw]
        self.debug("x2", self.x[:, :, :], self.xw)

    def fill(self, k=1):
        for _ in range(k):
            if self.nada >= self.adagoal:
                return
            n = self.nada
            self.nada += 1
            l, j, half = n // 72, n // 2 % 36, n % 2
            slot, r = n % NADA, (n // 2) % NACC
            dst, src = self.adaw[:, slot, :], self.io["wada"][n]
            ld = self.Q.dma("sp", lambda e, dst=dst, src=src: e.dma_start(dst, src), self.s_ada[slot], self.adafree[slot])
            w = self.adaw[:, slot, :].rearrange("p (k c) -> p k c", k=4)
            acc = self.acc[:, r, :]
            c = self.ca[:, 4 * half:4 * half + 4].unsqueeze(2).to_broadcast([128, 4, 256])
            first = [ld, self.cact]
            t = self.ptt(w, w, c, ALU.mult, first)
            t = self.ptt(w[:, 0:2, :], w[:, 0:2, :], w[:, 2:4, :], ALU.add, [t])
            if half:
                t = self.ptt(w[:, 0, :], w[:, 0, :], w[:, 1, :], ALU.add, [t])
                t = self.ptt(acc, w[:, 0, :], acc, ALU.add, [t, self.adalast])
            else:
                t = self.ptt(acc, w[:, 0, :], w[:, 1, :], ALU.add, [t, self.accfree[r]])
            self.adafree[slot] = self.adalast = t
            if half:
                self.accs.append((l, j, r, t))

    def sum_acc(self, bank, keep):
        tk = None
        out = self.accs[:max(0, len(self.accs) - keep)]
        self.accs = self.accs[len(out):]
        for i, (l, j, r, t) in enumerate(out):
            for k in range(2):
                c = 256 + 2 * i + k
                tk = self.mm(self.ps[:, bank, c:c + 1], self.acc[:, r, 128 * k:128 * k + 128], self.ones[:, 0:1],
                             True, True, [t, self.bfree[bank]])
            self.accfree[r] = tk
        return out, tk

    def put_mod(self, bank, done, w):
        if not done:
            return None
        l, j, n = done[0][0], done[0][1], 2 * len(done)
        t = self.tt(self.mod2[:, 72 * l + 2 * j:72 * l + 2 * j + n], self.ps[:, bank, 256:256 + n],
                    self.col("bada")[:, 72 * l + 2 * j:72 * l + 2 * j + n], ALU.add, [w, self.cw], chain=False)
        for l, _, _, _ in done:
            self.modt[l] = t
        return t

    def flush(self, bank=7, keep=0):
        if len(self.accs) > keep:
            done, tk = self.sum_acc(bank, keep)
            self.bfree[bank] = self.put_mod(bank, done, tk)

    def ada(self, l):
        while self.nada < 72 * (l + 1):
            self.fill()
            if len(self.accs) >= 3:
                self.flush(keep=1)
        self.flush()
        self.adagoal = 144
        self.mod = self.mod2[:, 72 * l:72 * l + 72]
        self.debug("mod%d" % l, self.mod, [self.modt[l]])
        m4 = self.mod.rearrange("p (i s k) -> p i s k", i=3, s=3)
        ng = self.col("ng2")[:, 24 * l:24 * l + 24].rearrange("p (i k) -> p i k", i=3)
        self.modw = self.dve(lambda e: e.scalar_tensor_tensor(m4[:, :, 1, :], m4[:, :, 1, :], 1.0, ng, ALU.add, ALU.mult),
                             [self.modt[l], self.cw], True)

    def gate_rows(self, i):
        m4 = self.mod.rearrange("p (i s k) -> p i s k", i=3, s=3)
        f = 0.5 if i != 1 else 1.0
        gw = []
        for c in range(2):
            for k in range(4):
                dgt = self.dgt[:, k, :]
                col = m4[:, i, 2, 4 * c + k:4 * c + k + 1]
                d = self.ts(dgt, self.ident, col, ALU.mult, f, ALU.mult, w=[self.modw, self.dgtf[k]], chain=False)
                self.dgtf[k] = tk = self.mm(self.ps[:, 4 + c, 128 * k:128 * k + 128], self.ones[:, 0:128], dgt, True, True,
                                            [d, self.bfree[4 + c]])
            e = self.acopy(self.gbc[:, 512 * c:512 * c + 512], self.ps[:, 4 + c, :], [tk, self.gbcfree], chain=False)
            self.bfree[4 + c] = e
            gw.append(e)
        self.gw = gw

    def gated_add(self, i, t_, c, bank, tk):
        tmp = self.xn[:, t_, c:c + 512]
        a = self.tt(tmp, bank, self.gbc[:, c:c + 512], ALU.mult, [tk, self.gw, self.xnfree], chain=False)
        self.gbcfree = a
        xs = self.x[:, t_, c:c + 512]
        b = self.tt(xs, xs, tmp, ALU.add, [a], chain=False)
        self.xw[t_].append(b)
        return a

    def ffn(self, l, i):
        mod = self.mod.rearrange("p (i s k) -> p i s k", i=3, s=3)
        hs = self.norm_T(mod[:, 2 * i, 1, :], mod[:, 2 * i, 0, :], self.modw)
        hid = []
        for j in range(11):
            ta, tb = self.up(("ffn", l, i), j, (self.hhi, self.hlo), hs, False)
            for f_ in range(2):
                ft = 2 * j + f_
                hid.append(self.hidden(f_, ta[f_], tb[f_], self.hidhi[:, ft, :], self.hidlo[:, ft, :], self.hidfree))
            self.fill()
        self.hfree = tb[1]
        self.flush()
        self.gate_rows(2 * i)
        tks = [None] * 4
        for j in range(11):
            n = self.take(("w2", l, i, j))
            m, th, tl = self.ready[n]
            for t_ in range(2):
                for c in range(2):
                    b = 2 * t_ + c
                    for k in range(2):
                        ft = 2 * j + k
                        hi = self.hidhi[:, ft, t_ * 128:t_ * 128 + 128]
                        lo = self.hidlo[:, ft, t_ * 128:t_ * 128 + 128]
                        wh = self.whi[:, m, k * 1024 + c * 512:k * 1024 + c * 512 + 512]
                        wl = self.wlo[:, m, k * 1024 + c * 512:k * 1024 + c * 512 + 512]
                        s = j == 0 and k == 0
                        self.mm(self.ps[:, b, :], hi, wh, s, False, [hid[ft], th, tl, self.bfree[b] if s else None])
                        self.mm(self.ps[:, b, :], lo, wh, False, False)
                        tk = self.mm(self.ps[:, b, :], hi, wl, False, j == 10 and k == 1)
                    tks[b] = tk
            self.give(n, tk)
            if j < 10:
                self.fill(1)
                self.flush(keep=1)
        self.hidfree = [tk]
        self.xw = [[], []]
        for t_ in range(2):
            for c in range(2):
                self.bfree[2 * t_ + c] = self.gated_add(2 * i, t_, 512 * c, self.ps[:, 2 * t_ + c, :], tks[2 * t_ + c])
        self.xnfree = None
        self.debug("xf%d%d" % (l, i), self.x[:, :, :], self.xw)

    def rope_tables(self):
        f = self.rsc
        pos, ang, k, r = f(0, [128, 2]), f(2, [128, 2, 8]), f(18, [128, 2, 8]), f(34, [128, 2, 8])
        self.cp(pos, self.posi, [self.cw])
        for t_ in range(2):
            self.ts(ang[:, t_, :], self.row("inv"), pos[:, t_:t_ + 1], ALU.mult)
        two_pi = 2 * np.pi
        c1 = 6.28125
        c2 = float(np.float32(int((two_pi - c1) * 2 ** 20) / 2 ** 20))
        c3 = float(np.float32(two_pi - c1 - c2))
        magic = 12582912.0
        for out, quarter, add in ((self.sinT, 0.0, 0.0), (self.cosT, 0.25, float(np.pi / 2))):
            self.ts(k, ang, float(1 / two_pi), ALU.mult, quarter, ALU.add)
            self.ts(k, k, magic, ALU.add)
            self.ts(k, k, magic, ALU.subtract)
            self.dve(lambda e: e.scalar_tensor_tensor(r, k, -c1, ang, ALU.mult, ALU.add), [], True)
            self.dve(lambda e: e.scalar_tensor_tensor(r, k, -c2, r, ALU.mult, ALU.add), [], True)
            self.dve(lambda e: e.scalar_tensor_tensor(r, k, -c3, r, ALU.mult, ALU.add), [], True)
            self.ts(r, r, add, ALU.add)
            t = self.ts(r, r, 3.1415925, ALU.min, -3.1415925, ALU.max)
            t = self.af(out, r, ACT.Sin, [t])
            self.cp(pos, pos, [t])
        self.ropew = t
        self.debug("cos", self.cosT, [t])

    def rope(self, lo, nh, w):
        pj = self.pj2
        v = pj[:, :, lo:lo + 64 * nh].rearrange("p t (h d) -> p t h d", d=64)
        r1, r2 = v[:, :, :, 0:8], v[:, :, :, 8:16]
        sh = [128, 2, nh, 8]
        c = self.cosT.unsqueeze(2).to_broadcast(sh)
        s = self.sinT.unsqueeze(2).to_broadcast(sh)
        a, b, d, e = [self.rsc(64 + 160 * i, [128, 2, nh, 8]) for i in range(4)]
        self.tt(a, r1, c, ALU.mult, [w, self.ropew])
        self.tt(b, r2, s, ALU.mult, chain=False)
        self.tt(d, r1, s, ALU.mult, chain=False)
        self.tt(e, r2, c, ALU.mult, chain=False)
        t = self.tt(r1, a, b, ALU.subtract)
        return self.tt(r2, e, d, ALU.add)

    def mixer(self, l):
        pj = self.pj2
        cw = self.cw
        mod = self.mod.rearrange("p (i s k) -> p i s k", i=3, s=3)
        hs = self.norm_T(mod[:, 1, 1, :], mod[:, 1, 0, :], self.modw)
        pw = []

        def evac(c, t, bank, width, tk):
            if t == 0:
                e = self.acopy(pj[:, t, c:c + width], bank, [tk, self.hidfree], chain=False)
            else:
                e = self.cp(pj[:, t, c:c + width], bank, [tk, self.hidfree], chain=False)
            pw.append(e)
            return e

        last = self.proj_cb(("w_in2", l), 2844, (self.hhi, self.hlo), hs, evac)
        self.hfree = last
        for lo, nh in ((0, 10), (768, 2), (1024, 2), (2076, 8)):
            rw = self.rope(lo, nh, pw)
        self.debug("pj2", pj[:, :, :], [rw])
        sc = self.scr
        QN = sc(0, [128, 4, 256])
        KS = sc(4, [128, 2, 256])
        ZZ = sc(6, [128, 4, 256])
        A = sc(10, [128, 2, 16, 30])
        Ah = self.ahi
        Al = self.alo
        w0 = [rw, pw, last]
        mixf = self.mix.rearrange("p a b -> p (a b)")
        QR = mixf[:, 0:1024].rearrange("p (t h g d) -> p t h g d", t=2, h=4, g=2)
        DU = mixf[:, 1024:2048].rearrange("p (t j r d) -> p t j r d", t=2, j=4, r=2)
        wq, wd = [], []
        for t_ in range(2):
            src = pj[:, t_, 0:512].rearrange("p (g h d) -> p h g d", g=2, d=64)
            wq.append(self.cp(QR[:, t_], src, [w0, self.mixfree], chain=False))
            src = pj[:, t_, 512:768].rearrange("p (j d) -> p j d", d=64).unsqueeze(2).to_broadcast([128, 4, 2, 64])
            wd.append(self.acopy(DU[:, t_], src, [w0, self.mixfree], chain=False))
        tq = []
        for hp in range(2):
            for j in range(2):
                h = 2 * hp + j
                for t_ in range(2):
                    tk = self.tr(self.ps[:, hp, (2 * j + t_) * 128:(2 * j + t_) * 128 + 128], QR[:, t_, h].rearrange("p g d -> p (g d)"), [wq, self.bfree[hp]])
            e = self.cp(QN[:, 2 * hp:2 * hp + 2, :].rearrange("p a b -> p (a b)"), self.ps[:, hp, :], [tk, last], chain=False)
            self.bfree[hp] = e
            tq.append(e)
        tks = self.T4(KS[:, 0:2, :].rearrange("p a b -> p (a b)"),
                      [pj[:, 0, 768:896], pj[:, 1, 768:896], pj[:, 0, 1024:1152], pj[:, 1, 1024:1152]], w0, b=2, eng="act")
        tz = []
        for kv in range(2):
            for g in range(2):
                j = 2 * kv + g
                for t_ in range(2):
                    dup = DU[:, t_, j].rearrange("p r d -> p (r d)")
                    tk = self.tr(self.ps[:, 4 + kv, (2 * g + t_) * 128:(2 * g + t_) * 128 + 128], dup, [wd, self.bfree[4 + kv]])
            src = self.ps[:, 4 + kv, :].rearrange("p (g t) -> p g t", g=2)
            e1 = self.cp(ZZ[0:64, 2 * kv:2 * kv + 2, :], src[0:64], [tk, last], chain=False)
            e2 = self.cp(ZZ[64:128, 2 * kv:2 * kv + 2, 0:255], src[64:128, :, 1:256], [tk, last], chain=False)
            self.bfree[4 + kv] = [e1, e2]
            tz += [e1, e2]
        ta = []
        for kv in range(2):
            for g in range(2):
                for m in range(2):
                    v = ZZ[:, 2 * kv + g, :].rearrange("p (c k two) -> p k c two", k=8, two=2)[:, :, m:m + 15, 0]
                    p = self.col("pos")[:, 32 * l + 16 * kv + 8 * m:32 * l + 16 * kv + 8 * m + 8]
                    ta.append(self.tt(A[:, kv, 8 * m:8 * m + 8, 15 * g:15 * g + 15], v,
                                      p.unsqueeze(2).to_broadcast([128, 8, 15]), ALU.add, [tz, cw, self.afree], chain=False))
        th = self.acopy(Ah, A, [ta, self.afree])
        tl = self.tt(Al, A, Ah.bitcast(F32), ALU.subtract, [th])
        hg = sc(14, [30, 2, 256])
        HT = sc(16, [128, 2, 2, 30])
        KC = sc(17, [128, 30])
        VC = self.rsc(64, [15, 2, 64])
        th2 = []
        for kv in range(2):
            b = 4 + kv
            for half in range(2):
                n = self.take(("cw1", l, kv, half))
                m, wh_, wl_ = self.ready[n]
                for k in range(8):
                    kt = 8 * half + k
                    wh, wl = self.whi[:, m, 256 * k:256 * k + 256], self.wlo[:, m, 256 * k:256 * k + 256]
                    o_ = self.ps[0:30, b, 0:256]
                    self.mm(o_, Ah[:, kv, kt, :], wh, kt == 0, False, [tl, th, wh_, wl_, self.bfree[b]])
                    self.mm(o_, Al[:, kv, kt, :], wh, False, False)
                    tk = self.mm(o_, Ah[:, kv, kt, :], wl, False, kt == 15)
                self.give(n, tk)
            e = self.af(hg[:, kv, :], self.ps[0:30, b, 0:256], ACT.Gelu_apprx_tanh, [tk])
            self.bfree[b] = e
            for k in range(2):
                tk2 = self.tr(self.ps[:, 6 + kv, 128 * k:128 * k + 30], hg[:, kv, 128 * k:128 * k + 128], [e, self.bfree[6 + kv]])
            e = self.cp(HT[:, kv], self.ps[:, 6 + kv, 0:256].rearrange("p (a b) -> p a b", a=2)[:, :, 0:30], [tk2])
            self.bfree[6 + kv] = e
            th2.append(e)
        self.afree = tk
        for k in range(2):
            tk = self.mm(self.ps[:, 4, 0:30], self.cw2k[:, l, k, :], HT[:, 0, k, :], k == 0, k == 1, [th2, self.cw2, self.bfree[4]])
        ek = self.cp(KC, self.ps[:, 4, 0:30], [tk])
        self.bfree[4] = ek
        for g in range(2):
            for k in range(2):
                tk = self.mm(self.ps[0:15, 5, 64 * g:64 * g + 64], HT[:, 1, k, 15 * g:15 * g + 15], self.cw2v[:, l, k, :],
                             k == 0, k == 1, [th2, self.cw2, self.bfree[5]])
        ev = self.cp(VC, self.ps[0:15, 5, 0:128].rearrange("p (g d) -> p g d", g=2), [tk, rw])
        self.bfree[5] = ev
        self.debug("kc", KC, [ek])
        sg = self.frt(0, [128, 2, 24])
        tsg = self.af(sg, pj[:, :, 1280:1304], ACT.Sigmoid, [pw])
        sg4 = sg.rearrange("p t (h s) -> p t h s", s=3)
        for t_ in range(2):
            for h in range(8):
                g = h // 4
                c = (4 * t_ + h % 4) * 16
                tk = self.mm(self.ps[:, 6 + g, c:c + 15],
                             QN[64 * g:64 * g + 64, h % 4, 128 * t_:128 * t_ + 128],
                             KC[64 * g:64 * g + 64, 15 * g:15 * g + 15], True, True, [ek, tq, self.bfree[6 + g]])
        Sc = sc(18, [128, 2, 8, 15])
        for t_ in range(2):
            for g in range(2):
                pS = self.ps[:, 6 + g, 64 * t_:64 * t_ + 64].rearrange("p (a c) -> p a c", c=16)
                t = self.tt(Sc[:, t_, 4 * g:4 * g + 4], pS[:, :, 0:15],
                            self.cmask[:, t_, :].unsqueeze(1).to_broadcast([128, 4, 15]), ALU.add, [tk, cw])
        self.bfree[6] = self.bfree[7] = t
        S16 = Sc.rearrange("p t h c -> p (t h) c")
        mx, sm = self.st[:, 40:56], self.st[:, 56:72]
        self.dve(lambda e: e.tensor_reduce(mx, S16, X, ALU.max), [], True)
        self.ts(mx, mx, -1.0e30, ALU.max)
        t = self.tt(S16, S16, mx.unsqueeze(2).to_broadcast([128, 16, 15]), ALU.subtract)
        t = self.af(S16, S16, ACT.Exp, [t], scale=0.125)
        self.dve(lambda e: e.tensor_reduce(sm, S16, X, ALU.add), [t], True)
        self.ts(sm, sm, 1.0e-30, ALU.max)
        self.dve(lambda e: e.reciprocal(sm, sm), [], True)
        self.tt(sm.rearrange("p (t h) -> p t h", t=2), sm.rearrange("p (t h) -> p t h", t=2), sg4[:, :, :, 0], ALU.mult, [tsg])
        t = self.tt(S16, S16, sm.unsqueeze(2).to_broadcast([128, 16, 15]), ALU.mult)
        PC = self.att(0, [15, 16, 128])
        te = []
        for b in range(4):
            for j in range(4):
                tk = self.tr(self.ps[0:15, b, 128 * j:128 * j + 128], S16[:, 4 * b + j, :], [t, self.bfree[b]])
            e = self.cp(PC[:, 4 * b:4 * b + 4, :].rearrange("p a b -> p (a b)"), self.ps[0:15, b, :], [tk, self.afr()], chain=False)
            self.bfree[b] = e
            te.append(e)
        for t_ in range(2):
            for h in range(8):
                tk = self.mm(self.ps[:, 4 + t_, 64 * h:64 * h + 64], PC[:, 8 * t_ + h, :], VC[:, h // 4, :], True, True,
                             [te, ev, self.bfree[4 + t_]])
            e = self.cp(self.mix[:, t_, 0:512], self.ps[:, 4 + t_, :], [tk, self.mixfree, tq, tz])
            self.bfree[4 + t_] = e
        mixc = e
        self.debug("ocmp", self.mix[:, :, 0:512], [e])
        self.apfree = [tk, tk]
        self.aptfree = [tk, tk]
        jobs = []
        for br, kc, vc in ((1, 0, 896), (2, 1, 1152)):
            for p in range(4):
                g = p // 2
                V = lambda t_, g=g, vc=vc: pj[:, t_, vc + 64 * g:vc + 64 * g + 64]
                k_ = KS[64 * g:64 * g + 64, kc, :]
                r = p % 2
                cf = self.frt(48 + 4 * r, [128, 2, 2])
                tmp = self.frt(128 + 256 * r, [128, 2, 2, 64])
                gate = sg4[:, :, 2 * p:2 * p + 2, br].rearrange("p t i -> p i t")
                dst = self.mix[:, :, 128 * p:128 * p + 128].rearrange("p t (i d) -> p i t d", i=2)

                def emit(o_, rib, ri, w_, cf=cf, tmp=tmp, gate=gate, dst=dst):
                    a_ = self.tt(cf, ri, gate, ALU.mult, [w_[1], tsg], chain=False)
                    b_ = self.tt(tmp, o_, cf.unsqueeze(3).to_broadcast([128, 2, 2, 64]), ALU.mult, [a_, w_[0]], chain=False)
                    return b_, self.tt(dst, tmp, dst, ALU.add, [b_, mixc], chain=False)

                jobs.append({"heads": [(QN[64 * g:64 * g + 64, (2 * p + i) % 4, :], k_, V) for i in range(2)],
                             "vd": 64, "w": [tq, tks, w0], "extra": None, "emit": emit})
        lf, la = self.frt(64, [128, 2, 4]), self.frt(72, [128, 2, 4])
        t = self.tt(lf, pj[:, :, 2072:2076], self.row("foxb")[:, 4 * l:4 * l + 4].unsqueeze(1).to_broadcast([128, 2, 4]),
                    ALU.add, [cw, pw])
        t = self.log_sigmoid(lf, la, [t])
        F8 = sc(19, [1, 4, 256])
        nF = sc(14, [1, 4, 256])
        for h in range(4):
            b = 4 + h // 2
            o_ = self.ps[0:1, b, 256 * (h % 2):256 * (h % 2) + 256]
            for t_ in range(2):
                tk = self.mm(o_, lf[:, t_, h:h + 1], self.triu[:, t_, :], t_ == 0, t_ == 1, [t, cw, self.bfree[b]])
        src = self.ps[0:1, 4:6, :].rearrange("p a (b c) -> p (a b) c", c=256)
        e1 = self.ts(F8, src, 8.0, ALU.mult, w=[tk, mixc])
        e2 = self.ts(nF, src, -8.0, ALU.mult, w=[tk])
        self.bfree[4] = self.bfree[5] = e2
        QF = sc(6, [128, 4, 256])
        QM = sc(10, [128, 4, 256])
        tf = []
        for base, dst in ((1304, QF), (2076, QM)):
            for j in range(2):
                a, b_ = base + 128 * j, base + 256 + 128 * j
                bnk = 6 + j
                tf.append(self.T4(dst[:, 2 * j:2 * j + 2, :].rearrange("p a b -> p (a b)"),
                                  [pj[:, 0, a:a + 128], pj[:, 1, a:a + 128], pj[:, 0, b_:b_ + 128], pj[:, 1, b_:b_ + 128]],
                                  [w0, tz, th], free=self.afree, b=bnk, eng="act" if j else "dve"))

        for base, Q_, vcol, fox in ((512, QF, 1816, True), (768, QM, 2588, False)):
            for p in range(2):
                heads = []
                for h in (2 * p, 2 * p + 1):
                    P = slice(64 * (h % 2), 64 * (h % 2) + 64)
                    heads.append((Q_[P, 2 * p, :], Q_[P, 2 * p + 1, :],
                                  lambda t_, h=h, vcol=vcol: pj[:, t_, vcol + 64 * h:vcol + 64 * h + 64]))
                dst = self.mix[:, :, base + 128 * p:base + 128 * p + 128].rearrange("p t (i d) -> p i t d", i=2)

                def extra(i, o_, qt, kt, stop, p=p):
                    h = 2 * p + i
                    self.mm(o_, F8[0:1, h, 128 * qt:128 * qt + 128], self.ones[0:1, 0:128], False, False, [e1, e2])
                    return self.mm(o_, self.ones[0:1, 0:128], nF[0:1, h, 128 * kt:128 * kt + 128], False, stop)

                def emit2(o_, rib, ri, w_, dst=dst):
                    e = self.tt(dst, o_, rib, ALU.mult, [w_, self.mixfree], chain=False)
                    return e, e

                jobs.append({"heads": heads, "vd": 64, "w": [tf], "extra": extra if fox else None, "emit": emit2})
        ow = self.attention(jobs, 0.125)
        self.debug("mix2", self.mix[:, :, :], [ow])
        self.hfree = [ow]
        hs, tl = self.to_T(self.mix, ow)
        self.mixfree = tl
        self.hidfree = [ow, tl]

        def evac2(c, t, bank, width, tk):
            return self.gated_add(1, t, c, bank, tk)

        self.dgtf = [ow] * 4
        self.gate_rows(1)
        self.xw = [[], []]
        self.hfree = self.proj_cb(("w_out2", l), 1024, (self.hhi, self.hlo), hs, evac2)
        self.xnfree = None
        self.debug("xm%d" % l, self.x[:, :, :], self.xw)

    def afr(self):
        return [self.apfree, self.aptfree, self.pjfree]

    def final(self):
        tn = []
        for t in range(2):
            tn.append(self.af(self.xn[:, t, :], self.x[:, t, :], ACT.Square, [self.xw[t], self.xnfree],
                              accum_out=self.st[:, t:t + 1]))
        r = self.rstd(self.st[:, 2:4], self.st[:, 0:2], D, tn)
        fg = self.fing
        dl = self.Q.dma("sp", lambda e: e.dma_start(fg, self.io["fing"].to_broadcast([128, D])), self.s_fg, [self.hfree])
        out = self.io["out"].rearrange("b (t p) d -> p (b t) d", p=128)
        for t in range(2):
            o = self.xn[:, t, :]
            e = self.dve(lambda e, t=t, o=o: e.scalar_tensor_tensor(o, self.x[:, t, :], self.st[:, 2 + t:3 + t], fg,
                                                                    ALU.mult, ALU.mult), [r, dl], True)
            self.Q.dma("sp", lambda e, t=t, o=o: e.dma_start(out[:, t, :], o), self.s_out, [e])

    def col(self, name):
        a, n = COFF[name]
        return self.colp[:, a:a + n]

    def row(self, name):
        a, n = ROFF[name]
        return self.rowp[:, a:a + n]

    def build(self):
        nc, io = self.nc, self.io
        with ExitStack() as ctx:
            def sb(name, shape, dt=F32):
                return ctx.enter_context(nc.sbuf_tensor(name, shape, dt))

            self.ps = ctx.enter_context(nc.psum_tensor("ps", [128, 8, 512], F32))[:, :, :]
            self.raw = sb("raw", [128, NRAW, UW])[:, :, :]
            self.whi = sb("whi", [128, NSPL, UW], F32R)[:, :, :]
            self.wlo = sb("wlo", [128, NSPL, UW], F32R)[:, :, :]
            self.x = sb("x", [128, 2, D])[:, :, :]
            def over(name, shape):
                at = (nc.sbuf_base + 31) // 32 * 32
                base = sb(name, shape)
                assert nc.sbuf_base == at + 4 * shape[1]
                return base, nc.alloc_sbuf_tensor_at(name + "_r", shape, F32R, offset=at)

            hreg, hr = over("hreg", [128, 6144])
            self.hhi = hr[:, 0:2048].rearrange("p (a b) -> p a b", b=256)
            self.hlo = hr[:, 2048:4096].rearrange("p (a b) -> p a b", b=256)
            self.xn = hreg[:, 4096:6144].rearrange("p (a b) -> p a b", a=2)
            self.xnT = hreg[:, 4096:6144].rearrange("p (a b) -> p a b", b=256)
            self.fing = hreg[:, 0:1024]
            ireg, ir = over("ireg", [128, 11264])
            self.hidhi = ir[:, 0:5632].rearrange("p (a b) -> p a b", b=256)
            self.hidlo = ir[:, 5632:11264].rearrange("p (a b) -> p a b", b=256)
            self.pj1 = ireg[:, 0:5664].rearrange("p (a b) -> p a b", a=2)
            self.pj2 = ireg[:, 0:5688].rearrange("p (a b) -> p a b", a=2)
            self.gateb = ireg[:, 0:4096].rearrange("p (a b) -> p a b", b=256)
            self.mhid = ir[:, 4096:6144].rearrange("p (a b c d) -> p a b c d", a=2, b=2, c=2)
            at = 5696
            self.apb = ireg[:, at + 1536:at + 3072].rearrange("p (a b c) -> p a b c", a=2, b=2)
            self.apt = ireg[:, at + 3072:at + 4608].rearrange("p (a b c) -> p a b c", a=2, b=2)
            self.frt_at = at + 4608
            self.mix = sb("mix", [128, 2, D])[:, :, :]
            mixf = self.mix.rearrange("p a b -> p (a b)")
            self.hT = mixf.rearrange("p (a b) -> p a b", b=256)
            self.sil = mixf[:, 0:1024].rearrange("p (a b) -> p a b", b=256)
            self.prd = mixf[:, 1024:2048].rearrange("p (a b) -> p a b", b=256)
            greg = sb("greg", [128, 3072])
            self.gbc = greg[:, 0:1024]
            self.mod2 = sb("mod", [128, 144])[:, :]
            self.acc = sb("acc", [128, NACC, 256])[:, :, :]
            self.adaw = sb("adaw", [128, NADA, 1024])[:, :, :]
            self.ca = sb("ca", [128, 8])[:, :]
            self.colp = sb("colp", [128, NCOL])[:, :]
            self.rowp = sb("rowp", [128, NROW])[:, :]
            cst = sb("cst", [128, NCST])
            def c_(name):
                a, n = CSOFF[name]
                return cst[:, a:a + n]
            self.ident, self.ones, self.mask = c_("ident"), c_("ones"), c_("mask")
            self.triu = c_("triu").rearrange("p (a b) -> p a b", a=2)
            self.mhalf, self.iom4 = c_("mhalf"), c_("iom4")
            self.cmask = c_("cmask").rearrange("p (a b) -> p a b", a=2)
            gf = greg[:, :]
            self.gmask = gf[:, 0:1024].rearrange("p (a b) -> p a b", b=128)
            self.sel16 = gf[0:16, 1024:3072].rearrange("p (a b) -> p a b", b=128)
            self.rw = sb("rw", [128, 8, 20])[:, :, :]
            w2 = greg[:, 1024:1792]
            self.w2 = w2
            self.cw2k = w2[:, 0:512].rearrange("p (l k c) -> p l k c", l=2, k=2)
            self.cw2v = w2[:, 512:768].rearrange("p (l k c) -> p l k c", l=2, k=2)
            self.posi = sb("posi", [128, 2], I32)[:, :]
            self.st = sb("st", [128, 72])[:, :]
            self.st2 = sb("st2", [128, 48])[:, :]
            self.cosT = sb("cosT", [128, 2, 8])[:, :, :]
            self.sinT = sb("sinT", [128, 2, 8])[:, :, :]
            rs = sb("rs", [128, 1088])
            self.dgt = rs[:, 512:1024].rearrange("p (a b) -> p a b", b=128)
            an = sb("an", [128, 40])
            bm = sb("bm", [128, 256], mybir.dt.bfloat16)
            self.identb, self.trib = bm[:, 0:128], bm[:, 128:256]
            self.amx = an[:, 0:8].rearrange("p (a b c) -> p a b c", a=2, b=2)
            self.anm = an[:, 8:16].rearrange("p (a b c) -> p a b c", a=2, b=2)
            self.ars = an[:, 16:24].rearrange("p (a b c) -> p a b c", a=2, b=2)
            self.ari = an[:, 24:32].rearrange("p (a b c) -> p a b c", a=2, b=2)
            hr2 = hreg[:, :]

            def view(base, at, shape):
                n = int(np.prod(shape[1:]))
                v = base[0:shape[0], at:at + n]
                names = "abcd"[:len(shape) - 1]
                if len(shape) == 2:
                    return v
                pat = "p (%s) -> p %s" % (" ".join(names), " ".join(names))
                return v.rearrange(pat, **{k: s for k, s in zip(names, shape[1:])})

            self.scr = lambda kb, shape: view(hr2, kb * 256, shape)
            self.att = lambda kb, shape: view(ireg[:, :], at + kb * 256, shape)
            self.frt = lambda o, shape: view(ireg[:, :], self.frt_at + o, shape)
            self.rsc = lambda o, shape: view(rs[:, :], o, shape)
            areg = ir[:, at + 2048:at + 3968]
            self.ahi = areg[:, 0:960].rearrange("p (a b c) -> p a b c", a=2, b=16)
            self.alo = areg[:, 960:1920].rearrange("p (a b c) -> p a b c", a=2, b=16)

            sems = {e: ctx.enter_context(nc.semaphore("s_" + e)) for e in ("pe", "dve", "act", "pool", "sp")}
            self.s_raw = [ctx.enter_context(nc.semaphore(f"s_raw{i}")) for i in range(NRAW)]
            self.s_c = [ctx.enter_context(nc.semaphore(f"s_c{i}")) for i in range(8)]
            self.s_ada = [ctx.enter_context(nc.semaphore(f"s_ada{i}")) for i in range(NADA)]
            self.s_x = [ctx.enter_context(nc.semaphore(f"s_x{i}")) for i in range(2)]
            self.s_out = ctx.enter_context(nc.semaphore("s_out"))
            self.s_fg = ctx.enter_context(nc.semaphore("s_fg"))

            self.Q = Queues(nc, sems)
            self.nunit = self.nload = self.nahead = self.nsplit = 0
            self.upn = self.hr = 0
            self.loaded, self.ready = [], {}
            self.rawfree = [[] for _ in range(NRAW)]
            self.splfree = [[] for _ in range(NSPL)]
            self.bfree = [None] * 8
            self.silfree = [None] * 4
            self.xnfree = self.hfree = self.pjfree = self.mixfree = None
            self.hidfree = self.modfree = self.gbcfree = self.afree = None
            self.dgtf = [None] * 4
            self.apfree, self.aptfree = [None] * 2, [None] * 2
            self.anfree, self.arfree, self.aifree = [None] * 2, [None] * 2, [None] * 2

            ld = lambda i, dst, src: self.Q.dma("act", lambda e: e.dma_start(dst, src), self.s_c[i])
            xs = io["x"].rearrange("b (t p) d -> p (b t) d", p=128)
            self.xw = [[self.Q.dma("sp", lambda e: e.dma_start(self.x[:, 0, :], xs[:, 0, :]), self.s_x[0])],
                       [self.Q.dma("sp", lambda e: e.dma_start(self.x[:, 1, :], xs[:, 1, :]), self.s_x[1])]]
            self.cw = [ld(3, cst[:, :], io["cst"]), ld(1, self.colp, io["colp"]),
                       ld(2, self.rowp, io["rowp"].to_broadcast([128, NROW])), ld(5, self.rw, io["rw"]),
                       ld(7, self.posi, io["pos"])]
            self.gf = gf
            self.nada, self.adafree, self.adalast = 0, [None] * NADA, None
            self.adagoal = 72
            self.accs, self.accfree, self.modt, self.modlate = [], [None] * NACC, [None] * 2, None
            self.bw = [self.cp(self.identb, self.ident, [self.cw]), self.cp(self.trib, self.mask[:, 0:128])]
            self.cact = self.af(self.ca, self.col("c"), ACT.Silu, [self.cw])
            self.run_stages()

            self.left = nc.sbuf_usable_end - nc.sbuf_base
            self.Q.number()
            block = ctx.enter_context(nc.Block())
            Q = self.Q
            n_out = Q.dma_count.get(id(self.s_out), 0)

            @block.sync
            def _(e):
                Q.run("sp", e)
                e.wait_ge(self.s_out, n_out)

            @block.scalar
            def _(e):
                Q.run("act", e)

            @block.vector
            def _(e):
                Q.run("dve", e)

            @block.gpsimd
            def _(e):
                Q.run("pool", e)

            @block.tensor
            def _(e):
                Q.run("pe", e)

    def run_stages(self):
        s = self.stage
        self.first_mixer()
        if s >= 2:
            self.moe()
        if s >= 3:
            self.rope_tables()
            for l in range(2):
                if l == 0:
                    self.gbcfree = self.xw
                self.ada(l)
                self.ffn(l, 0)
                if s >= 4:
                    self.mixer(l)
                    self.ffn(l, 1)
                if s < 5:
                    break
        self.final()


CONSTS = [("ident", 128), ("ones", 256), ("mask", 384), ("triu", 512), ("mhalf", 32), ("iom4", 8), ("cmask", 30)]
CSOFF, NCST = offsets(CONSTS)


def constants():
    f = np.float32
    c = np.zeros((128, NCST), f)
    p = np.arange(128)

    def put(name, a):
        at, n = CSOFF[name]
        c[:, at:at + n] = np.asarray(a, f).reshape(128, n)

    put("ident", np.eye(128))
    put("ones", np.ones((128, 256)))
    k = np.arange(256)
    put("mask", np.concatenate([np.where(k[None, :128] <= p[:, None], 0, NEG),
                                np.where(k[None, :] <= 128 + p[:, None], 0, NEG)], 1))
    put("triu", np.stack([(128 * t + p[:, None] <= k[None, :]) for t in range(2)], 1))
    put("mhalf", np.full((128, 32), -0.5))
    put("iom4", np.tile(np.arange(4) - 4, (128, 2)))
    ce = np.arange(15) * 16 + 31
    put("cmask", np.stack([np.where(ce[None, :] <= 128 * t + p[:, None], 0, NEG) for t in range(2)], 1))
    c2 = np.zeros((128, 3072), f)
    g = np.zeros((128, 8, 128), f)
    j, i = p[:, None], p[None, :]
    for n, s in enumerate([64, 32, 16, 8, 4, 2, 1]):
        g[:, n, :] = (j // (2 * s) == i // (2 * s)) & (j % (2 * s) < s) & (i % (2 * s) >= s)
    g[:, 7, :] = np.eye(128)
    c2[:, 0:1024] = g.reshape(128, 1024)
    for e in range(16):
        c2[e, 1024 + 128 * e:1152 + 128 * e] = 1.0
    return c, c2


def tall(w):
    return w.reshape(w.shape[0] // 128, 128, -1).transpose(1, 0, 2).reshape(128, -1)


def unit(inp, key):
    name = key[0]
    kind = name[0] if isinstance(name, tuple) else name
    if kind in ("w_in", "w_out", "w_in2", "w_out2"):
        w = inp[{"w_in": "w_in", "w_out": "w_out", "w_in2": "w_in_2", "w_out2": "w_out_2"}[kind]][name[1]]
        c, half = key[1], key[2]
        return tall(w[512 * half:512 * half + 512, c:c + 512])
    if kind == "moe":
        w = inp["expert_w_gate" if key[1] == "a" else "expert_w_up"][0, name[1]]
        return tall(w)
    if kind == "down":
        return tall(inp["expert_w_down"][0, key[1]])
    if kind == "ffn":
        c = 256 * key[2] + (0 if key[1] == "a" else 2816)
        return tall(inp["ffn_w13_2"][name[1], name[2]][:, c:c + 256])
    if kind == "w2":
        _, l, i, j = key
        return tall(inp["ffn_w2_2"][l, i][256 * j:256 * j + 256])
    if kind == "cw1":
        _, l, kv, half = key
        return tall(inp["cmp_w1_2"][l, kv][1024 * half:1024 * half + 1024])
    raise KeyError(key)


def stream(inp, order):
    out = np.zeros((len(order), 128, UW), np.float32)
    for n, (key, width) in enumerate(order):
        out[n, :, :width] = unit(inp, key)
    return out


def ada_stream(inp):
    w = inp["w_ada_2"].reshape(2, 2, 4, 128, 36, 256)
    return np.ascontiguousarray(w.transpose(0, 4, 1, 3, 2, 5)).reshape(144, 128, 1024)


def cols(v):
    return np.ascontiguousarray(v.reshape(-1, 128).T)


def small_inputs(inp):
    f = np.float32
    colp = np.zeros((128, NCOL), f)

    def put(name, a):
        at, n = COFF[name]
        colp[0:a.shape[0], at:at + n] = a.reshape(a.shape[0], n)

    put("mixg", cols(inp["mix_norm_g"]))
    put("ffng", cols(inp["ffn_norm_g"]))
    put("ng2", cols(inp["norm_g_2"]))
    put("glab", cols(inp["gla_gate_b"]))
    put("convb", cols(inp["conv_b"]))
    put("convw", inp["conv_w"][0].T.reshape(2, 128, 31).transpose(1, 0, 2))
    put("c", cols(inp["c_2"]))
    put("bada", cols(inp["b_ada_2"]))
    put("pos", cols(inp["cmp_pos_2"]))
    put("glaw", inp["gla_gate_w"][0])
    rowp = np.zeros((1, NROW), f)

    def row(name, a):
        at, n = ROFF[name]
        rowp[0, at:at + n] = a.reshape(-1)

    row("glang", inp["gla_norm_g"])
    row("cng", inp["conv_norm_g"])
    row("cnb", inp["conv_norm_b"])
    row("qn", inp["diff_qnorm_g"])
    row("kn", inp["diff_knorm_g"])
    row("lq1", inp["diff_lq1"])
    row("lk1", inp["diff_lk1"])
    row("lq2", inp["diff_lq2"])
    row("lk2", inp["diff_lk2"])
    row("subg", inp["diff_subln_g"])
    row("rb", np.concatenate([inp["router_group_b"][0], inp["router_expert_b"][0]]))
    row("foxb", inp["fox_fbias_2"])
    row("inv", np.float32(500000.0) ** (-np.arange(0, 16, 2, dtype=f) / f(16)))
    rw = np.concatenate([inp["router_group_w"][0], inp["router_expert_w"][0]], 1)
    rw = np.ascontiguousarray(rw.reshape(8, 128, 20).transpose(1, 0, 2))
    w2 = inp["cmp_w2_2"].reshape(2, 2, 2, 128, 64)
    wk = np.concatenate([w2[:, 0], w2[:, 0]], -1).transpose(2, 0, 1, 3).reshape(128, 512)
    wv = w2[:, 1].transpose(2, 0, 1, 3).reshape(128, 256)
    cw2 = np.ascontiguousarray(np.concatenate([wk, wv], 1))
    pos = np.ascontiguousarray(inp["positions_2"].reshape(2, 128).T)
    c, c2 = constants()
    return {"x": np.ascontiguousarray(inp["x"]), "colp": colp, "rowp": rowp, "rw": rw, "cw2": cw2, "pos": pos,
            "cst": c, "cst2": c2, "fing": np.ascontiguousarray(inp["final_g_2"].reshape(1, D))}


SHAPES = {"x": (1, 256, D), "colp": (128, NCOL), "rowp": (1, NROW), "rw": (128, 8, 20), "cw2": (128, 768),
          "cst": (128, NCST), "cst2": (128, 3072), "fing": (1, D)}


def program(nc, order, split, stage=9, dbg=None):
    io = {k: nc.dram_tensor("in_" + k, s, F32, kind="ExternalInput").ap() for k, s in SHAPES.items()}
    io["pos"] = nc.dram_tensor("in_pos", (128, 2), I32, kind="ExternalInput").ap()
    io["wu"] = nc.dram_tensor("in_wu", (len(order) if order else 400, 128, UW), F32, kind="ExternalInput").ap()
    io["wada"] = nc.dram_tensor("in_wada", (144, 128, 1024), F32, kind="ExternalInput").ap()
    io["out"] = nc.dram_tensor("out_0", (1, 256, D), F32, kind="ExternalOutput").ap()
    dd = {k: nc.dram_tensor("dbg_" + k, s, F32, kind="ExternalOutput").ap() for k, s in (dbg or {}).items()}
    b = Build(nc, io, order, order is None, stage, dd)
    b.order_split = split if order else {}
    if order is None:
        b.order = []
    b.build()
    return b.asked, b.order_split


def kernel(**inputs):
    import concourse.bacc as bacc
    from concourse.bass_utils import run_bass_kernel_spmd

    inp = {k: np.asarray(v) for k, v in inputs.items()}
    order, split = program(bacc.Bacc("TRN2", target_bir_lowering=False, num_devices=1), None, None)
    nc = bacc.Bacc("TRN2", target_bir_lowering=False, num_devices=1)
    program(nc, order, split)
    arrays = {"in_" + k: v for k, v in small_inputs(inp).items()}
    arrays["in_wu"] = stream(inp, order)
    arrays["in_wada"] = ada_stream(inp)
    r = run_bass_kernel_spmd(nc, [arrays], core_ids=[0])
    return r.results[0]["out_0"]
```

```python
from contextlib import ExitStack

import numpy as np
import concourse.bass as bass
from concourse import mybir

ALU = mybir.AluOpType
ACT = mybir.ActivationFunctionType
F32 = mybir.dt.float32
F32R = mybir.dt.float32r
I32 = mybir.dt.int32
X = mybir.AxisListType.X

D = 1024
EPS = 1e-6
UW = 2048
NRAW = 4
NADA = 2
NSPL = 3
NACC = 4
NEG = -3.0e38

COLS = [("mixg", 8), ("ffng", 8), ("ng2", 48), ("glab", 1), ("convb", 2), ("convw", 62),
        ("c", 8), ("bada", 144), ("pos", 64), ("glaw", 128)]
ROWS = [("glang", 64), ("cng", 256), ("cnb", 256), ("qn", 64), ("kn", 64), ("lq1", 64), ("lk1", 64),
        ("lq2", 64), ("lk2", 64), ("subg", 128), ("rb", 20), ("foxb", 8), ("inv", 8)]


def offsets(table):
    at, out = 0, {}
    for name, n in table:
        out[name] = (at, n)
        at += n
    return out, at


COFF, NCOL = offsets(COLS)
ROFF, NROW = offsets(ROWS)


class Tok:

    def __init__(self, eng, sem=None, value=None):
        self.eng, self.sem, self.value, self.used = eng, sem, value, False


class Queues:

    def __init__(self, nc, sems):
        self.nc, self.sems = nc, sems
        self.q = {e: [] for e in sems}
        self.last = {}
        self.dma_count = {}
        self.bar = {}

    def put(self, eng, fn, waits=(), chain=False):
        tok = Tok(eng)
        flat = []

        def add(w):
            if w is None:
                return
            if isinstance(w, Tok):
                w.used = True
                flat.append(w)
            else:
                for v in w:
                    add(v)

        add(waits)
        if eng in self.bar:
            flat.append(self.bar.pop(eng))
        if chain and eng in self.last:
            add(self.last[eng])
        self.q[eng].append((fn, flat, tok))
        self.last[eng] = tok
        return tok

    def dma(self, eng, fn, sem, waits=()):
        flat = []

        def add(w):
            if w is None:
                return
            if isinstance(w, Tok):
                w.used = True
                flat.append(w)
            else:
                for v in w:
                    add(v)

        add(waits)
        n = self.dma_count.get(id(sem), 0) + 16
        self.dma_count[id(sem)] = n
        tok = Tok("dma", sem, n)
        self.q[eng].append((lambda e: fn(e).then_inc(sem, 16), flat, None))
        return tok

    def number(self):
        for eng, items in self.q.items():
            n = 0
            for _, _, tok in items:
                if tok is not None and tok.used:
                    n += 1
                    tok.sem, tok.value = self.sems[eng], n

    def run(self, eng, e):
        seen = {}
        for fn, waits, tok in self.q[eng]:
            need = {}
            for w in waits:
                k = id(w.sem)
                if w.value > max(seen.get(k, 0), need.get(k, (None, 0))[1]):
                    need[k] = (w.sem, w.value)
            for k, (s, v) in need.items():
                e.wait_ge(s, v)
                seen[k] = v
            ins = fn(e)
            if tok is not None and tok.used:
                ins.then_inc(tok.sem, 1)


class Build:
    def __init__(self, nc, io, order, dry, stage, dbg):
        self.nc, self.io, self.order, self.dry = nc, io, order, dry
        self.stage, self.dbg = stage, dbg
        self.asked = []

    def pe(self, fn, w=()):
        return self.Q.put("pe", fn, w)

    def dve(self, fn, w=(), chain=True):
        return self.Q.put("dve", fn, w, chain)

    def act(self, fn, w=(), chain=True):
        return self.Q.put("act", fn, w, chain)

    def pool(self, fn, w=(), chain=True):
        return self.Q.put("pool", fn, w, chain)

    def tt(self, out, a, b, op, w=(), chain=True):
        return self.dve(lambda e: e.tensor_tensor(out, a, b, op), w, chain)

    def ptt(self, out, a, b, op, w=()):
        return self.pool(lambda e: e.tensor_tensor(out, a, b, op), w, False)

    def ts(self, out, a, s1, op0, s2=None, op1=None, w=(), chain=True):
        if op1 is None:
            return self.dve(lambda e: e.tensor_scalar(out, a, s1, None, op0), w, chain)
        return self.dve(lambda e: e.tensor_scalar(out, a, s1, s2, op0, op1), w, chain)

    def cp(self, out, a, w=(), chain=True):
        return self.dve(lambda e: e.tensor_copy(out, a), w, chain)

    def acopy(self, out, a, w=(), chain=True, scale=1.0):
        return self.act(lambda e: e.activation(out, a, ACT.Copy, scale=scale), w, chain)

    def af(self, out, a, f, w=(), chain=True, **kw):
        return self.act(lambda e: e.activation(out, a, f, **kw), w, chain)

    def mm(self, out, lhsT, rhs, start, stop, w=()):
        return self.pe(lambda e: e.matmul(out, lhsT, rhs, start=start, stop=stop), w)

    def tr(self, out, in_, w=()):
        ident = self.ident[0:in_.shape[0], 0:in_.shape[0]]
        return self.pe(lambda e: e.transpose(out, in_, ident), [w, self.cw])

    def debug(self, name, ap, w):
        if name in self.dbg and not self.dry:
            t = self.Q.dma("sp", lambda e: e.dma_start(self.dbg[name], ap), self.s_out, w)
            self.Q.bar = {e: t for e in ("pe", "dve", "act", "pool")}

    def load(self, n):
        key, width = self.order[n]
        slot = n % NRAW
        raw = self.raw[:, slot, 0:width]
        src = self.io["wu"][n, :, 0:width]
        self.loaded.append(self.Q.dma("sp", lambda e: e.dma_start(raw, src), self.s_raw[slot],
                                      [self.rawfree[slot], self.start if n else None]))
        self.rawfree[slot] = None

    def split(self, n):
        key, width = self.order[n]
        slot, m = n % NRAW, self.nsplit % NSPL
        self.nsplit += 1
        raw = self.raw[:, slot, 0:width]
        hi, lo = self.whi[:, m, 0:width], self.wlo[:, m, 0:width]
        th = self.acopy(hi, raw, [self.loaded[n], self.splfree[m]], chain=False)
        tl = self.tt(lo, raw, hi.bitcast(F32), ALU.subtract, [self.loaded[n], th, self.splfree[m]], chain=False)
        self.rawfree[slot] = [th, tl]
        self.splfree[m] = None
        self.ready[n] = (m, th, tl)

    def take(self, key, width=UW, split=True):
        n = self.nunit
        self.nunit += 1
        self.asked.append((key, width))
        if self.dry:
            self.order.append((key, width))
            self.order_split[n] = split
        assert self.order[n] == (key, width)
        total = n + 1 if self.dry else len(self.order)
        self.ahead(n)
        return n

    def ahead(self, n):
        total = n + 1 if self.dry else len(self.order)
        while self.nload < min(n + NRAW, total):
            if self.nload - NRAW >= 0 and self.rawfree[self.nload % NRAW] is None:
                break
            self.load(self.nload)
            self.nload += 1
        while self.nahead < min(n + NSPL, total, self.nload):
            if self.order_split[self.nahead]:
                if self.nsplit >= NSPL and self.splfree[self.nsplit % NSPL] is None:
                    break
                self.split(self.nahead)
            self.nahead += 1
            while self.nload < min(n + NRAW, total) and self.rawfree[self.nload % NRAW] is not None:
                self.load(self.nload)
                self.nload += 1
        assert self.nahead > n, (n, self.nahead, self.nload)

    def give(self, n, tok):
        if self.order_split[n]:
            self.splfree[self.ready[n][0]] = tok
        else:
            self.rawfree[n % NRAW] = tok

    def lin_rows(self, bank, hT, hw, kts, n, off, width, step, t, first, last, w=()):
        m, th, tl = self.ready[n]
        hi, lo = hT
        tok = None
        for i, kt in enumerate(kts):
            wh = self.whi[:, m, off + i * step:off + i * step + width]
            wl = self.wlo[:, m, off + i * step:off + i * step + width]
            xh, xl = hi[:, kt, t * 128:t * 128 + 128], lo[:, kt, t * 128:t * 128 + 128]
            f = first and i == 0
            la = last and i == len(kts) - 1
            self.mm(bank, xh, wh, f, False, [w, hw[kt // 2], th] if i == 0 else hw[kt // 2])
            self.mm(bank, xl, wh, False, False)
            tok = self.mm(bank, xh, wl, False, la, [tl] if i == 0 else ())
        return tok

    def up(self, name, j, hT, hw, first):
        n1 = self.take((name, "a", j))
        outs = []
        m1, th1, tl1 = self.ready[n1]
        hi, lo = hT
        ab = []

        def tile(n, f, bank, w):
            m, th, tl = self.ready[n]
            for kt in range(8):
                c = kt * 256 + f * 128
                wh, wl = self.whi[:, m, c:c + 128], self.wlo[:, m, c:c + 128]
                self.mm(bank, wh, hi[:, kt, :], kt == 0, False, [w, hw[kt // 2], th] if kt == 0 else hw[kt // 2])
                self.mm(bank, wh, lo[:, kt, :], False, False)
                tok = self.mm(bank, wl, hi[:, kt, :], False, kt == 7, [tl] if kt == 0 else ())
            return tok

        ta = [None, None]
        for f in range(2):
            ta[f] = tile(n1, f, self.ps[:, 4 + f, 0:256], [self.bfree[4 + f]])
        self.give(n1, ta[1])
        if name[0] == "moe":
            self.fill()
        n2 = self.take((name, "b", j))
        tb = [None, None]
        done = []
        for f in range(2):
            if f == 1 and len(self.accs) > 1:
                done, tk = self.sum_acc(7, 1)
            tb[f] = tile(n2, f, self.ps[:, 6 + f, 0:256], [self.bfree[6 + f]])
        self.give(n2, tb[1])
        self.modlate = self.put_mod(7, done, tb[1])
        return ta, tb

    def hidden(self, f, ta, tb, hi, lo, free, gate=None, gw=None):
        r = self.hr % 4
        self.hr += 1
        s, p = self.sil[:, r, :], self.prd[:, r, :]
        t1 = self.af(s, self.ps[:, 4 + f, 0:256], ACT.Silu, [ta, self.silfree[r]], chain=False)
        self.bfree[4 + f] = t1
        late = self.modlate if f == 1 else None
        if gate is not None:
            t0 = self.tt(p, self.ps[:, 6 + f, 0:256], gate, ALU.mult, [tb, gw, self.silfree[r]], chain=False)
            self.bfree[6 + f] = [t0, late]
            t2 = self.tt(p, p, s, ALU.mult, [t1, t0], chain=False)
        else:
            t2 = self.tt(p, self.ps[:, 6 + f, 0:256], s, ALU.mult, [tb, t1, self.silfree[r]], chain=False)
            self.bfree[6 + f] = [t2, late]
        t3 = self.acopy(hi, p, [t2, free], chain=False)
        t4 = self.tt(lo, p, hi.bitcast(F32), ALU.subtract, [t3, free], chain=False)
        self.silfree[r] = [t3, t4]
        return [t3, t4]

    def rstd(self, out, ss, n, w):
        m = ss.shape[-1]
        t = self.ts(out, ss, 1.0 / n, ALU.mult, EPS, ALU.add, w)
        return self.pool(lambda e: e.tensor_tensor(out, out, self.mhalf[:, 0:m], ALU.pow), [t, self.cw])

    def norm_T(self, g, shift, gw, early=False):
        dg, sq = [], []
        for t in range(2):
            tk = self.af(self.xn[:, t, :], self.x[:, t, :], ACT.Square, [self.xw[t], self.xnfree], chain=False,
                         accum_out=self.st[:, t:t + 1])
            sq.append(tk)
            if early and t == 1 and not self.dry:
                self.load(0)
                self.nload = 1
                self.split(0)
                self.nahead = 1
            r = self.rstd(self.st[:, 2 + t:3 + t], self.st[:, t:t + 1], D, [tk])
            d = self.ts(self.dgt[:, t, :], self.ident, self.st[:, 2 + t:3 + t], ALU.mult, w=[r, self.dgtf[t]])
            dg.append(d)
        self.xnfree = sq
        tk = [None] * 4
        for kp in range(4):
            for t in range(2):
                for k in range(2):
                    kt = 2 * kp + k
                    o = self.ps[:, kp, k * 256 + t * 128:k * 256 + t * 128 + 128]
                    tk[kp] = self.mm(o, self.x[:, t, kt * 128:kt * 128 + 128], self.dgt[:, t, :], True, True,
                                     [dg[t], self.bfree[kp]])
        self.dgtf[0] = self.dgtf[1] = tk[3]
        hs = []
        for kp in range(4):
            es = []
            for k in range(2):
                kt = 2 * kp + k
                src = self.ps[:, kp, k * 256:k * 256 + 256]
                w = [tk[kp], gw, self.mixfree]
                if kp % 2:
                    bias = 0.0 if shift is None else shift[:, kt:kt + 1]
                    e = self.af(self.hT[:, kt, :], src, ACT.Identity, w, chain=False, scale=g[:, kt:kt + 1], bias=bias)
                elif shift is None:
                    e = self.ts(self.hT[:, kt, :], src, g[:, kt:kt + 1], ALU.mult, w=w, chain=False)
                else:
                    e = self.ts(self.hT[:, kt, :], src, g[:, kt:kt + 1], ALU.mult, shift[:, kt:kt + 1], ALU.add,
                                w=w, chain=False)
                es.append(e)
            self.bfree[kp] = es
            hs.append(self.halves(kp, self.hT, es))
        self.mixfree = hs
        self.silfree = [hs] * 4
        return hs

    def halves(self, kp, src, w):
        c = slice(2 * kp, 2 * kp + 2)
        h = self.acopy(self.hhi[:, c, :], src[:, c, :], [w, self.hfree], chain=False)
        l = self.tt(self.hlo[:, c, :], src[:, c, :], self.hhi[:, c, :].bitcast(F32), ALU.subtract, [h, w], chain=False)
        return [h, l]

    def T4(self, dst, srcs, w, free=None, b=7, scale=None, eng="dve"):
        for i, s in enumerate(srcs):
            tk = self.tr(self.ps[0:s.shape[-1], b, i * 128:i * 128 + 128], s, [w, self.bfree[b]])
        n = len(srcs)
        src = self.ps[0:srcs[0].shape[-1], b, 0:n * 128]
        if scale is not None:
            e = self.ts(dst, src, scale, ALU.mult, w=[tk, free], chain=False)
        elif eng == "act":
            e = self.acopy(dst, src, [tk, free], chain=False)
        else:
            e = self.cp(dst, src, [tk, free], chain=False)
        self.bfree[b] = e
        return e

    def attention(self, jobs, scale, between=()):
        n = len(jobs)
        exps, moved = {}, {}

        def scores(g):
            r, job = g % 2, jobs[g]
            toks = []
            for i, (qT, kT, _) in enumerate(job["heads"]):
                b = 2 * r + i
                for j, (qt, kt) in enumerate(((0, 0), (1, 0), (1, 1))):
                    o = self.ps[:, b, 128 * j:128 * j + 128]
                    ex = job["extra"]
                    self.mm(o, qT[:, 128 * qt:128 * qt + 128], kT[:, 128 * kt:128 * kt + 128], True,
                            ex is None and qt != kt, [job["w"], self.bfree[b]])
                    if ex is not None:
                        ex(i, o, qt, kt, qt != kt)
                    if qt == kt:
                        self.mm(o, self.identb, self.trib, False, True, [self.bw])
                toks.append(self.Q.last["pe"])
            ps2 = self.ps[:, 2 * r:2 * r + 2, :]
            mx = self.amx[:, r, :, :]
            t1 = self.dve(lambda e: e.tensor_reduce(mx[:, :, 0], ps2[:, :, 0:128], X, ALU.max), [toks], chain=False)
            t2 = self.dve(lambda e: e.tensor_reduce(mx[:, :, 1], ps2[:, :, 128:384], X, ALU.max), [toks], chain=False)
            t3 = self.ts(self.anm[:, r, :, :], mx, -scale, ALU.mult, w=[t1, t2, self.anfree[r]], chain=False)
            P = self.apb[:, r, :, :]
            te = []
            for i in range(2):
                for t in range(2):
                    a, z = (0, 128) if t == 0 else (128, 384)
                    te.append(self.af(P[:, i, a:z], ps2[:, i, a:z], ACT.Exp, [t3, self.apfree[r], self.arfree[r]], chain=False,
                                      scale=scale, bias=self.anm[:, r, i, t:t + 1],
                                      accum_out=self.ars[:, r, i, t:t + 1]))
                self.bfree[2 * r + i] = te[-2:]
            self.anfree[r] = te
            exps[g] = te

        def turn(g):
            r, te = g % 2, exps[g]
            tr = self.dve(lambda e: e.reciprocal(self.ari[:, r, :, :], self.ars[:, r, :, :]), [te, self.aifree[r]], chain=False)
            self.arfree[r] = tr
            pt = self.apt[:, r, :, :]
            ev = []
            for i in range(2):
                b = 4 + i
                for c in range(3):
                    tk = self.tr(self.ps[:, b, c * 128:c * 128 + 128], self.apb[:, r, i, c * 128:c * 128 + 128],
                                 [te[2 * i:2 * i + 2], self.bfree[b]])
                if i == 0:
                    e = self.acopy(pt[:, i, :], self.ps[:, b, 0:384], [tk, self.aptfree[r]], chain=False)
                else:
                    e = self.cp(pt[:, i, :], self.ps[:, b, 0:384], [tk, self.aptfree[r]], chain=False)
                self.bfree[b] = e
                ev.append(e)
            self.apfree[r] = tk
            moved[g] = (ev, tr)

        def values(g):
            r, job = g % 2, jobs[g]
            ev, tr = moved[g]
            pt, vd, b = self.apt[:, r, :, :], job["vd"], 6 + r
            for i, (_, _, V) in enumerate(job["heads"]):
                for t in range(2):
                    o = self.ps[:, b, (i * 2 + t) * 128:(i * 2 + t) * 128 + vd]
                    if t == 0:
                        tk = self.mm(o, pt[:, i, 0:128], V(0), True, True, [ev[i], job["w"], self.bfree[b]])
                    else:
                        self.mm(o, pt[:, i, 128:256], V(0), True, False)
                        tk = self.mm(o, pt[:, i, 256:384], V(1), False, True)
            self.aptfree[r] = tk
            o = self.ps[:, b, :].rearrange("p (i t d) -> p i t d", i=2, t=2)[:, :, :, 0:vd]
            first, last = job["emit"](o, self.ari[:, r, :, :].unsqueeze(3).to_broadcast([128, 2, 2, vd]),
                                      self.ari[:, r, :, :], [tk, tr])
            self.bfree[b] = first
            self.aifree[r] = first
            return last

        out = []
        for g in range(n + 2):
            if g < n:
                scores(g)
            if 0 <= g - 1 < n:
                turn(g - 1)
            if g < len(between):
                between[g]()
            if g >= 2:
                out.append(values(g - 2))
                if self.nada < self.adagoal:
                    self.fill(1)
                    self.flush(keep=1)
        return out

    def to_T(self, src, w):
        es, last = [], None
        for kp in range(4):
            b = kp
            for k in range(2):
                kt = 2 * kp + k
                for t in range(2):
                    o = self.ps[:, b, k * 256 + t * 128:k * 256 + t * 128 + 128]
                    last = self.tr(o, src[:, t, kt * 128:kt * 128 + 128], [w, self.bfree[b]])
            dst = self.xnT[:, 2 * kp:2 * kp + 2, :].rearrange("p a b -> p (a b)")
            e = self.cp(dst, self.ps[:, b, :], [last, self.hfree], chain=False)
            self.bfree[b] = e
            es.append(e)
        return [self.halves(kp, self.xnT, [es[kp]]) for kp in range(4)], last

    def proj_cb(self, name, ncols, hT, hw, evac, hooks=None):
        for c in range(0, ncols, 512):
            width = min(512, ncols - c)
            bt = [None, None]
            for half in range(2):
                n = self.take((name, c, half), 4 * width)
                for t in range(2):
                    b = (2 * (c // 512) + t) % 4
                    bt[t] = self.lin_rows(self.ps[:, b, 0:width], hT, hw, range(4 * half, 4 * half + 4), n, 0, width,
                                          width, t, half == 0, half == 1, self.bfree[b] if half == 0 else None)
                self.give(n, bt[1])
                self.fill()
            for t in range(2):
                b = (2 * (c // 512) + t) % 4
                self.bfree[b] = evac(c, t, self.ps[:, b, 0:width], width, bt[t])
            if hooks and c in hooks:
                hooks[c]()
            if self.nada < self.adagoal:
                self.flush(keep=1)
        return bt[1]

    def norm_stats(self, y, gs, sq, st, w):
        self.tt(sq, y, y, ALU.mult, w)
        t = self.dve(lambda e: e.tensor_reduce(st, sq, X, ALU.add), chain=True)
        return self.rstd(st, st, gs, [t])

    def norm_scale(self, y, st, gs, w):
        return self.tt(y, y, st.unsqueeze(2).to_broadcast([128, y.shape[1], gs]), ALU.mult, w)

    def negabs(self, out, a, w):
        return self.dve(lambda e: e.scalar_tensor_tensor(out, a, -1.0, a, ALU.mult, ALU.min), w, True)

    def log_sigmoid(self, z, a, w):
        self.negabs(a, z, w)
        t = self.Q.last["dve"]
        self.af(a, a, ACT.Exp, [t])
        t = self.af(a, a, ACT.Ln, bias=1.0)
        self.ts(z, z, 0.0, ALU.min)
        return self.tt(z, z, a, ALU.subtract, [t])

    def first_mixer(self):
        pj = self.pj1
        hs = self.norm_T(self.col("mixg"), None, self.cw, early=True)
        self.bw = [self.cp(self.identb, self.ident, [self.cw]), self.cp(self.trib, self.mask[:, 0:128])]
        self.cact = self.af(self.ca, self.col("c"), ACT.Silu, [self.cw], chain=False)
        ld = lambda i, dst, src: self.Q.dma("act", lambda e: e.dma_start(dst, src), self.s_c[i], hs[0])
        cw = self.cw = self.cw + [ld(2, self.rowp, self.io["rowp"].to_broadcast([128, NROW])),
                                  ld(5, self.rw, self.io["rw"]), ld(7, self.posi, self.io["pos"])]

        def masks():
            self.gmw = self.Q.dma("act", lambda e: e.dma_start(self.gf, self.io["cst2"]), self.s_c[4], hs)

        pw = []

        def evac(c, t, bank, width, tk):
            if t == 0:
                e = self.acopy(pj[:, t, c:c + width], bank, [tk], chain=False)
            else:
                e = self.cp(pj[:, t, c:c + width], bank, [tk], chain=False)
            pw.append(e)
            return e

        last = self.proj_cb(("w_in", 0), 2832, (self.hhi, self.hlo), hs, evac, {1536: masks})
        self.hfree = last
        self.debug("pj1", pj[:, :, :], pw)
        sc = self.scr
        qk = sc(0, [128, 2, 256])
        bb = sc(2, [128, 256])
        aa = sc(3, [128, 256])
        qe = sc(4, [128, 8, 256])
        ke = sc(12, [128, 8, 256])
        o = sc(20, [128, 8, 64])
        osq = sc(22, [128, 8, 64])
        mk = self.att(0, [128, 8, 128])
        st = self.att(4, [128, 2, 3, 128])
        glr = self.att(8, [16, 256])
        cz = self.att(9, [128, 2, 256])
        dg = self.att(11, [128, 4, 128])
        yf = self.att(13, [128, 2, 256])
        zT = self.att(15, [128, 2, 288])
        y = self.att(9, [128, 8, 64])
        ysq = self.att(11, [128, 8, 64])
        tg = self.T4(glr, [pj[:, 0, 512:528], pj[:, 1, 512:528]], [pw, last], b=6)
        t = self.af(cz, pj[:, :, 1040:1296], ACT.Sigmoid, [pw])
        tq = self.T4(qk[:, 0, :], [pj[:, 0, 0:128], pj[:, 1, 0:128]], [pw, last], scale=float(32 ** -0.5), b=4)
        tk_ = self.T4(qk[:, 1, :], [pj[:, 0, 128:256], pj[:, 1, 128:256]], [pw, last], b=5, eng="act")
        tcz = self.tt(cz, cz, pj[:, :, 784:1040], ALU.mult, [t])
        z = self.ps[:, 7, 0:256]
        t = self.mm(z, self.col("glaw")[0:16, :], glr, True, True, [tg, cw, self.bfree[7]])
        t = self.ts(aa, z, self.col("glab"), ALU.add, w=[t, cw])
        self.bfree[7] = t
        t0 = self.dve(lambda e: e.memset(zT[:, :, 0:32], 0.0), [last], False)
        self.negabs(bb, aa, [t])
        t = self.Q.last["dve"]
        self.af(bb, bb, ACT.Exp, [t])
        tl = self.af(bb, bb, ACT.Ln, bias=1.0)
        tz = []
        for ct in range(2):
            tz.append(self.T4(zT[:, ct, 30:286], [cz[:, 0, 128 * ct:128 * ct + 128], cz[:, 1, 128 * ct:128 * ct + 128]],
                              [tcz], free=t0, b=4 + ct, eng="act"))
        dgf = [None] * 4
        taps = [(ct, k) for ct in range(2) for k in range(31)]
        cv = [None, None]

        def conv(n):
            for _ in range(n):
                ct, k = taps.pop(0)
                r = (31 * ct + k) % 4
                c = self.col("convw")[:, 31 * ct + k:31 * ct + k + 1]
                d = self.acopy(dg[:, r, :], self.ident, [cw, dgf[r], last], chain=False, scale=c)
                dgf[r] = cv[ct] = self.mm(self.ps[:, 6, 256 * ct:256 * ct + 256], dg[:, r, :], zT[:, ct, k:k + 256],
                                          k == 0, k == 30, [d, tz, self.bfree[6]])
                if k % 8 == 7:
                    self.fill(1)
                    self.flush(keep=1)

        lam = self.st[:, 32:36]
        lw = self.att(7, [128, 2, 64])
        self.tt(lw[:, 0, :], self.row("lq1"), self.row("lk1"), ALU.mult, [cw])
        self.tt(lw[:, 1, :], self.row("lq2"), self.row("lk2"), ALU.mult)
        t = self.dve(lambda e: e.tensor_reduce(lam[:, 0:2], lw, X, ALU.add), [], True)
        t = self.af(lam[:, 0:2], lam[:, 0:2], ACT.Exp, [t])
        t = self.tt(lam[:, 2:3], lam[:, 1:2], lam[:, 0:1], ALU.subtract, [t])
        self.lamt = self.ts(lam[:, 3:4], lam[:, 2:3], -0.2, ALU.add)
        conv(24)
        self.ts(aa, aa, 0.0, ALU.min)
        self.tt(aa, aa, bb, ALU.subtract, [tl])
        t = self.ts(aa, aa, 1.0 / 16.0, ALU.mult)
        t = self.dve(lambda e: e.tensor_tensor_scan(bb, self.ones[:, 0:256], aa, 0.0, ALU.mult, ALU.add), [t], True)
        lv = []
        for li, s in enumerate([128, 64, 32, 16, 8, 4, 2, 1]):
            nb = 128 // s
            bv = bb.rearrange("p (n s) -> p n s", s=2 * s)
            dv = ke[:, li, :].rearrange("p (n s) -> p n s", s=2 * s)
            lv.append(self.tt(dv, bv, bv[:, :, s - 1:s].to_broadcast([128, nb, 2 * s]), ALU.subtract, [t], chain=False))
        te = []
        for q_ in range(2):
            v = ke[:, 4 * q_:4 * q_ + 4, :]
            t = self.negabs(v, v, lv)
            te.append(self.af(v, v, ACT.Exp, [t], chain=False))
        t1, t2 = [], []
        for q_ in range(2):
            kv = ke[:, 4 * q_:4 * q_ + 4, :]
            qv = qe[:, 4 * q_:4 * q_ + 4, :]
            t1.append(self.tt(qv, kv, qk[:, 0, :].unsqueeze(1).to_broadcast([128, 4, 256]), ALU.mult, [te[q_], tq], chain=False))
            t2.append(self.tt(kv, kv, qk[:, 1, :].unsqueeze(1).to_broadcast([128, 4, 256]), ALU.mult, [t1[q_], tk_], chain=False))
        conv(38)
        tf = self.af(yf, self.ps[:, 6, :].rearrange("p (a b) -> p a b", a=2), ACT.Copy, [cv], chain=False)
        self.bfree[6] = tf
        e = []
        for ct in range(2):
            v = yf[:, ct, :]
            e.append(self.ts(v, v, self.col("convb")[:, ct:ct + 1], ALU.add, w=[tf], chain=False))
        q = pj[:, :, 1296:2320]
        q4 = pj[:, :, 1296:2320].rearrange("p t (g d) -> p t g d", d=64)
        ss = self.st2[:, 0:32].rearrange("p (t g) -> p t g", t=2)
        junk = self.att(8, [128, 4, 64])
        sqs = []

        def squares(t_):
            for g in range(16):
                sqs.append(self.af(junk[:, g % 4, :], q4[:, t_, g, :], ACT.Square, [tg, sqs[-4:-3]], chain=False, accum_out=ss[:, t_, g:g + 1]))

        ob = self.ps[:, 6, :].rearrange("p (a b) -> p a b", b=64)
        stf = [None, None]
        mu = self.st[:, 24:32]
        y2 = y.rearrange("p (t c) d -> p t (c d)", t=2)
        qk2 = []
        for h in range(4):
            P = slice(32 * h, 32 * h + 32)
            r = h % 2
            b01 = self.ps[:, 4 + r, 0:128]
            t = self.mm(b01, ke[P, 0, 0:128], qe[P, 0, 128:256], True, True, [t1, t2, self.bfree[4 + r]])
            e1 = self.acopy(st[:, r, 1, :], b01, [t, stf[r]], chain=False)
            self.bfree[4 + r] = e1
            ev = [e1]
            for blk in range(2):
                B = slice(128 * blk, 128 * blk + 128)
                for l in range(8):
                    bank = 2 * blk + l // 4
                    oo = self.ps[:, bank, (l % 4) * 128:(l % 4) * 128 + 128]
                    if l < 7:
                        a_, b_ = ke[P, l + 1, B], qe[P, l + 1, B]
                    else:
                        a_, b_ = qk[P, 1, B], qk[P, 0, B]
                    t = self.mm(oo, a_, b_, True, True, [self.bfree[bank], t1, t2])
                e2 = self.tt(mk, self.ps[:, 2 * blk:2 * blk + 2, :].rearrange("p a (b c) -> p (a b) c", c=128),
                             self.gmask, ALU.mult, [t, self.gmw])
                self.bfree[2 * blk] = self.bfree[2 * blk + 1] = e2
                ms = mk.rearrange("p l i -> p i l")
                dst = st[:, r, 2 * blk, :]
                ev.append(self.dve(lambda e, dst=dst, ms=ms: e.tensor_reduce(dst, ms, X, ALU.add), [stf[r]], True))
            if h == 0:
                for t_ in range(2):
                    for ct in range(2):
                        ty = self.tr(self.ps[:, 7, (2 * t_ + ct) * 128:(2 * t_ + ct) * 128 + 128],
                                     yf[:, ct, 128 * t_:128 * t_ + 128], [e, self.bfree[7]])
            v = [pj[:, t_, 256 + 64 * h:320 + 64 * h] for t_ in range(2)]
            self.mm(ob[:, h, :], st[:, r, 0, :], v[0], True, True, [ev, self.bfree[6]])
            self.mm(ob[:, 4 + h, :], st[:, r, 1, :], v[0], True, False)
            stf[r] = t = self.mm(ob[:, 4 + h, :], st[:, r, 2, :], v[1], False, True)
            if h == 0:
                ty = self.acopy(y, self.ps[:, 7, :].rearrange("p (a b) -> p a b", b=64), [ty], chain=False)
                self.bfree[7] = ty
                squares(0)
                self.dve(lambda e: e.tensor_reduce(mu, y, X, ALU.add), [ty], True)
                self.ts(mu, mu, 1.0 / 64, ALU.mult)
                self.tt(y, y, mu.unsqueeze(2).to_broadcast([128, 8, 64]), ALU.subtract)
                yr = self.norm_stats(y, 64, ysq, self.st[:, 56:64], [])
            if h == 1:
                squares(1)
                self.norm_scale(y, self.st[:, 56:64], 64, [yr])
                self.tt(y2, y2, self.row("cng").unsqueeze(1).to_broadcast([128, 2, 256]), ALU.mult)
                ty = self.tt(y2, y2, self.row("cnb").unsqueeze(1).to_broadcast([128, 2, 256]), ALU.add)
                m2 = self.af(self.mix[:, :, 256:512], y2, ACT.Silu, [ty], chain=False)
                rq = self.rstd(self.st2[:, 0:32], self.st2[:, 0:32], 64, sqs)
                for t_ in range(2):
                    w = self.ptt(q4[:, t_], q4[:, t_], ss[:, t_].unsqueeze(2).to_broadcast([128, 16, 64]), ALU.mult, [rq, sqs])
                    qk2.append(self.ptt(q4[:, t_, 0:8], q4[:, t_, 0:8], self.row("qn").unsqueeze(1).to_broadcast([128, 8, 64]),
                                        ALU.mult, [w]))
                    qk2.append(self.ptt(q4[:, t_, 8:16], q4[:, t_, 8:16], self.row("kn").unsqueeze(1).to_broadcast([128, 8, 64]),
                                        ALU.mult, [w]))
        tpe = t
        t = self.cp(o, ob, [t])
        self.bfree[6] = t
        lam, lamt = self.st[:, 32:36], self.lamt
        gr = self.norm_stats(o, 64, osq, self.st[:, 16:24], [t])
        QK = sc(0, [128, 4, 2, 256])
        qw = []
        for h in range(4):
            c = 128 * h
            qw.append(self.T4(QK[:, h].rearrange("p a b -> p (a b)"), [q[:, 0, c:c + 128], q[:, 1, c:c + 128],
                      q[:, 0, 512 + c:640 + c], q[:, 1, 512 + c:640 + c]], [qk2, tpe], b=4 + h, eng="act" if h % 2 else "dve"))
        self.norm_scale(o, self.st[:, 16:24], 64, [gr])
        t = self.tt(o, o, self.row("glang").unsqueeze(1).to_broadcast([128, 8, 64]), ALU.mult, [cw])
        tz = self.af(osq, pj[:, :, 528:784], ACT.Silu, [t, gr])
        mg = [self.tt(self.mix[:, t_, 0:256], o[:, 4 * t_:4 * t_ + 4, :].rearrange("p a b -> p (a b)"),
                      osq[:, 4 * t_:4 * t_ + 4, :].rearrange("p a b -> p (a b)"), ALU.mult, [tz]) for t_ in range(2)]
        t = [m2, mg]
        DO = sc(8, [128, 2, 8, 128])
        jobs = []
        for h in range(4):
            dst = DO[:, :, 2 * h:2 * h + 2, :].rearrange("p t i d -> p i t d")

            def emit(o_, rib, ri, w_, dst=dst):
                e = self.tt(dst, o_, rib, ALU.mult, w_, chain=False)
                return e, e

            jobs.append({"heads": [(QK[64 * m:64 * m + 64, h, 0, :], QK[64 * m:64 * m + 64, h, 1, :],
                                    lambda t_, h=h: pj[:, t_, 2320 + 128 * h:2448 + 128 * h]) for m in range(2)],
                         "vd": 128, "w": [qw, t], "extra": None, "emit": emit})
        self.apfree = [[t], [t]]
        ow = self.attention(jobs, 0.125)
        D5 = DO.rearrange("p t (h m) d -> p t h m d", m=2)
        od = sc(0, [128, 8, 128])
        odq = sc(16, [128, 8, 128])
        for t_ in range(2):
            t = self.dve(lambda e, t_=t_: e.scalar_tensor_tensor(od[:, 4 * t_:4 * t_ + 4, :], D5[:, t_, :, 1, :],
                         lam[:, 3:4], D5[:, t_, :, 0, :], ALU.mult, ALU.add), [ow, lamt], True)
        t = self.norm_stats(od, 128, odq, self.st[:, 16:24], [t])
        t = self.ts(self.st[:, 16:24], self.st[:, 16:24], 0.8, ALU.mult, w=[t])
        self.norm_scale(od, self.st[:, 16:24], 128, [t])
        for t_ in range(2):
            m3 = self.tt(self.mix[:, t_, 512:1024].rearrange("p (h d) -> p h d", d=128), od[:, 4 * t_:4 * t_ + 4, :],
                         self.row("subg").unsqueeze(1).to_broadcast([128, 4, 128]), ALU.mult)
        self.debug("mix1", self.mix[:, :, :], [m3, m2, mg])
        self.pjfree = [ow, m3]
        self.hfree = [m3, ow]
        hs, tl = self.to_T(self.mix, [m3, m2, mg])

        def evac2(c, t, bank, width, tk):
            e = self.tt(self.x[:, t, c:c + width], bank, self.x[:, t, c:c + width], ALU.add, [tk])
            self.xw[t].append(e)
            return e

        self.xw = [[], []]
        self.hfree = self.proj_cb(("w_out", 0), 1024, (self.hhi, self.hlo), hs, evac2)
        self.debug("x1", self.x[:, :, :], self.xw)

    def first_max(self, oh, v, big, n, w):
        mx, eq, idx = big
        self.dve(lambda e: e.tensor_reduce(mx, v, X, ALU.max), w, True)
        self.tt(eq, v, mx.unsqueeze(2).to_broadcast([128, 2, 4]), ALU.is_equal)
        self.tt(eq, eq, self.iom4[:, 0:8].rearrange("p (a b) -> p a b", a=2), ALU.mult)
        self.dve(lambda e: e.tensor_reduce(idx, eq, X, ALU.min), [], True)
        self.tt(oh, self.iom4[:, 0:8].rearrange("p (a b) -> p a b", a=2), idx.unsqueeze(2).to_broadcast([128, 2, 4]),
                ALU.is_equal)
        return mx

    def moe(self):
        cw = self.cw
        hs = self.norm_T(self.col("ffng"), None, cw)
        for t in range(2):
            for kt in range(8):
                tk = self.mm(self.ps[:, 3, t * 32:t * 32 + 20], self.hT[:, kt, t * 128:t * 128 + 128],
                             self.rw[:, kt, :], kt == 0, kt == 7, [hs, cw, self.bfree[3]])
        selr = self.acopy(self.selr, self.sel16, [self.gmw, self.pjfree, tk], chain=False)
        f = self.frt
        lg = f(0, [128, 2, 20])
        t = self.tt(lg, self.ps[:, 3, 0:64].rearrange("p (t c) -> p t c", t=2)[:, :, 0:20],
                    self.row("rb").unsqueeze(1).to_broadcast([128, 2, 20]), ALU.add, [tk, cw, self.pjfree])
        self.bfree[3] = t
        self.debug("lg", lg, [t])
        mx, eq, idx = f(40, [128, 2]), f(42, [128, 2, 4]), f(50, [128, 2])
        goh, e8, pg = f(52, [128, 2, 4]), f(60, [128, 2, 4]), f(68, [128, 2])
        g = lg[:, :, 0:4]
        self.first_max(goh, g, (mx, eq, idx), 4, [])
        t = self.tt(e8, g, mx.unsqueeze(2).to_broadcast([128, 2, 4]), ALU.subtract)
        t = self.af(e8, e8, ACT.Exp, [t])
        self.dve(lambda e: e.tensor_reduce(pg, e8, X, ALU.add), [t], True)
        self.dve(lambda e: e.reciprocal(pg, pg), [], True)
        es, tmp = f(70, [128, 2, 4, 4]), f(102, [128, 2, 4])
        el = lg[:, :, 4:20].rearrange("p t (g e) -> p t g e", g=4)
        for t_ in range(2):
            self.tt(es[:, t_], el[:, t_], goh[:, t_].unsqueeze(2).to_broadcast([128, 4, 4]), ALU.mult)
        for t_ in range(2):
            t = self.dve(lambda e, t_=t_: e.tensor_reduce(tmp[:, t_, :], es[:, t_].rearrange("p g e -> p e g"), X, ALU.add), [], True)
        m1, oh1, oh2, m2 = f(110, [128, 2]), f(112, [128, 2, 4]), f(120, [128, 2, 4]), f(128, [128, 2])
        self.dve(lambda e: e.tensor_reduce(m1, tmp, X, ALU.max), [], True)
        t = self.tt(tmp, tmp, m1.unsqueeze(2).to_broadcast([128, 2, 4]), ALU.subtract)
        t = self.af(tmp, tmp, ACT.Exp, [t])
        self.first_max(oh1, tmp, (mx, eq, idx), 4, [t])
        self.ts(e8, oh1, -2.0, ALU.mult)
        self.tt(e8, e8, tmp, ALU.add)
        self.first_max(oh2, e8, (mx, eq, idx), 4, [])
        self.cp(m2, mx)
        den = f(130, [128, 2])
        self.ts(den, m2, 1.0, ALU.add)
        self.dve(lambda e: e.reciprocal(den, den), [], True)
        self.tt(den, den, pg, ALU.mult)
        self.tt(oh2, oh2, m2.unsqueeze(2).to_broadcast([128, 2, 4]), ALU.mult)
        self.tt(oh1, oh1, oh2, ALU.add)
        self.tt(oh1, oh1, den.unsqueeze(2).to_broadcast([128, 2, 4]), ALU.mult)
        for t_ in range(2):
            t = self.tt(es[:, t_], goh[:, t_].unsqueeze(2).to_broadcast([128, 4, 4]),
                        oh1[:, t_].unsqueeze(1).to_broadcast([128, 4, 4]), ALU.mult)
        self.debug("gates", es, [t])
        up0 = self.up(("moe", 0), 0, (self.hhi, self.hlo), hs, False)
        gT = f(160, [16, 256])
        t = self.T4(gT, [es[:, 0].rearrange("p a b -> p (a b)"), es[:, 1].rearrange("p a b -> p (a b)")], [t], b=3)
        ghi, glo = self.gth[:, 0, :], self.gth[:, 1, :]
        th = self.acopy(ghi, gT, [t], chain=False)
        tl = self.tt(glo, gT, ghi.bitcast(F32), ALU.subtract, [th], chain=False)
        gb = self.gateb
        gw = []
        for p in range(8):
            b = p % 4
            for k in range(2):
                o_, oh = self.ps[:, b, 256 * k:256 * k + 256], self.selr[:, 2 * p + k, :]
                self.mm(o_, oh, ghi, True, False, [th, selr, self.bfree[b]])
                tk = self.mm(o_, oh, glo, False, True, [tl])
            dst = gb[:, 2 * p:2 * p + 2, :].rearrange("p a b -> p (a b)")
            if p % 2:
                e = self.acopy(dst, self.ps[:, b, :], [tk, self.pjfree], chain=False)
            else:
                e = self.cp(dst, self.ps[:, b, :], [tk, self.pjfree], chain=False)
            self.bfree[b] = e
            gw.append(e)
        self.cw2 = self.Q.dma("act", lambda e: e.dma_start(self.w2, self.io["cw2"]), self.s_c[6], [tk])
        hf = [None, None]
        tk0 = tk
        tks = [None] * 4

        def down(e_, hid):
            n = self.take(("down", e_))
            m, th, tl = self.ready[n]
            for t_ in range(2):
                for c in range(2):
                    b = 2 * t_ + c
                    for k in range(2):
                        hi = self.mhid[:, e_ % 2, 0, k, t_ * 128:t_ * 128 + 128]
                        lo = self.mhid[:, e_ % 2, 1, k, t_ * 128:t_ * 128 + 128]
                        wh = self.whi[:, m, k * 1024 + c * 512:k * 1024 + c * 512 + 512]
                        wl = self.wlo[:, m, k * 1024 + c * 512:k * 1024 + c * 512 + 512]
                        s = e_ == 0 and k == 0
                        w = [hid, th, tl, self.bfree[b] if s else None]
                        self.mm(self.ps[:, b, :], hi, wh, s, False, w)
                        self.mm(self.ps[:, b, :], lo, wh, False, False)
                        tk = self.mm(self.ps[:, b, :], hi, wl, False, e_ == 15 and k == 1)
                    tks[b] = tk
            self.give(n, tk)
            hf[e_ % 2] = tk
            return tk

        prev = None
        for e_ in range(16):
            ta, tb = up0 if e_ == 0 else self.up(("moe", e_), 0, (self.hhi, self.hlo), hs, False)
            hid = []
            for f_ in range(2):
                hid += self.hidden(f_, ta[f_], tb[f_], self.mhid[:, e_ % 2, 0, f_, :], self.mhid[:, e_ % 2, 1, f_, :],
                                   [hf[e_ % 2], self.pjfree, tk0], gate=gb[:, e_, :], gw=gw)
            self.fill()
            if prev is not None:
                down(e_ - 1, prev)
                self.fill()
            prev = hid
        self.hfree = tb[1]
        tk = down(15, prev)
        self.flush()
        self.xw = [[], []]
        for t_ in range(2):
            for c in range(2):
                b = 2 * t_ + c
                e = self.tt(self.x[:, t_, c * 512:c * 512 + 512], self.ps[:, b, :], self.x[:, t_, c * 512:c * 512 + 512],
                            ALU.add, [tks[b]])
                self.bfree[b] = e
                self.xw[t_].append(e)
        self.hidfree = [tk, self.xw]
        self.debug("x2", self.x[:, :, :], self.xw)

    def fill(self, k=1):
        for _ in range(k):
            if self.nada >= self.adagoal:
                return
            n = self.nada
            self.nada += 1
            l, j, half = n // 72, n // 2 % 36, n % 2
            slot, r = n % NADA, (n // 2) % NACC
            dst, src = self.adaw[:, slot, :], self.io["wada"][n]
            ld = self.Q.dma("sp", lambda e, dst=dst, src=src: e.dma_start(dst, src), self.s_ada[slot], self.adafree[slot])
            w = self.adaw[:, slot, :].rearrange("p (k c) -> p k c", k=4)
            acc = self.acc[:, r, :]
            c = self.ca[:, 4 * half:4 * half + 4].unsqueeze(2).to_broadcast([128, 4, 256])
            first = [ld, self.cact]
            t = self.ptt(w, w, c, ALU.mult, first)
            t = self.ptt(w[:, 0:2, :], w[:, 0:2, :], w[:, 2:4, :], ALU.add, [t])
            if half:
                t = self.ptt(w[:, 0, :], w[:, 0, :], w[:, 1, :], ALU.add, [t])
                t = self.ptt(acc, w[:, 0, :], acc, ALU.add, [t, self.adalast])
            else:
                t = self.ptt(acc, w[:, 0, :], w[:, 1, :], ALU.add, [t, self.accfree[r]])
            self.adafree[slot] = self.adalast = t
            if half:
                self.accs.append((l, j, r, t))

    def sum_acc(self, bank, keep):
        tk = None
        out = self.accs[:max(0, len(self.accs) - keep)]
        self.accs = self.accs[len(out):]
        for i, (l, j, r, t) in enumerate(out):
            for k in range(2):
                c = 256 + 2 * i + k
                tk = self.mm(self.ps[:, bank, c:c + 1], self.acc[:, r, 128 * k:128 * k + 128], self.ones[:, 0:1],
                             True, True, [t, self.bfree[bank]])
            self.accfree[r] = tk
        return out, tk

    def put_mod(self, bank, done, w):
        if not done:
            return None
        l, j, n = done[0][0], done[0][1], 2 * len(done)
        t = self.tt(self.mod2[:, 72 * l + 2 * j:72 * l + 2 * j + n], self.ps[:, bank, 256:256 + n],
                    self.col("bada")[:, 72 * l + 2 * j:72 * l + 2 * j + n], ALU.add, [w, self.cw], chain=False)
        for l, _, _, _ in done:
            self.modt[l] = t
        return t

    def flush(self, bank=7, keep=0):
        if len(self.accs) > keep:
            done, tk = self.sum_acc(bank, keep)
            self.bfree[bank] = self.put_mod(bank, done, tk)

    def ada(self, l):
        while self.nada < 72 * (l + 1):
            self.fill()
            if len(self.accs) >= 3:
                self.flush(keep=1)
        self.flush()
        self.adagoal = 144
        self.mod = self.mod2[:, 72 * l:72 * l + 72]
        self.debug("mod%d" % l, self.mod, [self.modt[l]])
        m4 = self.mod.rearrange("p (i s k) -> p i s k", i=3, s=3)
        ng = self.col("ng2")[:, 24 * l:24 * l + 24].rearrange("p (i k) -> p i k", i=3)
        self.modw = self.dve(lambda e: e.scalar_tensor_tensor(m4[:, :, 1, :], m4[:, :, 1, :], 1.0, ng, ALU.add, ALU.mult),
                             [self.modt[l], self.cw], True)

    def gate_rows(self, i):
        m4 = self.mod.rearrange("p (i s k) -> p i s k", i=3, s=3)
        f = 0.5 if i != 1 else 1.0
        gw = []
        for c in range(2):
            for k in range(4):
                dgt = self.dgt[:, k, :]
                col = m4[:, i, 2, 4 * c + k:4 * c + k + 1]
                d = self.ts(dgt, self.ident, col, ALU.mult, f, ALU.mult, w=[self.modw, self.dgtf[k]], chain=False)
                self.dgtf[k] = tk = self.mm(self.ps[:, 4 + c, 128 * k:128 * k + 128], self.ones[:, 0:128], dgt, True, True,
                                            [d, self.bfree[4 + c]])
            e = self.acopy(self.gbc[:, 512 * c:512 * c + 512], self.ps[:, 4 + c, :], [tk, self.gbcfree], chain=False)
            self.bfree[4 + c] = e
            gw.append(e)
        self.gw = gw

    def gated_add(self, i, t_, c, bank, tk):
        tmp = self.xn[:, t_, c:c + 512]
        a = self.tt(tmp, bank, self.gbc[:, c:c + 512], ALU.mult, [tk, self.gw, self.xnfree], chain=False)
        self.gbcfree = a
        xs = self.x[:, t_, c:c + 512]
        b = self.tt(xs, xs, tmp, ALU.add, [a], chain=False)
        self.xw[t_].append(b)
        return a

    def ffn(self, l, i):
        mod = self.mod.rearrange("p (i s k) -> p i s k", i=3, s=3)
        hs = self.norm_T(mod[:, 2 * i, 1, :], mod[:, 2 * i, 0, :], self.modw)
        hid = []
        for j in range(11):
            if (l, i, j) == (0, 0, 3):
                self.rope_tables()
            ta, tb = self.up(("ffn", l, i), j, (self.hhi, self.hlo), hs, False)
            for f_ in range(2):
                ft = 2 * j + f_
                hid.append(self.hidden(f_, ta[f_], tb[f_], self.hidhi[:, ft, :], self.hidlo[:, ft, :], self.hidfree))
            self.fill()
        self.hfree = tb[1]
        self.flush()
        self.gate_rows(2 * i)
        tks = [None] * 4
        for j in range(11):
            n = self.take(("w2", l, i, j))
            m, th, tl = self.ready[n]
            for t_ in range(2):
                for c in range(2):
                    b = 2 * t_ + c
                    for k in range(2):
                        ft = 2 * j + k
                        hi = self.hidhi[:, ft, t_ * 128:t_ * 128 + 128]
                        lo = self.hidlo[:, ft, t_ * 128:t_ * 128 + 128]
                        wh = self.whi[:, m, k * 1024 + c * 512:k * 1024 + c * 512 + 512]
                        wl = self.wlo[:, m, k * 1024 + c * 512:k * 1024 + c * 512 + 512]
                        s = j == 0 and k == 0
                        self.mm(self.ps[:, b, :], hi, wh, s, False, [hid[ft], th, tl, self.bfree[b] if s else None])
                        self.mm(self.ps[:, b, :], lo, wh, False, False)
                        tk = self.mm(self.ps[:, b, :], hi, wl, False, j == 10 and k == 1)
                    tks[b] = tk
            self.give(n, tk)
            if j < 10:
                self.fill(1)
                self.flush(keep=1)
        self.hidfree = [tk]
        self.xw = [[], []]
        for t_ in range(2):
            for c in range(2):
                self.bfree[2 * t_ + c] = self.gated_add(2 * i, t_, 512 * c, self.ps[:, 2 * t_ + c, :], tks[2 * t_ + c])
        self.xnfree = None
        self.debug("xf%d%d" % (l, i), self.x[:, :, :], self.xw)

    def rope_tables(self):
        f = self.rsc
        pos, ang, k, r = f(0, [128, 2]), f(2, [128, 2, 8]), f(18, [128, 2, 8]), f(34, [128, 2, 8])
        self.cp(pos, self.posi, [self.cw])
        for t_ in range(2):
            self.ts(ang[:, t_, :], self.row("inv"), pos[:, t_:t_ + 1], ALU.mult)
        two_pi = 2 * np.pi
        c1 = 6.28125
        c2 = float(np.float32(int((two_pi - c1) * 2 ** 20) / 2 ** 20))
        c3 = float(np.float32(two_pi - c1 - c2))
        magic = 12582912.0
        for out, quarter, add in ((self.sinT, 0.0, 0.0), (self.cosT, 0.25, float(np.pi / 2))):
            self.ts(k, ang, float(1 / two_pi), ALU.mult, quarter, ALU.add)
            self.ts(k, k, magic, ALU.add)
            self.ts(k, k, magic, ALU.subtract)
            self.dve(lambda e: e.scalar_tensor_tensor(r, k, -c1, ang, ALU.mult, ALU.add), [], True)
            self.dve(lambda e: e.scalar_tensor_tensor(r, k, -c2, r, ALU.mult, ALU.add), [], True)
            self.dve(lambda e: e.scalar_tensor_tensor(r, k, -c3, r, ALU.mult, ALU.add), [], True)
            self.ts(r, r, add, ALU.add)
            t = self.ts(r, r, 3.1415925, ALU.min, -3.1415925, ALU.max)
            t = self.af(out, r, ACT.Sin, [t])
            self.cp(pos, pos, [t])
        self.ropew = t
        self.debug("cos", self.cosT, [t])

    def rope(self, lo, nh, w):
        pj = self.pj2
        v = pj[:, :, lo:lo + 64 * nh].rearrange("p t (h d) -> p t h d", d=64)
        r1, r2 = v[:, :, :, 0:8], v[:, :, :, 8:16]
        sh = [128, 2, nh, 8]
        c = self.cosT.unsqueeze(2).to_broadcast(sh)
        s = self.sinT.unsqueeze(2).to_broadcast(sh)
        a, b, d, e = [self.rsc(64 + 160 * i, [128, 2, nh, 8]) for i in range(4)]
        self.tt(a, r1, c, ALU.mult, [w, self.ropew])
        self.tt(b, r2, s, ALU.mult, chain=False)
        self.tt(d, r1, s, ALU.mult, chain=False)
        self.tt(e, r2, c, ALU.mult, chain=False)
        t = self.tt(r1, a, b, ALU.subtract)
        return self.tt(r2, e, d, ALU.add)

    def mixer(self, l):
        pj = self.pj2
        cw = self.cw
        mod = self.mod.rearrange("p (i s k) -> p i s k", i=3, s=3)
        hs = self.norm_T(mod[:, 1, 1, :], mod[:, 1, 0, :], self.modw)
        pw = []

        def evac(c, t, bank, width, tk):
            if t == 0:
                e = self.acopy(pj[:, t, c:c + width], bank, [tk, self.hidfree], chain=False)
            else:
                e = self.cp(pj[:, t, c:c + width], bank, [tk, self.hidfree], chain=False)
            pw.append(e)
            return e

        sc = self.scr
        QN = sc(0, [128, 4, 256])
        KS = sc(4, [128, 2, 256])
        ZZ = sc(16, [128, 4, 256])
        A = sc(20, [128, 2, 16, 30])
        hg = sc(16, [30, 2, 256])
        HT = sc(18, [128, 2, 2, 30])
        KC = sc(19, [128, 30])
        Ah, Al = self.ahi, self.alo
        VC = self.rsc(960, [15, 2, 64])
        PC = [self.att(0, [15, 8, 128]), self.gf[0:15, 1792:2816].rearrange("p (a b) -> p a b", a=8)]
        mixf = self.mix.rearrange("p a b -> p (a b)")
        QR = mixf[:, 0:1024].rearrange("p (t h g d) -> p t h g d", t=2, h=4, g=2)
        DU = mixf[:, 1024:2048].rearrange("p (t j r d) -> p t j r d", t=2, j=4, r=2)
        wq, wd, th2, rws = [], [], [], []
        v = {}

        def heads_out():
            rws.append(self.rope(0, 10, pw))
            for t_ in range(2):
                src = pj[:, t_, 512:768].rearrange("p (j d) -> p j d", d=64).unsqueeze(2).to_broadcast([128, 4, 2, 64])
                wd.append(self.acopy(DU[:, t_], src, [rws, self.mixfree], chain=False))
                src = pj[:, t_, 0:512].rearrange("p (g h d) -> p h g d", g=2, d=64)
                wq.append(self.cp(QR[:, t_], src, [rws, self.mixfree], chain=False))

        def compress_in():
            tz = []
            for kv in range(2):
                for g in range(2):
                    j = 2 * kv + g
                    for t_ in range(2):
                        dup = DU[:, t_, j].rearrange("p r d -> p (r d)")
                        tk = self.tr(self.ps[:, 4 + kv, (2 * g + t_) * 128:(2 * g + t_) * 128 + 128], dup, [wd, self.bfree[4 + kv]])
                src = self.ps[:, 4 + kv, :].rearrange("p (g t) -> p g t", g=2)
                e1 = self.cp(ZZ[0:64, 2 * kv:2 * kv + 2, :], src[0:64], [tk, self.xnfree], chain=False)
                e2 = self.cp(ZZ[64:128, 2 * kv:2 * kv + 2, 0:255], src[64:128, :, 1:256], [tk, self.xnfree], chain=False)
                self.bfree[4 + kv] = [e1, e2]
                tz += [e1, e2]
            ta = []
            for kv in range(2):
                for g in range(2):
                    for m in range(2):
                        z = ZZ[:, 2 * kv + g, :].rearrange("p (c k two) -> p k c two", k=8, two=2)[:, :, m:m + 15, 0]
                        p = self.col("pos")[:, 32 * l + 16 * kv + 8 * m:32 * l + 16 * kv + 8 * m + 8]
                        ta.append(self.tt(A[:, kv, 8 * m:8 * m + 8, 15 * g:15 * g + 15], z,
                                          p.unsqueeze(2).to_broadcast([128, 8, 15]), ALU.add, [tz, cw, self.afree, self.xnfree],
                                          chain=False))
            th = self.acopy(Ah, A, [ta, self.afree, self.hidfree], chain=False)
            v["tl"] = [th, self.tt(Al, A, Ah.bitcast(F32), ALU.subtract, [th, self.hidfree], chain=False)]
            v["tz"] = tz
            rws.append(self.rope(768, 2, pw))
            rws.append(self.rope(1024, 2, pw))

        def compress(kv):
            b = 4 + kv
            for half in range(2):
                n = self.take(("cw1", l, kv, half))
                m, wh_, wl_ = self.ready[n]
                for k in range(8):
                    kt = 8 * half + k
                    wh, wl = self.whi[:, m, 256 * k:256 * k + 256], self.wlo[:, m, 256 * k:256 * k + 256]
                    o_ = self.ps[0:30, b, 0:256]
                    self.mm(o_, Ah[:, kv, kt, :], wh, kt == 0, False, [v["tl"], wh_, wl_, self.bfree[b]])
                    self.mm(o_, Al[:, kv, kt, :], wh, False, False)
                    tk = self.mm(o_, Ah[:, kv, kt, :], wl, False, kt == 15)
                self.give(n, tk)
            self.afree = tk
            e = self.af(hg[:, kv, :], self.ps[0:30, b, 0:256], ACT.Gelu_apprx_tanh, [tk, v["tl"]], chain=False)
            self.bfree[b] = e
            th2.append(e)

        def compress_out():
            for kv in range(2):
                for k in range(2):
                    tk2 = self.tr(self.ps[:, 6, 256 * kv + 128 * k:256 * kv + 128 * k + 30], hg[:, kv, 128 * k:128 * k + 128],
                                  [th2, self.bfree[6]])
            e = self.cp(HT, self.ps[:, 6, :].rearrange("p (v a b) -> p v a b", v=2, a=2)[:, :, :, 0:30], [tk2, v["tl"]], chain=False)
            self.bfree[6] = e
            for k in range(2):
                tk = self.mm(self.ps[:, 4, 0:30], self.cw2k[:, l, k, :], HT[:, 0, k, :], k == 0, k == 1, [e, self.cw2, self.bfree[4]])
            ek = self.cp(KC, self.ps[:, 4, 0:30], [tk], chain=False)
            self.bfree[4] = ek
            for g in range(2):
                for k in range(2):
                    tk = self.mm(self.ps[0:15, 5, 64 * g:64 * g + 64], HT[:, 1, k, 15 * g:15 * g + 15], self.cw2v[:, l, k, :],
                                 k == 0, k == 1, [e, self.cw2, self.bfree[5]])
            ev = self.cp(VC, self.ps[0:15, 5, 0:128].rearrange("p (g d) -> p g d", g=2), [tk, rws], chain=False)
            self.bfree[5] = ev
            v["ek"], v["ev"] = ek, ev

        last = self.proj_cb(("w_in2", l), 2844, (self.hhi, self.hlo), hs, evac,
                            {512: heads_out, 1024: compress_in, 1536: lambda: compress(0), 2048: lambda: compress(1),
                             2560: compress_out})
        self.hfree = last
        ek, ev, tz = v["ek"], v["ev"], v["tz"]
        w0 = [rws, pw, last]
        tq = []
        for hp in range(2):
            for j in range(2):
                h = 2 * hp + j
                for t_ in range(2):
                    tk = self.tr(self.ps[:, hp, (2 * j + t_) * 128:(2 * j + t_) * 128 + 128], QR[:, t_, h].rearrange("p g d -> p (g d)"), [wq, self.bfree[hp]])
            e = self.cp(QN[:, 2 * hp:2 * hp + 2, :].rearrange("p a b -> p (a b)"), self.ps[:, hp, :], [tk, last], chain=False)
            self.bfree[hp] = e
            tq.append(e)
        tks = self.T4(KS[:, 0:2, :].rearrange("p a b -> p (a b)"),
                      [pj[:, 0, 768:896], pj[:, 1, 768:896], pj[:, 0, 1024:1152], pj[:, 1, 1024:1152]], w0, b=2, eng="act")
        rw = self.rope(2076, 8, [pw, ev])
        self.debug("pj2", pj[:, :, :], [rw])
        self.debug("kc", KC, [ek])
        sg = self.frt(0, [128, 2, 24])
        tsg = self.af(sg, pj[:, :, 1280:1304], ACT.Sigmoid, [pw])
        sg4 = sg.rearrange("p t (h s) -> p t h s", s=3)
        for t_ in range(2):
            for h in range(8):
                g = h // 4
                c = (4 * t_ + h % 4) * 16
                tk = self.mm(self.ps[:, 6 + g, c:c + 15],
                             QN[64 * g:64 * g + 64, h % 4, 128 * t_:128 * t_ + 128],
                             KC[64 * g:64 * g + 64, 15 * g:15 * g + 15], True, True, [ek, tq, self.bfree[6 + g]])
        tcs = tk
        Sc = sc(22, [128, 2, 8, 15])
        S16 = Sc.rearrange("p t h c -> p (t h) c")
        mx, sm = self.st[:, 40:56], self.st[:, 56:72]
        for t_ in range(2):
            for g in range(2):
                pS = self.ps[:, 6 + g, 64 * t_:64 * t_ + 64].rearrange("p (a c) -> p a c", c=16)
                t = self.tt(Sc[:, t_, 4 * g:4 * g + 4], pS[:, :, 0:15],
                            self.cmask[:, t_, :].unsqueeze(1).to_broadcast([128, 4, 15]), ALU.add, [tk, cw], chain=False)
        self.bfree[6] = self.bfree[7] = t
        self.dve(lambda e: e.tensor_reduce(mx, S16, X, ALU.max), [], True)
        self.ts(mx, mx, -1.0e30, ALU.max)
        t = self.tt(S16, S16, mx.unsqueeze(2).to_broadcast([128, 16, 15]), ALU.subtract)
        v["s"] = self.af(S16, S16, ACT.Exp, [t], scale=0.125)

        def probs():
            self.dve(lambda e: e.tensor_reduce(sm, S16, X, ALU.add), [v["s"]], True)
            self.ts(sm, sm, 1.0e-30, ALU.max)
            self.dve(lambda e: e.reciprocal(sm, sm), [], True)
            self.tt(sm.rearrange("p (t h) -> p t h", t=2), sm.rearrange("p (t h) -> p t h", t=2), sg4[:, :, :, 0], ALU.mult, [tsg])
            v["s"] = self.tt(S16, S16, sm.unsqueeze(2).to_broadcast([128, 16, 15]), ALU.mult)

        def compressed():
            te = []
            for b in range(4):
                for j in range(4):
                    tk = self.tr(self.ps[0:15, 6 + b % 2, 128 * j:128 * j + 128], S16[:, 4 * b + j, :], [v["s"], self.bfree[6 + b % 2]])
                e = self.acopy(PC[b // 2][:, 4 * (b % 2):4 * (b % 2) + 4, :].rearrange("p a b -> p (a b)"), self.ps[0:15, 6 + b % 2, :],
                               [tk, self.pjfree], chain=False)
                self.bfree[6 + b % 2] = e
                te.append(e)
            for t_ in range(2):
                for h in range(8):
                    tk = self.mm(self.ps[:, 6 + t_, 64 * h:64 * h + 64], PC[t_][:, h, :], VC[:, h // 4, :], True, True,
                                 [te, ev, self.bfree[6 + t_]])
                self.bfree[6 + t_] = self.cp(self.mix[:, t_, 0:512], self.ps[:, 6 + t_, :], [tk, self.mixfree, tq, tz], chain=False)
                mixc.append(self.bfree[6 + t_])

        mixc = []
        self.apfree = [tk, tk]
        self.aptfree = [tk, tk]
        jobs = []
        for br, kc, vc in ((1, 0, 896), (2, 1, 1152)):
            for p in range(4):
                g = p // 2
                V = lambda t_, g=g, vc=vc: pj[:, t_, vc + 64 * g:vc + 64 * g + 64]
                k_ = KS[64 * g:64 * g + 64, kc, :]
                r = p % 2
                cf = self.frt(48 + 4 * r, [128, 2, 2])
                tmp = self.frt(128 + 256 * r, [128, 2, 2, 64])
                gate = sg4[:, :, 2 * p:2 * p + 2, br].rearrange("p t i -> p i t")
                dst = self.mix[:, :, 128 * p:128 * p + 128].rearrange("p t (i d) -> p i t d", i=2)

                def emit(o_, rib, ri, w_, cf=cf, tmp=tmp, gate=gate, dst=dst):
                    a_ = self.tt(cf, ri, gate, ALU.mult, [w_[1], tsg], chain=False)
                    b_ = self.tt(tmp, o_, cf.unsqueeze(3).to_broadcast([128, 2, 2, 64]), ALU.mult, [a_, w_[0]], chain=False)
                    return b_, self.tt(dst, tmp, dst, ALU.add, [b_, mixc], chain=False)

                jobs.append({"heads": [(QN[64 * g:64 * g + 64, (2 * p + i) % 4, :], k_, V) for i in range(2)],
                             "vd": 64, "w": [tq, tks, w0], "extra": None, "emit": emit})
        lf, la = self.frt(64, [128, 2, 4]), self.frt(72, [128, 2, 4])
        t = self.tt(lf, pj[:, :, 2072:2076], self.row("foxb")[:, 4 * l:4 * l + 4].unsqueeze(1).to_broadcast([128, 2, 4]),
                    ALU.add, [cw, pw])
        t = self.log_sigmoid(lf, la, [t])
        F8 = sc(18, [1, 4, 256])
        nF = sc(14, [1, 4, 256])
        for h in range(4):
            b = 4 + h // 2
            o_ = self.ps[0:1, b, 256 * (h % 2):256 * (h % 2) + 256]
            for t_ in range(2):
                tk = self.mm(o_, lf[:, t_, h:h + 1], self.triu[:, t_, :], t_ == 0, t_ == 1, [t, cw, self.bfree[b]])
        src = self.ps[0:1, 4:6, :].rearrange("p a (b c) -> p (a b) c", c=256)
        e1 = self.ts(F8, src, 8.0, ALU.mult, w=[tk, tcs])
        e2 = self.ts(nF, src, -8.0, ALU.mult, w=[tk])
        self.bfree[4] = self.bfree[5] = e2
        QF = sc(6, [128, 4, 256])
        QM = sc(10, [128, 4, 256])
        tf = []
        for base, dst in ((1304, QF), (2076, QM)):
            for j in range(2):
                a, b_ = base + 128 * j, base + 256 + 128 * j
                bnk = 6 + j
                tf.append(self.T4(dst[:, 2 * j:2 * j + 2, :].rearrange("p a b -> p (a b)"),
                                  [pj[:, 0, a:a + 128], pj[:, 1, a:a + 128], pj[:, 0, b_:b_ + 128], pj[:, 1, b_:b_ + 128]],
                                  [w0, rw], free=self.afree, b=bnk, eng="act" if j else "dve"))

        for base, Q_, vcol, fox in ((512, QF, 1816, True), (768, QM, 2588, False)):
            for p in range(2):
                heads = []
                for h in (2 * p, 2 * p + 1):
                    P = slice(64 * (h % 2), 64 * (h % 2) + 64)
                    heads.append((Q_[P, 2 * p, :], Q_[P, 2 * p + 1, :],
                                  lambda t_, h=h, vcol=vcol: pj[:, t_, vcol + 64 * h:vcol + 64 * h + 64]))
                dst = self.mix[:, :, base + 128 * p:base + 128 * p + 128].rearrange("p t (i d) -> p i t d", i=2)

                def extra(i, o_, qt, kt, stop, p=p):
                    h = 2 * p + i
                    self.mm(o_, F8[0:1, h, 128 * qt:128 * qt + 128], self.ones[0:1, 0:128], False, False, [e1, e2])
                    return self.mm(o_, self.ones[0:1, 0:128], nF[0:1, h, 128 * kt:128 * kt + 128], False, stop)

                def emit2(o_, rib, ri, w_, dst=dst):
                    e = self.tt(dst, o_, rib, ALU.mult, [w_, self.mixfree], chain=False)
                    return e, e

                jobs.append({"heads": heads, "vd": 64, "w": [tf], "extra": extra if fox else None, "emit": emit2})
        ow = self.attention(jobs, 0.125, (probs, lambda: None, compressed))
        self.debug("mix2", self.mix[:, :, :], [ow])
        self.hfree = [ow]
        hs, tl = self.to_T(self.mix, ow)
        self.mixfree = tl
        self.hidfree = [ow, tl]

        def evac2(c, t, bank, width, tk):
            return self.gated_add(1, t, c, bank, tk)

        self.dgtf = [ow] * 4
        self.gate_rows(1)
        self.xw = [[], []]
        self.hfree = self.proj_cb(("w_out2", l), 1024, (self.hhi, self.hlo), hs, evac2)
        self.xnfree = None
        self.debug("xm%d" % l, self.x[:, :, :], self.xw)

    def afr(self):
        return [self.apfree, self.aptfree, self.pjfree]

    def final(self):
        tn = []
        for t in range(2):
            tn.append(self.af(self.xn[:, t, :], self.x[:, t, :], ACT.Square, [self.xw[t], self.xnfree],
                              accum_out=self.st[:, t:t + 1]))
        r = self.rstd(self.st[:, 2:4], self.st[:, 0:2], D, tn)
        fg = self.fing
        dl = self.Q.dma("sp", lambda e: e.dma_start(fg, self.io["fing"].to_broadcast([128, D])), self.s_fg, [self.hfree])
        out = self.io["out"].rearrange("b (t p) d -> p (b t) d", p=128)
        for t in range(2):
            o = self.xn[:, t, :]
            e = self.dve(lambda e, t=t, o=o: e.scalar_tensor_tensor(o, self.x[:, t, :], self.st[:, 2 + t:3 + t], fg,
                                                                    ALU.mult, ALU.mult), [r, dl], True)
            self.Q.dma("sp", lambda e, t=t, o=o: e.dma_start(out[:, t, :], o), self.s_out, [e])

    def col(self, name):
        a, n = COFF[name]
        return self.colp[:, a:a + n]

    def row(self, name):
        a, n = ROFF[name]
        return self.rowp[:, a:a + n]

    def build(self):
        nc, io = self.nc, self.io
        with ExitStack() as ctx:
            def sb(name, shape, dt=F32):
                return ctx.enter_context(nc.sbuf_tensor(name, shape, dt))

            self.ps = ctx.enter_context(nc.psum_tensor("ps", [128, 8, 512], F32))[:, :, :]
            self.raw = sb("raw", [128, NRAW, UW])[:, :, :]
            self.whi = sb("whi", [128, NSPL, UW], F32R)[:, :, :]
            self.wlo = sb("wlo", [128, NSPL, UW], F32R)[:, :, :]
            self.x = sb("x", [128, 2, D])[:, :, :]
            def over(name, shape):
                at = (nc.sbuf_base + 31) // 32 * 32
                base = sb(name, shape)
                assert nc.sbuf_base == at + 4 * shape[1]
                return base, nc.alloc_sbuf_tensor_at(name + "_r", shape, F32R, offset=at)

            hreg, hr = over("hreg", [128, 6144])
            self.hhi = hr[:, 0:2048].rearrange("p (a b) -> p a b", b=256)
            self.hlo = hr[:, 2048:4096].rearrange("p (a b) -> p a b", b=256)
            self.xn = hreg[:, 4096:6144].rearrange("p (a b) -> p a b", a=2)
            self.xnT = hreg[:, 4096:6144].rearrange("p (a b) -> p a b", b=256)
            self.fing = hreg[:, 0:1024]
            ireg, ir = over("ireg", [128, 11264])
            self.hidhi = ir[:, 0:5632].rearrange("p (a b) -> p a b", b=256)
            self.hidlo = ir[:, 5632:11264].rearrange("p (a b) -> p a b", b=256)
            self.pj1 = ireg[:, 0:5664].rearrange("p (a b) -> p a b", a=2)
            self.pj2 = ireg[:, 0:5688].rearrange("p (a b) -> p a b", a=2)
            self.gateb = ireg[:, 0:4096].rearrange("p (a b) -> p a b", b=256)
            self.selr = ir[0:16, 4096:6144].rearrange("p (a b) -> p a b", b=128)
            self.gth = ir[0:16, 10720:11232].rearrange("p (a b) -> p a b", a=2)
            self.mhid = ir[:, 4096:6144].rearrange("p (a b c d) -> p a b c d", a=2, b=2, c=2)
            at = 5696
            self.apb = ireg[:, at + 1536:at + 3072].rearrange("p (a b c) -> p a b c", a=2, b=2)
            self.apt = ireg[:, at + 3072:at + 4608].rearrange("p (a b c) -> p a b c", a=2, b=2)
            self.frt_at = at + 4608
            self.mix = sb("mix", [128, 2, D])[:, :, :]
            mixf = self.mix.rearrange("p a b -> p (a b)")
            self.hT = mixf.rearrange("p (a b) -> p a b", b=256)
            self.sil = mixf[:, 0:1024].rearrange("p (a b) -> p a b", b=256)
            self.prd = mixf[:, 1024:2048].rearrange("p (a b) -> p a b", b=256)
            greg = sb("greg", [128, 3072])
            self.gbc = greg[:, 0:1024]
            self.mod2 = sb("mod", [128, 144])[:, :]
            self.acc = sb("acc", [128, NACC, 256])[:, :, :]
            self.adaw = sb("adaw", [128, NADA, 1024])[:, :, :]
            self.ca = sb("ca", [128, 8])[:, :]
            self.colp = sb("colp", [128, NCOL])[:, :]
            self.rowp = sb("rowp", [128, NROW])[:, :]
            cst = sb("cst", [128, NCST])
            def c_(name):
                a, n = CSOFF[name]
                return cst[:, a:a + n]
            self.ident, self.ones, self.mask = c_("ident"), c_("ones"), c_("mask")
            self.triu = c_("triu").rearrange("p (a b) -> p a b", a=2)
            self.mhalf, self.iom4 = c_("mhalf"), c_("iom4")
            self.cmask = c_("cmask").rearrange("p (a b) -> p a b", a=2)
            gf = greg[:, :]
            self.gmask = gf[:, 0:1024].rearrange("p (a b) -> p a b", b=128)
            self.sel16 = gf[0:16, 1024:3072].rearrange("p (a b) -> p a b", b=128)
            self.rw = sb("rw", [128, 8, 20])[:, :, :]
            w2 = greg[:, 1024:1792]
            self.w2 = w2
            self.cw2k = w2[:, 0:512].rearrange("p (l k c) -> p l k c", l=2, k=2)
            self.cw2v = w2[:, 512:768].rearrange("p (l k c) -> p l k c", l=2, k=2)
            self.posi = sb("posi", [128, 2], I32)[:, :]
            self.st = sb("st", [128, 72])[:, :]
            self.st2 = sb("st2", [128, 48])[:, :]
            self.cosT = sb("cosT", [128, 2, 8])[:, :, :]
            self.sinT = sb("sinT", [128, 2, 8])[:, :, :]
            rs = sb("rs", [128, 1088])
            self.dgt = rs[:, 512:1024].rearrange("p (a b) -> p a b", b=128)
            an = sb("an", [128, 40])
            bm = sb("bm", [128, 256], mybir.dt.bfloat16)
            self.identb, self.trib = bm[:, 0:128], bm[:, 128:256]
            self.amx = an[:, 0:8].rearrange("p (a b c) -> p a b c", a=2, b=2)
            self.anm = an[:, 8:16].rearrange("p (a b c) -> p a b c", a=2, b=2)
            self.ars = an[:, 16:24].rearrange("p (a b c) -> p a b c", a=2, b=2)
            self.ari = an[:, 24:32].rearrange("p (a b c) -> p a b c", a=2, b=2)
            hr2 = hreg[:, :]

            def view(base, at, shape):
                n = int(np.prod(shape[1:]))
                v = base[0:shape[0], at:at + n]
                names = "abcd"[:len(shape) - 1]
                if len(shape) == 2:
                    return v
                pat = "p (%s) -> p %s" % (" ".join(names), " ".join(names))
                return v.rearrange(pat, **{k: s for k, s in zip(names, shape[1:])})

            self.scr = lambda kb, shape: view(hr2, kb * 256, shape)
            self.att = lambda kb, shape: view(ireg[:, :], at + kb * 256, shape)
            self.frt = lambda o, shape: view(ireg[:, :], self.frt_at + o, shape)
            self.rsc = lambda o, shape: view(rs[:, :], o, shape)
            areg = ir[:, at + 2048:at + 3968]
            self.ahi = areg[:, 0:960].rearrange("p (a b c) -> p a b c", a=2, b=16)
            self.alo = areg[:, 960:1920].rearrange("p (a b c) -> p a b c", a=2, b=16)

            sems = {e: ctx.enter_context(nc.semaphore("s_" + e)) for e in ("pe", "dve", "act", "pool", "sp")}
            self.s_raw = [ctx.enter_context(nc.semaphore(f"s_raw{i}")) for i in range(NRAW)]
            self.s_c = [ctx.enter_context(nc.semaphore(f"s_c{i}")) for i in range(8)]
            self.s_ada = [ctx.enter_context(nc.semaphore(f"s_ada{i}")) for i in range(NADA)]
            self.s_x = [ctx.enter_context(nc.semaphore(f"s_x{i}")) for i in range(2)]
            self.s_out = ctx.enter_context(nc.semaphore("s_out"))
            self.s_fg = ctx.enter_context(nc.semaphore("s_fg"))

            self.Q = Queues(nc, sems)
            self.nunit = self.nload = self.nahead = self.nsplit = 0
            self.upn = self.hr = 0
            self.loaded, self.ready = [], {}
            self.rawfree = [[] for _ in range(NRAW)]
            self.splfree = [[] for _ in range(NSPL)]
            self.bfree = [None] * 8
            self.silfree = [None] * 4
            self.xnfree = self.hfree = self.pjfree = self.mixfree = None
            self.hidfree = self.modfree = self.gbcfree = self.afree = None
            self.dgtf = [None] * 4
            self.apfree, self.aptfree = [None] * 2, [None] * 2
            self.anfree, self.arfree, self.aifree = [None] * 2, [None] * 2, [None] * 2

            ld = lambda i, dst, src: self.Q.dma("act", lambda e: e.dma_start(dst, src), self.s_c[i])
            xs = io["x"].rearrange("b (t p) d -> p (b t) d", p=128)
            self.xw = [[self.Q.dma("sp", lambda e: e.dma_start(self.x[:, 0, :], xs[:, 0, :]), self.s_x[0])],
                       [self.Q.dma("sp", lambda e: e.dma_start(self.x[:, 1, :], xs[:, 1, :]), self.s_x[1])]]
            self.cw = [ld(3, cst[:, :], io["cst"]), ld(1, self.colp, io["colp"])]
            self.start = self.cw
            self.gf = gf
            self.nada, self.adafree, self.adalast = 0, [None] * NADA, None
            self.adagoal = 72
            self.accs, self.accfree, self.modt, self.modlate = [], [None] * NACC, [None] * 2, None
            self.run_stages()

            self.left = nc.sbuf_usable_end - nc.sbuf_base
            self.Q.number()
            block = ctx.enter_context(nc.Block())
            Q = self.Q
            n_out = Q.dma_count.get(id(self.s_out), 0)

            @block.sync
            def _(e):
                Q.run("sp", e)
                e.wait_ge(self.s_out, n_out)

            @block.scalar
            def _(e):
                Q.run("act", e)

            @block.vector
            def _(e):
                Q.run("dve", e)

            @block.gpsimd
            def _(e):
                Q.run("pool", e)

            @block.tensor
            def _(e):
                Q.run("pe", e)

    def run_stages(self):
        s = self.stage
        self.first_mixer()
        if s >= 2:
            self.moe()
        if s >= 3:
            for l in range(2):
                if l == 0:
                    self.gbcfree = self.xw
                self.ada(l)
                self.ffn(l, 0)
                if s >= 4:
                    self.mixer(l)
                    self.ffn(l, 1)
                if s < 5:
                    break
        self.final()


CONSTS = [("ident", 128), ("ones", 256), ("mask", 384), ("triu", 512), ("mhalf", 32), ("iom4", 8), ("cmask", 30)]
CSOFF, NCST = offsets(CONSTS)


def constants():
    f = np.float32
    c = np.zeros((128, NCST), f)
    p = np.arange(128)

    def put(name, a):
        at, n = CSOFF[name]
        c[:, at:at + n] = np.asarray(a, f).reshape(128, n)

    put("ident", np.eye(128))
    put("ones", np.ones((128, 256)))
    k = np.arange(256)
    put("mask", np.concatenate([np.where(k[None, :128] <= p[:, None], 0, NEG),
                                np.where(k[None, :] <= 128 + p[:, None], 0, NEG)], 1))
    put("triu", np.stack([(128 * t + p[:, None] <= k[None, :]) for t in range(2)], 1))
    put("mhalf", np.full((128, 32), -0.5))
    put("iom4", np.tile(np.arange(4) - 4, (128, 2)))
    ce = np.arange(15) * 16 + 31
    put("cmask", np.stack([np.where(ce[None, :] <= 128 * t + p[:, None], 0, NEG) for t in range(2)], 1))
    c2 = np.zeros((128, 3072), f)
    g = np.zeros((128, 8, 128), f)
    j, i = p[:, None], p[None, :]
    for n, s in enumerate([64, 32, 16, 8, 4, 2, 1]):
        g[:, n, :] = (j // (2 * s) == i // (2 * s)) & (j % (2 * s) < s) & (i % (2 * s) >= s)
    g[:, 7, :] = np.eye(128)
    c2[:, 0:1024] = g.reshape(128, 1024)
    for e in range(16):
        c2[e, 1024 + 128 * e:1152 + 128 * e] = 1.0
    return c, c2


def tall(w):
    return w.reshape(w.shape[0] // 128, 128, -1).transpose(1, 0, 2).reshape(128, -1)


def unit(inp, key):
    name = key[0]
    kind = name[0] if isinstance(name, tuple) else name
    if kind in ("w_in", "w_out", "w_in2", "w_out2"):
        w = inp[{"w_in": "w_in", "w_out": "w_out", "w_in2": "w_in_2", "w_out2": "w_out_2"}[kind]][name[1]]
        c, half = key[1], key[2]
        return tall(w[512 * half:512 * half + 512, c:c + 512])
    if kind == "moe":
        w = inp["expert_w_gate" if key[1] == "a" else "expert_w_up"][0, name[1]]
        return tall(w)
    if kind == "down":
        return tall(inp["expert_w_down"][0, key[1]])
    if kind == "ffn":
        c = 256 * key[2] + (0 if key[1] == "a" else 2816)
        return tall(inp["ffn_w13_2"][name[1], name[2]][:, c:c + 256])
    if kind == "w2":
        _, l, i, j = key
        return tall(inp["ffn_w2_2"][l, i][256 * j:256 * j + 256])
    if kind == "cw1":
        _, l, kv, half = key
        return tall(inp["cmp_w1_2"][l, kv][1024 * half:1024 * half + 1024])
    raise KeyError(key)


def stream(inp, order):
    out = np.zeros((len(order), 128, UW), np.float32)
    for n, (key, width) in enumerate(order):
        out[n, :, :width] = unit(inp, key)
    return out


def ada_stream(inp):
    w = inp["w_ada_2"].reshape(2, 2, 4, 128, 36, 256)
    return np.ascontiguousarray(w.transpose(0, 4, 1, 3, 2, 5)).reshape(144, 128, 1024)


def cols(v):
    return np.ascontiguousarray(v.reshape(-1, 128).T)


def small_inputs(inp):
    f = np.float32
    colp = np.zeros((128, NCOL), f)

    def put(name, a):
        at, n = COFF[name]
        colp[0:a.shape[0], at:at + n] = a.reshape(a.shape[0], n)

    put("mixg", cols(inp["mix_norm_g"]))
    put("ffng", cols(inp["ffn_norm_g"]))
    put("ng2", cols(inp["norm_g_2"]))
    put("glab", cols(inp["gla_gate_b"]))
    put("convb", cols(inp["conv_b"]))
    put("convw", inp["conv_w"][0].T.reshape(2, 128, 31).transpose(1, 0, 2))
    put("c", cols(inp["c_2"]))
    put("bada", cols(inp["b_ada_2"]))
    put("pos", cols(inp["cmp_pos_2"]))
    put("glaw", inp["gla_gate_w"][0])
    rowp = np.zeros((1, NROW), f)

    def row(name, a):
        at, n = ROFF[name]
        rowp[0, at:at + n] = a.reshape(-1)

    row("glang", inp["gla_norm_g"])
    row("cng", inp["conv_norm_g"])
    row("cnb", inp["conv_norm_b"])
    row("qn", inp["diff_qnorm_g"])
    row("kn", inp["diff_knorm_g"])
    row("lq1", inp["diff_lq1"])
    row("lk1", inp["diff_lk1"])
    row("lq2", inp["diff_lq2"])
    row("lk2", inp["diff_lk2"])
    row("subg", inp["diff_subln_g"])
    row("rb", np.concatenate([inp["router_group_b"][0], inp["router_expert_b"][0]]))
    row("foxb", inp["fox_fbias_2"])
    row("inv", np.float32(500000.0) ** (-np.arange(0, 16, 2, dtype=f) / f(16)))
    rw = np.concatenate([inp["router_group_w"][0], inp["router_expert_w"][0]], 1)
    rw = np.ascontiguousarray(rw.reshape(8, 128, 20).transpose(1, 0, 2))
    w2 = inp["cmp_w2_2"].reshape(2, 2, 2, 128, 64)
    wk = np.concatenate([w2[:, 0], w2[:, 0]], -1).transpose(2, 0, 1, 3).reshape(128, 512)
    wv = w2[:, 1].transpose(2, 0, 1, 3).reshape(128, 256)
    cw2 = np.ascontiguousarray(np.concatenate([wk, wv], 1))
    pos = np.ascontiguousarray(inp["positions_2"].reshape(2, 128).T)
    c, c2 = constants()
    return {"x": np.ascontiguousarray(inp["x"]), "colp": colp, "rowp": rowp, "rw": rw, "cw2": cw2, "pos": pos,
            "cst": c, "cst2": c2, "fing": np.ascontiguousarray(inp["final_g_2"].reshape(1, D))}


SHAPES = {"x": (1, 256, D), "colp": (128, NCOL), "rowp": (1, NROW), "rw": (128, 8, 20), "cw2": (128, 768),
          "cst": (128, NCST), "cst2": (128, 3072), "fing": (1, D)}


def program(nc, order, split, stage=9, dbg=None):
    io = {k: nc.dram_tensor("in_" + k, s, F32, kind="ExternalInput").ap() for k, s in SHAPES.items()}
    io["pos"] = nc.dram_tensor("in_pos", (128, 2), I32, kind="ExternalInput").ap()
    io["wu"] = nc.dram_tensor("in_wu", (len(order) if order else 400, 128, UW), F32, kind="ExternalInput").ap()
    io["wada"] = nc.dram_tensor("in_wada", (144, 128, 1024), F32, kind="ExternalInput").ap()
    io["out"] = nc.dram_tensor("out_0", (1, 256, D), F32, kind="ExternalOutput").ap()
    dd = {k: nc.dram_tensor("dbg_" + k, s, F32, kind="ExternalOutput").ap() for k, s in (dbg or {}).items()}
    b = Build(nc, io, order, order is None, stage, dd)
    b.order_split = split if order else {}
    if order is None:
        b.order = []
    b.build()
    return b.asked, b.order_split


def kernel(**inputs):
    import concourse.bacc as bacc
    from concourse.bass_utils import run_bass_kernel_spmd

    inp = {k: np.asarray(v) for k, v in inputs.items()}
    order, split = program(bacc.Bacc("TRN2", target_bir_lowering=False, num_devices=1), None, None)
    nc = bacc.Bacc("TRN2", target_bir_lowering=False, num_devices=1)
    program(nc, order, split)
    arrays = {"in_" + k: v for k, v in small_inputs(inp).items()}
    arrays["in_wu"] = stream(inp, order)
    arrays["in_wada"] = ada_stream(inp)
    r = run_bass_kernel_spmd(nc, [arrays], core_ids=[0])
    return r.results[0]["out_0"]
```
